# Optimizing a Trainium2 kernel written in Bass

```python
import math
import jax, jax.numpy as jnp
from jax import lax
import numpy as np

D_MODEL = 2048
BATCH = 1
SEQ = 256
DEPTH = 1

CHUNK = 64
EPS = 1e-6
RW_HEADS = 16
RW_HEAD_DIM = 64
RW_WIDTH = RW_HEADS * RW_HEAD_DIM
RW_DECAY_RANK = 64
RW_ICL_RANK = 64
RW_GATE_RANK = 160
RW_GN_EPS = 64e-5
RW_SPLITS = (RW_WIDTH, RW_WIDTH, RW_WIDTH, RW_DECAY_RANK, RW_ICL_RANK, RW_GATE_RANK)
RW_IN = 3 * RW_WIDTH + RW_DECAY_RANK + RW_ICL_RANK + RW_GATE_RANK
SA_HEADS = 16
SA_HEAD_DIM = 64
SA_WIDTH = SA_HEADS * SA_HEAD_DIM
SA_SCALE = SA_HEAD_DIM ** -0.5
KV_RANK = 256
IDX_HEADS = 8
IDX_DIM = 64
IDX_SCALE = (IDX_HEADS * IDX_DIM) ** -0.5
TOPK_MAX = 256
Q_BLOCK = 128
REL_BUCKETS = 32
REL_MAX_DIST = 1024
N_BRANCHES = 2
IN_SPLITS = (RW_IN, SA_WIDTH, KV_RANK, IDX_HEADS * IDX_DIM, IDX_DIM, IDX_HEADS, N_BRANCHES * D_MODEL)
IN_TOTAL = RW_IN + SA_WIDTH + KV_RANK + IDX_HEADS * IDX_DIM + IDX_DIM + IDX_HEADS + N_BRANCHES * D_MODEL
PEER_HEADS = 8
PEER_KEYS = 128
PEER_EXPERTS = PEER_KEYS * PEER_KEYS
PEER_QDIM = 256
PEER_HALF = PEER_QDIM // 2
PEER_TOPK = 16
PEER_BLOCK = 128


def _split(x, sizes):
    idx = []
    acc = 0
    for s in sizes[:-1]:
        acc += s
        idx.append(acc)
    return jnp.split(x, idx, axis=-1)

def _rmsnorm(x, g):
    x32 = x.astype(jnp.float32)
    y = x32 * lax.rsqrt(jnp.mean(x32 * x32, axis=-1, keepdims=True) + EPS)
    return (y * g.astype(jnp.float32)).astype(x.dtype)

def _rel_bucket(rel):
    nb = REL_BUCKETS // 2
    max_exact = nb // 2
    ret = (rel > 0).astype(jnp.int32) * nb
    n = jnp.abs(rel)
    large = max_exact + (jnp.log(jnp.maximum(n, 1).astype(jnp.float32) / max_exact)
                         / math.log(REL_MAX_DIST / max_exact) * (nb - max_exact)).astype(jnp.int32)
    large = jnp.minimum(large, nb - 1)
    return ret + jnp.where(n < max_exact, n, large)

def _rwkv7_time_mix(p, shift_mix, w0, w_decay_up, a0, w_icl_up, w_gate_up, k_k, k_a, r_k, ln_x_w, ln_x_b):
    B, T, _ = p.shape
    H, N = RW_HEADS, RW_HEAD_DIM
    f32 = jnp.float32
    prev = jnp.pad(p, ((0, 0), (1, 0), (0, 0)))[:, :T]
    z = p + (prev - p) * shift_mix
    r, k, v, zw, za, zg = _split(z, RW_SPLITS)
    w_log = -jax.nn.softplus(-(w0 + jnp.tanh(zw) @ w_decay_up).astype(f32)) - 0.5
    decay = jnp.exp(-jnp.exp(w_log))
    a = jax.nn.sigmoid((a0 + za @ w_icl_up).astype(f32))
    g = jax.nn.sigmoid(zg) @ w_gate_up
    kf = k.astype(f32)
    kk = (kf * k_k.astype(f32)).reshape(B, T, H, N)
    kk = kk / jnp.maximum(jnp.linalg.norm(kk, axis=-1, keepdims=True), 1e-12)
    k4 = (kf * (1.0 + (a - 1.0) * k_a.astype(f32))).reshape(B, T, H, N)
    r4 = r.astype(f32).reshape(B, T, H, N)
    v4 = v.astype(f32).reshape(B, T, H, N)
    a4 = a.reshape(B, T, H, N)
    w4 = decay.reshape(B, T, H, N)

    def step(S, inp):
        r_t, k_t, v_t, kk_t, a_t, w_t = inp
        sa = jnp.einsum('bhvk,bhk->bhv', S, -kk_t)
        S = (S * w_t[:, :, None, :] + sa[..., None] * (kk_t * a_t)[:, :, None, :]
             + v_t[..., None] * k_t[:, :, None, :])
        return S, jnp.einsum('bhvk,bhk->bhv', S, r_t)

    xs = tuple(jnp.moveaxis(t, 1, 0) for t in (r4, k4, v4, kk, a4, w4))
    _, ys = lax.scan(step, jnp.zeros((B, H, N, N), f32), xs)
    y = jnp.moveaxis(ys, 0, 1)
    mean = jnp.mean(y, axis=-1, keepdims=True)
    var = jnp.mean(jnp.square(y - mean), axis=-1, keepdims=True)
    y = ((y - mean) * lax.rsqrt(var + RW_GN_EPS)).reshape(B, T, RW_WIDTH)
    y = y * ln_x_w.astype(f32) + ln_x_b.astype(f32)
    bonus = jnp.sum(r4 * k4 * r_k.astype(f32), axis=-1, keepdims=True) * v4
    y = (y + bonus.reshape(B, T, RW_WIDTH)) * g.astype(f32)
    return y.astype(p.dtype)

def _dsa_attention(q, c_kv, iq, ik, iw, kv_norm_g, w_uk, w_uv, rel_bias):
    B, T, _ = q.shape
    topk = min(TOPK_MAX, T // 4)
    f32 = jnp.float32
    c = _rmsnorm(c_kv, kv_norm_g)
    q_lat = jnp.einsum('bthd,hrd->bthr', q.reshape(B, T, SA_HEADS, SA_HEAD_DIM), w_uk)
    iq = iq.reshape(B, T, IDX_HEADS, IDX_DIM)
    iw = iw * IDX_SCALE
    key_chunk = jnp.arange(T) // CHUNK

    def block(i):
        s0 = i * Q_BLOCK
        qi = lax.dynamic_slice_in_dim(iq, s0, Q_BLOCK, axis=1)
        wi = lax.dynamic_slice_in_dim(iw, s0, Q_BLOCK, axis=1)
        ql = lax.dynamic_slice_in_dim(q_lat, s0, Q_BLOCK, axis=1)
        tq = s0 + jnp.arange(Q_BLOCK)
        score = jnp.einsum('bqhs,bqh->bqs', jax.nn.relu(jnp.einsum('bqhd,bsd->bqhs', qi, ik)), wi).astype(f32)
        allowed = key_chunk[None, :] <= (tq // CHUNK)[:, None]
        score = jnp.where(allowed[None], score, -jnp.inf)
        top_s, idx = lax.top_k(score, topk)
        valid = jnp.isfinite(top_s)
        c_sel = jax.vmap(lambda cb, ib: cb[ib])(c, idx)
        logits = jnp.einsum('bqhr,bqkr->bqhk', ql, c_sel).astype(f32) * SA_SCALE
        bias = rel_bias[_rel_bucket(idx - tq[None, :, None])]
        logits = logits + jnp.transpose(bias, (0, 1, 3, 2)).astype(f32)
        logits = jnp.where(valid[:, :, None, :], logits, -jnp.inf)
        pr = jax.nn.softmax(logits, axis=-1).astype(c.dtype)
        o_lat = jnp.einsum('bqhk,bqkr->bqhr', pr, c_sel)
        o = jnp.einsum('bqhr,hrd->bqhd', o_lat, w_uv)
        return o.reshape(B, Q_BLOCK, SA_WIDTH)

    out = lax.map(block, jnp.arange(T // Q_BLOCK))
    return jnp.moveaxis(out, 0, 1).reshape(B, T, SA_WIDTH)

def _peer_ffn(h, w_query, sub_keys, expert_u, expert_v):
    B, T, D = h.shape
    q = (h @ w_query).reshape(B, T, PEER_HEADS, 2, PEER_HALF)
    s = jnp.einsum('bthcq,hcnq->bthcn', q, sub_keys).astype(jnp.float32)
    s1, i1 = lax.top_k(s[..., 0, :], PEER_TOPK)
    s2, i2 = lax.top_k(s[..., 1, :], PEER_TOPK)
    cand = (s1[..., :, None] + s2[..., None, :]).reshape(B, T, PEER_HEADS, PEER_TOPK * PEER_TOPK)
    cand_id = (i1[..., :, None] * PEER_KEYS + i2[..., None, :]).reshape(B, T, PEER_HEADS, PEER_TOPK * PEER_TOPK)
    top_s, pos = lax.top_k(cand, PEER_TOPK)
    eid = jnp.take_along_axis(cand_id, pos, axis=-1)
    gate = jax.nn.softmax(top_s, axis=-1).astype(h.dtype)
    nb = (B * T) // PEER_BLOCK
    hb = h.reshape(nb, PEER_BLOCK, D)
    eb = eid.reshape(nb, PEER_BLOCK, PEER_HEADS, PEER_TOPK)
    gb = gate.reshape(nb, PEER_BLOCK, PEER_HEADS, PEER_TOPK)

    def blk(args):
        hx, e, gt = args
        act = jax.nn.gelu(jnp.einsum('nd,nhkd->nhk', hx, expert_u[e]), approximate=False)
        return jnp.einsum('nhk,nhkd->nd', gt * act, expert_v[e])

    return lax.map(blk, (hb, eb, gb)).reshape(B, T, D)

def first_inputs(seed: int = 0) -> dict:
    key = jax.random.key(seed)
    ks = iter(jax.random.split(key, 40))
    L, D = DEPTH, D_MODEL
    nrm = lambda shape, scale: jax.random.normal(next(ks), shape, jnp.float32) * scale
    uni = lambda shape, lo, hi: jax.random.uniform(next(ks), shape, jnp.float32, lo, hi)
    gain = lambda shape: 1.0 + nrm(shape, 0.02)
    return {
        'x': nrm((BATCH, SEQ, D), 1.0),
        'norm_mix_g': gain((L, D)),
        'w_in': nrm((L, D, IN_TOTAL), D ** -0.5),
        'shift_mix': uni((L, RW_IN), 0.0, 1.0),
        'w0': uni((L, RW_WIDTH), -4.0, 0.0),
        'w_decay_up': nrm((L, RW_DECAY_RANK, RW_WIDTH), 0.3 * RW_DECAY_RANK ** -0.5),
        'a0': nrm((L, RW_WIDTH), 0.3),
        'w_icl_up': nrm((L, RW_ICL_RANK, RW_WIDTH), RW_ICL_RANK ** -0.5),
        'w_gate_up': nrm((L, RW_GATE_RANK, RW_WIDTH), RW_GATE_RANK ** -0.5),
        'k_k': 0.85 + nrm((L, RW_WIDTH), 0.05),
        'k_a': 1.0 + nrm((L, RW_WIDTH), 0.05),
        'r_k': nrm((L, RW_HEADS, RW_HEAD_DIM), 0.1),
        'ln_x_w': gain((L, RW_WIDTH)),
        'ln_x_b': nrm((L, RW_WIDTH), 0.02),
        'kv_norm_g': gain((L, KV_RANK)),
        'w_uk': nrm((L, SA_HEADS, KV_RANK, SA_HEAD_DIM), KV_RANK ** -0.5),
        'w_uv': nrm((L, SA_HEADS, KV_RANK, SA_HEAD_DIM), KV_RANK ** -0.5),
        'rel_bias': nrm((REL_BUCKETS, SA_HEADS), 0.5),
        'w_branch_rwkv': nrm((L, RW_WIDTH, D), RW_WIDTH ** -0.5),
        'w_branch_dsa': nrm((L, SA_WIDTH, D), SA_WIDTH ** -0.5),
        'w_out': nrm((L, D, D), D ** -0.5),
        'norm_ffn_g': gain((L, D)),
        'w_peer_query': nrm((L, D, PEER_HEADS * PEER_QDIM), D ** -0.5),
        'peer_sub_keys': nrm((L, PEER_HEADS, 2, PEER_KEYS, PEER_HALF), PEER_HALF ** -0.5),
        'peer_u': nrm((L, PEER_EXPERTS, D), D ** -0.5),
        'peer_v': nrm((L, PEER_EXPERTS, D), 0.25),
        'norm_final_g': gain((D,)),
    }

def first_block(x, norm_mix_g, w_in, shift_mix, w0, w_decay_up, a0, w_icl_up, w_gate_up, k_k, k_a, r_k,
              ln_x_w, ln_x_b, kv_norm_g, w_uk, w_uv, rel_bias, w_branch_rwkv, w_branch_dsa, w_out,
              norm_ffn_g, w_peer_query, peer_sub_keys, peer_u, peer_v, norm_final_g):
    h = x
    for l in range(DEPTH):
        xn = _rmsnorm(h, norm_mix_g[l])
        p_rw, q, c_kv, iq, ik, iw, gates = _split(xn @ w_in[l], IN_SPLITS)
        y_a = _rwkv7_time_mix(p_rw, shift_mix[l], w0[l], w_decay_up[l], a0[l], w_icl_up[l], w_gate_up[l],
                              k_k[l], k_a[l], r_k[l], ln_x_w[l], ln_x_b[l]) @ w_branch_rwkv[l]
        y_b = _dsa_attention(q, c_kv, iq, ik, iw, kv_norm_g[l], w_uk[l], w_uv[l], rel_bias) @ w_branch_dsa[l]
        g_a, g_b = jnp.split(jax.nn.sigmoid(gates), N_BRANCHES, axis=-1)
        h = h + (g_a * y_a + g_b * y_b) @ w_out[l]
        h = h + _peer_ffn(_rmsnorm(h, norm_ffn_g[l]), w_peer_query[l], peer_sub_keys[l], peer_u[l], peer_v[l])
    return _rmsnorm(h, norm_final_g)


DEPTH_2 = 2

N_A_LAYERS = max(DEPTH_2 // 2, 1)
N_B_LAYERS = DEPTH_2 - N_A_LAYERS

SSM_EXPAND = 2
D_INNER = SSM_EXPAND * D_MODEL
SSM_HEAD_DIM = 64
SSM_HEADS = D_INNER // SSM_HEAD_DIM
SSM_GROUPS = 8
D_STATE = 128
D_CONV = 4
CHUNK_2 = 128
GN = SSM_GROUPS * D_STATE
CONV_DIM = D_INNER + 2 * GN
D_IN_PROJ = D_INNER + CONV_DIM + SSM_HEADS

ATT_HEAD_DIM = 64
ATT_HEADS = D_MODEL // ATT_HEAD_DIM
KV_HEADS = 4
Q_PER_KV = ATT_HEADS // KV_HEADS
Q_WIDTH = ATT_HEADS * ATT_HEAD_DIM
KV_WIDTH = KV_HEADS * ATT_HEAD_DIM
WINDOW = 128
ROT_DIM = ATT_HEAD_DIM // 4
ROPE_THETA = 500000.0

ALPHA = (2.0 * DEPTH_2) ** 0.25
BETA = (8.0 * DEPTH_2) ** -0.25
EPS_2 = 1e-5


def _layernorm(x, g, b):
    xf = x.astype(jnp.float32)
    mu = jnp.mean(xf, axis=-1, keepdims=True)
    var = jnp.mean(jnp.square(xf - mu), axis=-1, keepdims=True)
    y = (xf - mu) * lax.rsqrt(var + EPS_2) * g.astype(jnp.float32) + b.astype(jnp.float32)
    return y.astype(x.dtype)

def _segsum(x):
    t = x.shape[-1]
    xe = jnp.broadcast_to(x[..., :, None], x.shape + (t,))
    xe = jnp.where(jnp.tril(jnp.ones((t, t), dtype=bool), -1), xe, 0.0)
    s = jnp.cumsum(xe, axis=-2)
    return jnp.where(jnp.tril(jnp.ones((t, t), dtype=bool)), s, -jnp.inf)

def _ssd_chunked(xs, dt, a, bm, cm):
    bsz, seqlen, nh, hp = xs.shape
    ng = bm.shape[2]
    rg = nh // ng
    nc = seqlen // CHUNK_2
    x_c = (xs * dt[..., None]).reshape(bsz, nc, CHUNK_2, ng, rg, hp)
    b_c = bm.reshape(bsz, nc, CHUNK_2, ng, D_STATE)
    c_c = cm.reshape(bsz, nc, CHUNK_2, ng, D_STATE)
    da = (dt * a).reshape(bsz, nc, CHUNK_2, ng, rg).transpose(0, 3, 4, 1, 2)
    da_cum = jnp.cumsum(da, axis=-1)
    decay_in = jnp.exp(_segsum(da))
    cb = jnp.einsum("bcqgn,bcsgn->bgcqs", c_c, b_c)
    y_diag = jnp.einsum("bgcqs,bgrcqs,bcsgrp->bcqgrp", cb, decay_in, x_c)
    decay_st = jnp.exp(da_cum[..., -1:] - da_cum)
    states = jnp.einsum("bcsgn,bgrcs,bcsgrp->bcgrpn", b_c, decay_st, x_c)
    chunk_tot = jnp.pad(da_cum[..., -1], ((0, 0), (0, 0), (0, 0), (1, 0)))
    decay_ch = jnp.exp(_segsum(chunk_tot))
    states0 = jnp.concatenate([jnp.zeros_like(states[:, :1]), states], axis=1)
    start_states = jnp.einsum("bgrzc,bcgrpn->bzgrpn", decay_ch, states0)[:, :-1]
    y_off = jnp.einsum("bcqgn,bcgrpn,bgrcq->bcqgrp", c_c, start_states, jnp.exp(da_cum))
    return (y_diag + y_off).reshape(bsz, seqlen, nh, hp)

def _mamba2_mixer(x, w_in, conv_w, conv_b, dt_bias, a_log, d_skip, norm_w, w_out):
    bsz, seqlen, _ = x.shape
    zxbcdt = x @ w_in
    z = zxbcdt[..., :D_INNER]
    xbc = zxbcdt[..., D_INNER:D_INNER + CONV_DIM]
    dt_raw = zxbcdt[..., D_INNER + CONV_DIM:]
    xbc = lax.conv_general_dilated(
        xbc, conv_w[:, None, :].astype(xbc.dtype), window_strides=(1,),
        padding=[(D_CONV - 1, 0)], dimension_numbers=("NWC", "WIO", "NWC"),
        feature_group_count=CONV_DIM) + conv_b
    xbc = jax.nn.silu(xbc)
    xs = xbc[..., :D_INNER].reshape(bsz, seqlen, SSM_HEADS, SSM_HEAD_DIM).astype(jnp.float32)
    bm = xbc[..., D_INNER:D_INNER + GN].reshape(bsz, seqlen, SSM_GROUPS, D_STATE).astype(jnp.float32)
    cm = xbc[..., D_INNER + GN:].reshape(bsz, seqlen, SSM_GROUPS, D_STATE).astype(jnp.float32)
    dt = jax.nn.softplus(dt_raw.astype(jnp.float32) + dt_bias.astype(jnp.float32))
    a = -jnp.exp(a_log.astype(jnp.float32))
    y = _ssd_chunked(xs, dt, a, bm, cm) + xs * d_skip.astype(jnp.float32)[:, None]
    y = y.reshape(bsz, seqlen, D_INNER) * jax.nn.silu(z.astype(jnp.float32))
    yg = y.reshape(bsz, seqlen, SSM_GROUPS, D_INNER // SSM_GROUPS)
    yg = yg * lax.rsqrt(jnp.mean(jnp.square(yg), axis=-1, keepdims=True) + EPS_2)
    y = yg.reshape(bsz, seqlen, D_INNER) * norm_w.astype(jnp.float32)
    return y.astype(x.dtype) @ w_out

def _rope_tables(positions):
    inv_freq = ROPE_THETA ** (-jnp.arange(0, ROT_DIM, 2, dtype=jnp.float32) / ROT_DIM)
    ang = positions.astype(jnp.float32)[..., None] * inv_freq
    return jnp.cos(ang), jnp.sin(ang)

def _rope_partial(x, cos, sin):
    half = ROT_DIM // 2
    xf = x.astype(jnp.float32)
    x1, x2, rest = xf[..., :half], xf[..., half:ROT_DIM], xf[..., ROT_DIM:]
    out = jnp.concatenate([x1 * cos - x2 * sin, x2 * cos + x1 * sin, rest], axis=-1)
    return out.astype(x.dtype)

def _shared_kv(x, kv_w, kv_b, cos, sin):
    bsz, seqlen, _ = x.shape
    kv = x @ kv_w + kv_b
    k = kv[..., :KV_WIDTH].reshape(bsz, seqlen, KV_HEADS, ATT_HEAD_DIM)
    v = kv[..., KV_WIDTH:].reshape(bsz, seqlen, KV_HEADS, ATT_HEAD_DIM)
    k = _rope_partial(k, cos[:, :, None, :], sin[:, :, None, :])
    return k, v

def _swa_sink_attention(q, k, v, sinks):
    bsz, seqlen, hk, rq, hd = q.shape
    nb = seqlen // WINDOW
    qb = q.reshape(bsz, nb, WINDOW, hk, rq, hd)
    kb = k.reshape(bsz, nb, WINDOW, hk, hd)
    vb = v.reshape(bsz, nb, WINDOW, hk, hd)
    pad = ((0, 0), (1, 0), (0, 0), (0, 0), (0, 0))
    kk = jnp.concatenate([jnp.pad(kb, pad)[:, :-1], kb], axis=2)
    vv = jnp.concatenate([jnp.pad(vb, pad)[:, :-1], vb], axis=2)
    s = jnp.einsum("bcqhrd,bckhd->bchrqk", qb, kk).astype(jnp.float32) * (hd ** -0.5)
    qi = jnp.arange(WINDOW)[:, None] + WINDOW
    ki = jnp.arange(2 * WINDOW)[None, :]
    diff = qi - ki
    kpos = jnp.arange(nb)[:, None, None] * WINDOW + ki[None] - WINDOW
    valid = (diff >= 0)[None] & (diff < WINDOW)[None] & (kpos >= 0)
    s = jnp.where(valid[None, :, None, None], s, -jnp.inf)
    sk = sinks.astype(jnp.float32)[None, None, :, :, None, None]
    m = jnp.maximum(jnp.max(s, axis=-1, keepdims=True), sk)
    p = jnp.exp(s - m)
    p = p / (jnp.sum(p, axis=-1, keepdims=True) + jnp.exp(sk - m))
    o = jnp.einsum("bchrqk,bckhd->bcqhrd", p.astype(vv.dtype), vv)
    return o.reshape(bsz, seqlen, hk * rq * hd)

def _swa_mixer(x, k, v, cos, sin, w_in, q_bias, sinks, w_out):
    bsz, seqlen, _ = x.shape
    proj = x @ w_in
    q = (proj[..., :Q_WIDTH] + q_bias).reshape(bsz, seqlen, KV_HEADS, Q_PER_KV, ATT_HEAD_DIM)
    gate = proj[..., Q_WIDTH:]
    q = _rope_partial(q, cos[:, :, None, None, :], sin[:, :, None, None, :])
    o = _swa_sink_attention(q, k, v, sinks.reshape(KV_HEADS, Q_PER_KV))
    o = o * jax.nn.silu(gate)
    return o @ w_out

def second_inputs(seed: int = 0) -> dict:
    key = jax.random.key(seed)
    ks = jax.random.split(key, 20)
    f32 = jnp.float32
    x = jax.random.normal(ks[0], (BATCH, SEQ, D_MODEL), f32)
    offs = jax.random.randint(ks[1], (BATCH, 1), 0, 1024, dtype=jnp.int32)
    positions = (offs + jnp.arange(SEQ, dtype=jnp.int32)[None, :]).astype(jnp.int32)
    ln_g = 1.0 + 0.02 * jax.random.normal(ks[2], (DEPTH_2, D_MODEL), f32)
    ln_b = 0.02 * jax.random.normal(ks[3], (DEPTH_2, D_MODEL), f32)
    a_w_in = jax.random.normal(ks[4], (N_A_LAYERS, D_MODEL, D_IN_PROJ), f32) * D_MODEL ** -0.5
    a_conv_w = jax.random.normal(ks[5], (N_A_LAYERS, D_CONV, CONV_DIM), f32) * D_CONV ** -0.5
    a_conv_b = 0.02 * jax.random.normal(ks[6], (N_A_LAYERS, CONV_DIM), f32)
    dt0 = jnp.exp(jax.random.uniform(ks[7], (N_A_LAYERS, SSM_HEADS), f32,
                                     math.log(1e-3), math.log(1e-1)))
    a_dt_bias = dt0 + jnp.log(-jnp.expm1(-dt0))
    a_log = jnp.log(jax.random.uniform(ks[8], (N_A_LAYERS, SSM_HEADS), f32, 1.0, 16.0))
    a_d = 1.0 + 0.1 * jax.random.normal(ks[9], (N_A_LAYERS, SSM_HEADS), f32)
    a_norm_w = 1.0 + 0.02 * jax.random.normal(ks[10], (N_A_LAYERS, D_INNER), f32)
    a_w_out = jax.random.normal(ks[11], (N_A_LAYERS, D_INNER, D_MODEL), f32) * (D_INNER ** -0.5 * BETA)
    kv_scale = jnp.concatenate([jnp.ones((KV_WIDTH,), f32), jnp.full((KV_WIDTH,), BETA, f32)])
    kv_w = jax.random.normal(ks[12], (D_MODEL, 2 * KV_WIDTH), f32) * D_MODEL ** -0.5 * kv_scale
    kv_b = 0.02 * jax.random.normal(ks[13], (2 * KV_WIDTH,), f32)
    b_w_in = jax.random.normal(ks[14], (N_B_LAYERS, D_MODEL, 2 * Q_WIDTH), f32) * D_MODEL ** -0.5
    b_q_bias = 0.02 * jax.random.normal(ks[15], (N_B_LAYERS, Q_WIDTH), f32)
    b_sinks = 0.5 * jax.random.normal(ks[16], (N_B_LAYERS, ATT_HEADS), f32)
    b_w_out = jax.random.normal(ks[17], (N_B_LAYERS, Q_WIDTH, D_MODEL), f32) * (Q_WIDTH ** -0.5 * BETA)
    return {"x": x, "positions": positions, "ln_g": ln_g, "ln_b": ln_b,
            "a_w_in": a_w_in, "a_conv_w": a_conv_w, "a_conv_b": a_conv_b,
            "a_dt_bias": a_dt_bias, "a_log": a_log, "a_d": a_d, "a_norm_w": a_norm_w,
            "a_w_out": a_w_out, "kv_w": kv_w, "kv_b": kv_b, "b_w_in": b_w_in,
            "b_q_bias": b_q_bias, "b_sinks": b_sinks, "b_w_out": b_w_out}

def second_block(x, positions, ln_g, ln_b, a_w_in, a_conv_w, a_conv_b, a_dt_bias, a_log, a_d,
              a_norm_w, a_w_out, kv_w, kv_b, b_w_in, b_q_bias, b_sinks, b_w_out):
    cos, sin = _rope_tables(positions)
    k_sh = None
    v_sh = None
    for layer in range(DEPTH_2):
        if layer < N_A_LAYERS:
            i = layer
            h = _mamba2_mixer(x, a_w_in[i], a_conv_w[i], a_conv_b[i], a_dt_bias[i], a_log[i],
                              a_d[i], a_norm_w[i], a_w_out[i])
        else:
            if layer == N_A_LAYERS:
                k_sh, v_sh = _shared_kv(x, kv_w, kv_b, cos, sin)
            j = layer - N_A_LAYERS
            h = _swa_mixer(x, k_sh, v_sh, cos, sin, b_w_in[j], b_q_bias[j], b_sinks[j], b_w_out[j])
        x = _layernorm(ALPHA * x + h, ln_g[layer], ln_b[layer])
    return x


def setup_inputs(seed=0):
    out = dict(first_inputs(seed))
    for name, value in second_inputs(seed + 1).items():
        if name != "x":
            out[name + "_2"] = value
    return out


def reference(
    x, norm_mix_g, w_in, shift_mix, w0, w_decay_up, a0, w_icl_up, w_gate_up, k_k, k_a, r_k,
    ln_x_w, ln_x_b, kv_norm_g, w_uk, w_uv, rel_bias, w_branch_rwkv, w_branch_dsa, w_out,
    norm_ffn_g, w_peer_query, peer_sub_keys, peer_u, peer_v, norm_final_g, positions_2, ln_g_2,
    ln_b_2, a_w_in_2, a_conv_w_2, a_conv_b_2, a_dt_bias_2, a_log_2, a_d_2, a_norm_w_2,
    a_w_out_2, kv_w_2, kv_b_2, b_w_in_2, b_q_bias_2, b_sinks_2, b_w_out_2,
):
    x = first_block(
        x, norm_mix_g, w_in, shift_mix, w0, w_decay_up, a0, w_icl_up, w_gate_up, k_k, k_a, r_k,
        ln_x_w, ln_x_b, kv_norm_g, w_uk, w_uv, rel_bias, w_branch_rwkv, w_branch_dsa, w_out,
        norm_ffn_g, w_peer_query, peer_sub_keys, peer_u, peer_v, norm_final_g,
    )
    return second_block(
        x, positions_2, ln_g_2, ln_b_2, a_w_in_2, a_conv_w_2, a_conv_b_2, a_dt_bias_2, a_log_2,
        a_d_2, a_norm_w_2, a_w_out_2, kv_w_2, kv_b_2, b_w_in_2, b_q_bias_2, b_sinks_2,
        b_w_out_2,
    )


_drawn_inputs = setup_inputs


def setup_inputs(seed=0):
    import zlib

    import numpy as np

    out = dict(_drawn_inputs(seed))
    spreads = {}
    factors = {'w_decay_up': 4.114,
     'k_k': 11.612,
     'ln_x_w': 14.425,
     'ln_x_b': 13.584,
     'kv_norm_g': 6.115,
     'norm_ffn_g': 10.213,
     'norm_final_g': 2.709,
     'a_conv_b_2': 5.857,
     'a_norm_w_2': 87.339,
     'kv_b_2': 8.0,
     'b_q_bias_2': 200.0,
     'b_sinks_2': 34.987,
     'a_d_2': 24.925}
    for name, (base, spread) in spreads.items():
        noise = np.random.default_rng([zlib.crc32(name.encode()), seed]).standard_normal(out[name].shape)
        drawn = base * np.exp(spread * noise) if base else spread * noise
        out[name] = __import__('jax').numpy.asarray(drawn.astype(out[name].dtype))
    for name, factor in factors.items():
        out[name] = (out[name] * factor).astype(out[name].dtype)
    return out
```

```python
from contextlib import ExitStack

import concourse.bass as bass
import numpy as np
from concourse import mybir

F32 = mybir.dt.float32
F32R = mybir.dt.float32r
U32 = mybir.dt.uint32
I32 = mybir.dt.int32
ACT = mybir.ActivationFunctionType
ALU = mybir.AluOpType
AX = mybir.AxisListType.X

P = 128
T = 256
TT = T // P
D = 2048
DC = D // P
H = 16
HD = 64
HC = H * HD // P
GATE_RANK = 160
IDX_HEADS = 8
IDX_SCALE = (IDX_HEADS * 64) ** -0.5
SA_SCALE = HD ** -0.5
KV_CHUNKS = 2
TOPK = 64
CH = 32
NCH = T // CH
EXP_HALF = float(np.float32(np.exp(-0.5)))
PK_HEADS, PK_KEYS, PK_TOP = 8, 128, 16
PK_SEL = PK_HEADS * PK_TOP
NEG = -1.0e30
DROPPED, TAKEN = -1.0e38, -3.0e38
SSM_H, GROUPS = 64, 8
ZC, CONVC = 32, 48
ALPHA = 4.0 ** 0.25
EPS_RMS, EPS_GN, EPS_2 = 1e-6, 64e-5, 1e-5
QH, KVH = 32, 4
TWO_PI = 2 * np.pi
PI_A = 6.28125
PI_B = 0.0019350051879882812
PI_C = float(TWO_PI - PI_A - PI_B)
PI_LOW = 3.1415925
ROUND = 12582912.0

C_R, C_K, C_V, C_WA, C_G, C_GI, C_Q, C_KV, C_IQ, C_IK = 0, 8, 16, 24, 25, 26, 27, 35, 37, 41
C_IN = 42
IW_ROW = 32

PARAM_COLS = dict(
    norm_mix=16, mix=27, w0=8, a0=8, k_k=8, k_a=8, r_k=8, ln_x_w=8, ln_x_b=8, kv_norm=2, norm_ffn=16,
    norm_final=16, ln_g=32, ln_b=32, conv_w=4 * CONVC, conv_b=CONVC, dt_bias=1, a_log=1, a_d=32, a_norm=32,
    q_bias=16, k_bias=4)
CONST_COLS = dict(ident=128, ones=128, heads=128, flip=128, decay_mask=64, scan=T, turn=128, freq=1, iota=16, eps_rms=1,
                  eps_gn=1, eps_2=1)


def columns(sizes):
    at, out = 0, {}
    for name, n in sizes.items():
        out[name] = (at, n)
        at += n
    return out, at


PARAM_AT, N_PARAM = columns(PARAM_COLS)
CONST_AT, N_CONST = columns(CONST_COLS)


class Order:

    def __init__(self, sem):
        self.sem, self.n = sem, 0

    def mark(self, ins):
        self.n += 1
        ins.then_inc(self.sem, 1)
        return self.n

    def settle(self, eng):
        eng.wait_ge(self.sem, self.n)

    def after(self, eng, ins):
        self.mark(ins)
        self.settle(eng)


class Ring:

    SLOTS = 4

    def __init__(self, nc, ctx):
        self.buf = ctx.enter_context(nc.sbuf_tensor("weights", [P, self.SLOTS, 4, 512], F32))
        self.loaded = [ctx.enter_context(nc.semaphore(f"weights_loaded{q}")) for q in range(self.SLOTS)]
        self.high = ctx.enter_context(nc.semaphore("part_high"))
        self.split = ctx.enter_context(nc.semaphore("part_split"))
        self.used = ctx.enter_context(nc.semaphore("part_used"))
        self.evacuated = ctx.enter_context(nc.semaphore("evacuated"))
        self.parts = 0
        self.groups = 0
        self.ahead = False

    def load(self, sp, w, g, q, part, columns=512):
        slot = q % self.SLOTS if w.shape[2] >= 16 else q
        if not isinstance(part, int) or part >= self.SLOTS:
            sp.wait_ge(self.split, part - self.SLOTS + 1)
        rows = 4 * (q % (w.shape[2] // 4))
        src = w[bass.ds(g, 1), :, rows:rows + 4, 0:columns].rearrange("a p k n -> (a p) k n")
        sp.dma_start(self.buf[:, slot, :, 0:columns], src).then_inc(self.loaded[slot], 16)

    def prefetch(self, sp, w, part):
        parts = w.shape[2] // 4
        for s in range(self.SLOTS):
            self.load(sp, w, s // parts, s, part + s)
        self.ahead = True


def linear(nc, ring, ps, w, chunks, rhs, evac, next_w=None):
    parts = w.shape[2] // 4
    groups = (chunks + 3) // 4
    live = [min(4, chunks - 4 * g) for g in range(groups)]
    pairs = sum(n == 4 for n in live) // 2
    p0, g0 = ring.parts, ring.groups
    ahead, ring.ahead = ring.ahead, False
    tail = list(range(2 * pairs, groups))
    S = ring.SLOTS

    with ExitStack() as scope:
        w_half = scope.enter_context(nc.sbuf_tensor(f"w_half{g0}", [P, 2, 2, 4, 512], F32R))
        x_half = scope.enter_context(nc.sbuf_tensor(f"x_half{g0}", [P, 2, 2, 4, T], F32R))

        def schedule(group):
            def run(eng):
                if pairs:
                    for half in range(2):
                        group(eng, half, half, p0 + half * parts, 4)
                if pairs > 1:
                    with eng.Fori(1, pairs) as j:
                        for half in range(2):
                            group(eng, 2 * j + half, half, p0 + half * parts + 2 * parts * j, 4)
                for g in tail:
                    group(eng, g, g - 2 * pairs, p0 + g * parts, live[g])
            return run

        with nc.Block() as block:
            @block.sync
            def _(sp):
                if not ahead:
                    ring.prefetch(sp, w, p0)
                    ring.ahead = False

                def group(sp, g, half, part, n_live):
                    for q in range(parts):
                        if isinstance(part, int) and part + q < p0 + S:
                            continue
                        ring.load(sp, w, g, (half * parts + q) % max(S, parts), part + q, P * n_live)

                schedule(group)(sp)
                if next_w is not None:
                    ring.prefetch(sp, next_w, p0 + groups * parts)

            @block.tensor
            def _(pe):
                def group(pe, g, half, part, n_live):
                    if not isinstance(g, int) or (g >= 2 and g0 + g > 1):
                        pe.wait_ge(ring.evacuated, g0 + g - 1)
                    for q in range(parts):
                        b = (half * parts + q) % 2
                        pe.wait_ge(ring.split, part + q + 1)
                        for n in range(n_live):
                            for k in range(4):
                                for i, (wh, xh) in enumerate(((0, 0), (0, 1), (1, 0))):
                                    last = nc.tensor.matmul(
                                        ps[:, 4 * half + n, 0:T], w_half[:, b, wh, k, P * n:P * n + P], x_half[:, b, xh, k, :],
                                        start=(q == 0 and k == 0 and i == 0), stop=(q == parts - 1 and k == 3 and i == 2))
                        last.then_inc(ring.used, 1)

                schedule(group)(pe)

            def parts_and_sums(eng, one, f):
                def sums(g, half, part, n_live):
                    eng.wait_ge(ring.used, part + parts)
                    f(eng, g, ps[:, 4 * half:4 * half + n_live, 0:T], half)

                def group(eng, g, half, part, n_live):
                    for q in range(parts):
                        one(eng, (half * parts + q) % 2, (half * parts + q) % S, q, part + q, P * n_live)
                        if q == 1 and f and not (isinstance(g, int) and g == 0):
                            sums(g - 1, 1 - half, part - parts, 4)

                schedule(group)(eng)
                if f:
                    sums(groups - 1, (groups - 1) % 2, p0 + (groups - 1) * parts, live[-1])

            @block.scalar
            def _(act):
                def high(act, b, slot, q, part, columns):
                    act.wait_ge(ring.loaded[slot], 4 * (part - slot) + 16)
                    if not isinstance(part, int) or part >= p0 + 2:
                        act.wait_ge(ring.used, part - 1)
                    nc.scalar.activation(w_half[:, b, 0, :, 0:columns], ring.buf[:, slot, :, 0:columns], ACT.Copy)
                    nc.scalar.activation(x_half[:, b, 0, :, :], rhs[:, 4 * q:4 * q + 4, :], ACT.Copy).then_inc(ring.high, 1)

                parts_and_sums(act, high, evac.get("scalar"))

            @block.vector
            def _(dve):
                def low(dve, b, slot, q, part, columns):
                    dve.wait_ge(ring.high, part + 1)
                    nc.vector.tensor_tensor(x_half[:, b, 1, :, :], rhs[:, 4 * q:4 * q + 4, :], x_half[:, b, 0, :, :].bitcast(F32), ALU.subtract)
                    nc.vector.tensor_tensor(w_half[:, b, 1, :, 0:columns], ring.buf[:, slot, :, 0:columns],
                                            w_half[:, b, 0, :, 0:columns].bitcast(F32), ALU.subtract).then_inc(ring.split, 1)

                parts_and_sums(dve, low, evac.get("vector"))
    ring.parts = p0 + groups * parts
    ring.groups = g0 + groups


def sum_over_channels(pe, nc, ones, sq, out, chunks):
    for c in range(chunks):
        last = nc.tensor.matmul(out, ones, sq[:, c, :], start=(c == 0), stop=(c == chunks - 1))
    return last


def rmsnorm(nc, sem, cst, ps, src, dst, gain, tmp, chunks, eps, prefetch=None):
    squared, summed, rooted = sem("squared"), sem("summed"), sem("rooted")
    order = Order(sem("norm_order"))
    with nc.Block() as block:
        if prefetch:
            @block.sync
            def _(sp):
                prefetch(sp)

        @block.scalar
        def _(act):
            nc.scalar.activation(dst, src, ACT.Square).then_inc(squared, 1)
            act.wait_ge(summed, 1)
            nc.scalar.activation(tmp, ps[:, 0, 0:T], ACT.Sqrt, bias=cst(eps), scale=1.0 / (P * chunks)).then_inc(rooted, 1)

        @block.tensor
        def _(pe):
            pe.wait_ge(squared, 1)
            sum_over_channels(pe, nc, cst("ones"), dst, ps[:, 0, 0:T], chunks).then_inc(summed, 1)

        @block.vector
        def _(dve):
            dve.wait_ge(rooted, 1)
            order.after(dve, nc.vector.reciprocal(tmp, tmp))
            for c in range(chunks):
                nc.vector.scalar_tensor_tensor(dst[:, c, :], src[:, c, :], gain[:, c:c + 1], tmp, ALU.mult, ALU.mult)


def build(nc, d, out):
    ctx = ExitStack()
    made = {}

    in_use = []

    def sem(name):
        made[name] = made.get(name, 0) + 1
        in_use.append(nc.alloc_semaphore(f"{name}_{made[name]}"))
        return in_use[-1]

    def recycle():
        nc.clear_and_free_semaphores(list(in_use))
        nc.all_engine_barrier()
        in_use.clear()

    def sbuf(scope, name, shape, dt=F32):
        return scope.enter_context(nc.sbuf_tensor(name, [P] + shape, dt))

    with ctx:
        params = sbuf(ctx, "params", [N_PARAM])
        const = sbuf(ctx, "const", [N_CONST])
        ps = ctx.enter_context(nc.psum_tensor("ps", [P, 8, 512], F32))
        ring = Ring(nc, ctx)

        def par(name, i=0, n=1):
            return params[:, PARAM_AT[name][0] + i:PARAM_AT[name][0] + i + n]

        def par_at(name, i):
            return params[:, bass.ds(PARAM_AT[name][0] + i, 1)]

        def cst(name):
            at, n = CONST_AT[name]
            return const[:, at:at + n]

        scratch = {n: nc.dram_tensor(n, s, F32, kind="Internal").ap() for n, s in dict(
            solve_in=[P, CH, CH], solve_out=[P, CH, CH], bias_rows=[H, 2 * T]).items()}
        env = dict(nc=nc, d=d, sem=sem, sbuf=sbuf, par=par, par_at=par_at, cst=cst, ps=ps, ring=ring, scratch=scratch)

        x1 = sbuf(ctx, "x1", [DC, T])
        y_rwkv, y_dsa = x1[:, 0:HC, :], x1[:, HC:2 * HC, :]
        with ExitStack() as scope:
            xn = sbuf(scope, "xn", [DC, T])
            with ExitStack() as mix:
                pin = sbuf(mix, "pin", [C_IN, T])
                load_and_norm(mix, xn, params, const, **env)
                linear(nc, ring, ps, d["w_in"], C_IN, xn, dict(scalar=copy_out(nc, ring, pin)))
                shift_tokens(pin, **env)
                sparse_attention(pin, y_dsa, **env)
                recycle()
                rwkv(pin, y_rwkv, **env)
                recycle()
            with ExitStack() as mix:
                gates = sbuf(mix, "gates", [2 * DC, T])
                mixed = sbuf(mix, "mixed", [DC, T])
                mix_branches(gates, mixed, xn, y_rwkv, y_dsa, **env)
                add_mixed(mixed, xn, **env)
            recycle()
            peer(xn, x1, **env)
        recycle()
        with ExitStack() as scope:
            z = sbuf(scope, "z", [ZC, T])
            xbc = sbuf(scope, "xbc", [CONVC, T])
            x2 = xbc[:, ZC:CONVC, :]
            mamba(x1, x2, z, xbc, recycle, **env)
            recycle()
            attention(x2, x1, z, out, **env)


def copy_out(nc, ring, dst):
    def f(act, g, sums, half):
        nc.scalar.activation(dst[:, bass.ds(4 * g, sums.shape[1]), :], sums, ACT.Copy).then_inc(ring.evacuated, 1)
    return f


def load_and_norm(scope, xn, params, const, *, nc, d, sem, sbuf, par, cst, ps, ring, **_):
    with ExitStack() as inner:
        x = sbuf(inner, "x_in", [DC, T])
        tmp = sbuf(inner, "rms", [T])
        arrived = [sem("params_arrived"), sem("const_arrived"), sem("x_arrived")]
        with nc.Block() as block:
            @block.sync
            def _(sp):
                sp.dma_start(x[:, :, :], d["x"]).then_inc(arrived[2], 16)
                sp.dma_start(params[:, :], d["params"]).then_inc(arrived[0], 16)
                sp.dma_start(const[:, :], d["const"]).then_inc(arrived[1], 16)
                ring.prefetch(sp, d["w_in"], 0)
                for a in arrived:
                    sp.wait_ge(a, 16)
        rmsnorm(nc, sem, cst, ps, x[:, :, :], xn[:, :, :], par("norm_mix", 0, DC), tmp[:, :], DC, "eps_rms")


def shift_tokens(pin, *, nc, sem, sbuf, par, cst, **_):
    n = C_GI + 1
    order = Order(sem("shift_order"))
    with ExitStack() as inner:
        diff = sbuf(inner, "diff", [n, T])
        with nc.Block() as block:
            @block.vector
            def _(dve):
                order.mark(nc.vector.tensor_tensor(diff[:, :, 1:T], pin[:, 0:n, 0:T - 1], pin[:, 0:n, 1:T], ALU.subtract))
                order.mark(nc.vector.tensor_scalar(diff[:, :, 0], pin[:, 0:n, 0], -1.0, None, ALU.mult))
                order.settle(dve)
                for c in range(n):
                    nc.vector.scalar_tensor_tensor(pin[:, c, :], diff[:, c, :], par("mix", c), pin[:, c, :], ALU.mult, ALU.add)


def sparse_attention(pin, y, *, nc, d, sem, sbuf, par, cst, ps, ring, scratch, **_):
    with ExitStack() as scope:
        k_t = sbuf(scope, "k_t", [HC, T])
        v_tok = sbuf(scope, "v_tok", [TT, H * HD])
        logits = sbuf(scope, "logits", [TT, H, T])
        with ExitStack() as inner:
            latent = sbuf(inner, "latent", [KV_CHUNKS, T])
            tmp = sbuf(inner, "latent_rms", [T])
            w_uk = sbuf(inner, "w_uk", [KV_CHUNKS, H * HD])
            w_uv = sbuf(inner, "w_uv", [KV_CHUNKS, H * HD])
            rel = inner.enter_context(nc.sbuf_tensor("rel", [32, H], F32))
            hot = inner.enter_context(nc.sbuf_tensor("hot", [32, 2 * T], F32))
            rows = inner.enter_context(nc.sbuf_tensor("rows", [H, 2 * T], F32))
            up_in, rel_in, rows_out, bias_in = sem("up_in"), sem("rel_in"), sem("rows_out"), sem("bias_in")
            made, rows_ready, keys_made, values_made, copied, normed = (sem("rows_made"), sem("rows_ready"),
                sem("keys_made"), sem("values_made"), sem("kv_copied"), sem("latent_ready"))
            rmsnorm(nc, sem, cst, ps, pin[:, C_KV:C_KV + 2, :], latent[:, :, :], par("kv_norm", 0, 2), tmp[:, :],
                    KV_CHUNKS, "eps_rms")
            with nc.Block() as block:
                @block.sync
                def _(sp):
                    sp.dma_start(rel[:, :], d["rel_bias"]).then_inc(rel_in, 16)
                    sp.dma_start(hot[:, :], d["bucket_hot"]).then_inc(rel_in, 16)
                    sp.dma_start(w_uk[:, :, :], d["w_uk"]).then_inc(up_in, 16)
                    sp.dma_start(w_uv[:, :, :], d["w_uv"]).then_inc(up_in, 16)
                    sp.wait_ge(rows_ready, 1)
                    sp.dma_start(scratch["bias_rows"], rows[:, :]).then_inc(rows_out, 16)
                    sp.wait_ge(rows_out, 16)
                    for i in range(TT):
                        src = bass.AP(scratch["bias_rows"].tensor, P - P * i, [[1, P], [2 * T, H], [1, T]])
                        sp.dma_start(logits[:, i, :, :], src).then_inc(bias_in, 16)
                    sp.wait_ge(bias_in, 16 * TT)

                @block.tensor
                def _(pe):
                    pe.wait_ge(rel_in, 32)
                    nc.tensor.matmul(ps[0:H, 7, :], rel[:, :], hot[:, :], start=True, stop=True).then_inc(made, 1)
                    pe.wait_ge(up_in, 32)
                    for c in range(HC):
                        if c == 7:
                            pe.wait_ge(rows_ready, 1)
                        for k in range(KV_CHUNKS):
                            last = nc.tensor.matmul(ps[:, c, 0:T], w_uk[:, k, P * c:P * c + P], latent[:, k, :],
                                                    start=(k == 0), stop=(k == 1))
                        last.then_inc(keys_made, 1)
                    for i in range(TT):
                        for n in range(2):
                            b = 2 * i + n
                            pe.wait_ge(copied, b + 1)
                            for k in range(KV_CHUNKS):
                                last = nc.tensor.matmul(ps[:, b, :], latent[:, k, P * i:P * i + P],
                                                        w_uv[:, k, 512 * n:512 * n + 512], start=(k == 0), stop=(k == 1))
                            last.then_inc(values_made, 1)

                @block.vector
                def _(dve):
                    dve.wait_ge(made, 1)
                    nc.vector.tensor_copy(rows[:, :], ps[0:H, 7, :]).then_inc(rows_ready, 1)

                @block.scalar
                def _(act):
                    for c in range(HC):
                        act.wait_ge(keys_made, c + 1)
                        nc.scalar.activation(k_t[:, c, :], ps[:, c, 0:T], ACT.Copy, scale=SA_SCALE).then_inc(copied, 1)
                    for b in range(4):
                        act.wait_ge(values_made, b + 1)
                        nc.scalar.activation(v_tok[:, b // 2, 512 * (b % 2):512 * (b % 2) + 512], ps[:, b, :], ACT.Copy)
        score = sbuf(scope, "score", [TT, T])
        index_scores(pin, score, nc=nc, sem=sem, sbuf=sbuf, cst=cst, ps=ps)
        softmax_heads(pin, k_t, v_tok, logits, score, y, nc=nc, sem=sem, sbuf=sbuf, cst=cst, ps=ps)


def index_scores(pin, score, *, nc, sem, sbuf, cst, ps):
    with ExitStack() as inner:
        iw = sbuf(inner, "iw", [TT, IDX_HEADS])
        relu = sbuf(inner, "relu", [4, T])
        top = sbuf(inner, "top", [TT, 8])
        turned, scored, rectified, added = sem("iw_turned"), sem("scored"), sem("rectified"), sem("score_added")
        order = Order(sem("score_order"))
        with nc.Block() as block:
            @block.tensor
            def _(pe):
                for i in range(TT):
                    nc.tensor.transpose(ps[:, 7, P * i:P * i + P], pin[:, C_GI, P * i:P * i + P], cst("ident")).then_inc(turned, 1)
                for n in range(TT * IDX_HEADS):
                    i, h = n // IDX_HEADS, n % IDX_HEADS
                    rows = slice(64 * (h % 2), 64 * (h % 2) + 64)
                    if n >= 4:
                        pe.wait_ge(rectified, n - 3)
                    nc.tensor.matmul(ps[:, n % 4, 0:T], pin[rows, C_IQ + h // 2, P * i:P * i + P], pin[rows, C_IK, :],
                                     start=True, stop=True).then_inc(scored, 1)

            @block.scalar
            def _(act):
                for n in range(TT * IDX_HEADS):
                    act.wait_ge(scored, n + 1)
                    if n >= 4:
                        act.wait_ge(added, n - 3)
                    nc.scalar.activation(relu[:, n % 4, :], ps[:, n % 4, 0:T], ACT.Relu).then_inc(rectified, 1)

            @block.vector
            def _(dve):
                dve.wait_ge(turned, 2)
                for i in range(TT):
                    order.mark(nc.vector.tensor_scalar(iw[:, i, :], ps[:, 7, P * i + IW_ROW:P * i + IW_ROW + IDX_HEADS],
                                                       IDX_SCALE, None, ALU.mult))
                order.settle(dve)
                for n in range(TT * IDX_HEADS):
                    i, h = n // IDX_HEADS, n % IDX_HEADS
                    dve.wait_ge(rectified, n + 1)
                    if h == 0:
                        nc.vector.tensor_scalar(score[:, i, :], relu[:, n % 4, :], iw[:, i, h:h + 1], None, ALU.mult).then_inc(added, 1)
                    else:
                        dve.wait_ge(added, n)
                        nc.vector.scalar_tensor_tensor(score[:, i, :], relu[:, n % 4, :], iw[:, i, h:h + 1], score[:, i, :],
                                                       ALU.mult, ALU.add).then_inc(added, 1)
                dve.wait_ge(added, TT * IDX_HEADS)
                for q in range(T // 64 - 1):
                    order.mark(nc.vector.memset(score[64 * (q % 2):64 * (q % 2) + 64, q // 2, 64 * q + 64:T], DROPPED))
                order.settle(dve)
                for _ in range(TOPK // 8):
                    for i in range(TT):
                        order.mark(nc.vector.max(top[:, i, :], score[:, i, :]))
                    order.settle(dve)
                    for i in range(TT):
                        order.mark(nc.vector.match_replace(score[:, i, :], top[:, i, :], score[:, i, :], TAKEN))
                    order.settle(dve)
                nc.vector.tensor_scalar(score[:, :, :], score[:, :, :], (DROPPED + TAKEN) / 2, NEG, ALU.is_gt, ALU.mult)


def softmax_heads(pin, k_t, v_tok, logits, mask, y, *, nc, sem, sbuf, cst, ps):
    with ExitStack() as inner:
        p_t = sbuf(inner, "p_t", [2, TT, T])
        peak = sbuf(inner, "peak", [TT, H])
        total = sbuf(inner, "total", [TT, H])
        dotted, added, peaked, exped, scaled = sem("dotted"), sem("logit_added"), sem("peaked"), sem("exped"), sem("scaled")
        turned, p_copied, valued, y_copied = sem("p_turned"), sem("p_copied"), sem("valued"), sem("y_copied")
        order = Order(sem("softmax_order"))
        with nc.Block() as block:
            def values(pe, h):
                base = 64 * (h % 2)
                pe.wait_ge(p_copied, h + 1)
                if h >= 2:
                    pe.wait_ge(y_copied, h - 1)
                for s in range(TT):
                    last = nc.tensor.matmul(ps[base:base + 64, 6 + h % 2, 0:T], v_tok[:, s, HD * h:HD * h + HD],
                                            p_t[:, h % 2, s, :], start=(s == 0), stop=(s == 1))
                last.then_inc(valued, 1)

            @block.tensor
            def _(pe):
                for n in range(TT * H):
                    i, h = n // H, n % H
                    rows = slice(64 * (h % 2), 64 * (h % 2) + 64)
                    if n >= 4:
                        pe.wait_ge(added, n - 3)
                    nc.tensor.matmul(ps[:, n % 4, 0:T], cst("flip"), logits[:, i, h, :], start=True, stop=False)
                    nc.tensor.matmul(ps[:, n % 4, 0:T], pin[rows, C_Q + h // 2, P * i:P * i + P], k_t[rows, h // 2, :],
                                     start=False, stop=True).then_inc(dotted, 1)
                pe.wait_ge(scaled, TT)
                for h in range(H):
                    if h >= 2:
                        pe.wait_ge(p_copied, h - 1)
                    for i in range(TT):
                        for s in range(TT):
                            last = nc.tensor.transpose(ps[:, 4 + h % 2, T * s + P * i:T * s + P * i + P],
                                                       logits[:, i, h, P * s:P * s + P], cst("ident"))
                    last.then_inc(turned, 1)
                    if h >= 1:
                        values(pe, h - 1)
                values(pe, H - 1)

            @block.vector
            def _(dve):
                for n in range(TT * H):
                    i, h = n // H, n % H
                    dve.wait_ge(dotted, n + 1)
                    nc.vector.tensor_tensor(logits[:, i, h, :], ps[:, n % 4, 0:T], mask[:, i, :], ALU.add).then_inc(added, 1)
                    if h == H - 1:
                        dve.wait_ge(added, n + 1)
                        nc.vector.tensor_reduce(peak[:, i, :], logits[:, i, :, :], AX, ALU.max, negate=True).then_inc(peaked, 1)
                for i in range(TT):
                    dve.wait_ge(exped, H * (i + 1))
                    order.after(dve, nc.vector.reciprocal(total[:, i, :], total[:, i, :]))
                    nc.vector.tensor_tensor(logits[:, i, :, :], logits[:, i, :, :],
                                            total[:, i, :].unsqueeze(2).to_broadcast([P, H, T]), ALU.mult).then_inc(scaled, 1)
                for h in range(H):
                    base = 64 * (h % 2)
                    dve.wait_ge(valued, h + 1)
                    nc.vector.tensor_copy(y[base:base + 64, h // 2, :], ps[base:base + 64, 6 + h % 2, 0:T]).then_inc(y_copied, 1)

            @block.scalar
            def _(act):
                for n in range(TT * H):
                    i, h = n // H, n % H
                    if h == 0:
                        act.wait_ge(peaked, i + 1)
                    nc.scalar.activation(logits[:, i, h, :], logits[:, i, h, :], ACT.Exp, bias=peak[:, i, h:h + 1],
                                         accum_out=total[:, i, h:h + 1]).then_inc(exped, 1)
                for h in range(H):
                    act.wait_ge(turned, h + 1)
                    if h >= 2:
                        act.wait_ge(valued, h - 1)
                    nc.scalar.activation(p_t[:, h % 2, :, :].rearrange("p s q -> p (s q)"), ps[:, 4 + h % 2, :], ACT.Copy).then_inc(p_copied, 1)


def rwkv(pin, y, *, nc, d, sem, sbuf, par, cst, ps, ring, scratch, **_):
    with ExitStack() as scope:
        left = sbuf(scope, "left", [HC, NCH, 2 * CH])
        right = sbuf(scope, "right", [HC, NCH, 2 * CH])
        gate = sbuf(scope, "gate", [HC, T])
        bonus = sbuf(scope, "bonus", [HC, T])
        chunk_decay = sbuf(scope, "chunk_decay", [HC, NCH])
        with ExitStack() as inner:
            prepare_recurrence(inner, pin, left, right, gate, bonus, chunk_decay, nc=nc, d=d, sem=sem, sbuf=sbuf,
                               par=par, cst=cst, ps=ps)
        with ExitStack() as inner:
            pairs = inner.enter_context(nc.sbuf_tensor("pairs", [2 * CH, NCH, 2, HC, 2 * CH], F32))
            solve_corrections(pin, left, right, pairs, nc=nc, sem=sem, sbuf=sbuf, cst=cst, ps=ps, scratch=scratch)
            recur(pin, left, right, pairs, chunk_decay, y, nc=nc, sem=sem, sbuf=sbuf, cst=cst, ps=ps)
        with ExitStack() as inner:
            finish_rwkv(inner, y, gate, bonus, nc=nc, sem=sem, sbuf=sbuf, par=par, cst=cst, ps=ps)


def prepare_recurrence(scope, pin, left, right, gate, bonus, chunk_decay, *, nc, d, sem, sbuf, par, cst, ps):
    log_decay = sbuf(scope, "log_decay", [HC, T])
    icl = sbuf(scope, "icl", [HC, T])
    kk = sbuf(scope, "kk", [HC, T])
    t1 = sbuf(scope, "t1", [HC, T])
    t2 = sbuf(scope, "t2", [HC, T])
    lora = t1[:, 0:4, :].rearrange("p a b -> p (a b)")
    gate_up = t2[:, :, :].rearrange("p (k a) b -> p k (a b)", k=2)
    lora_in, squashed, ranked, unranked = sem("lora_in"), sem("squashed"), sem("ranked"), sem("unranked")
    with nc.Block() as block:
        @block.sync
        def _(sp):
            sp.dma_start(lora, d["lora"]).then_inc(lora_in, 16)
            sp.dma_start(gate_up, d["gate_up"]).then_inc(lora_in, 16)

        @block.scalar
        def _(act):
            nc.scalar.activation(pin[0:64, C_WA, :], pin[0:64, C_WA, :], ACT.Tanh).then_inc(squashed, 1)
            nc.scalar.activation(pin[:, C_G, :], pin[:, C_G, :], ACT.Sigmoid).then_inc(squashed, 1)
            nc.scalar.activation(pin[0:GATE_RANK - P, C_GI, :], pin[0:GATE_RANK - P, C_GI, :], ACT.Sigmoid).then_inc(squashed, 1)
            for n in range(3 * HC):
                c, kind = n // 3, n % 3
                act.wait_ge(ranked, n + 1)
                if kind < 2:
                    to, bias = (log_decay, par("w0", c)) if kind == 0 else (icl, par("a0", c))
                    nc.scalar.activation(to[:, c, :], ps[:, n % 8, 0:T], ACT.Sigmoid, bias=bias).then_inc(unranked, 1)
                else:
                    nc.scalar.activation(gate[:, c, :], ps[:, n % 8, 0:T], ACT.Copy).then_inc(unranked, 1)

        @block.tensor
        def _(pe):
            pe.wait_ge(lora_in, 32)
            pe.wait_ge(squashed, 3)
            for n in range(3 * HC):
                c, kind = n // 3, n % 3
                if n >= 8:
                    pe.wait_ge(unranked, n - 7)
                sums = ps[:, n % 8, 0:T]
                if kind < 2:
                    rows = slice(64 * kind, 64 * kind + 64)
                    last = nc.tensor.matmul(sums, lora[rows, P * c:P * c + P], pin[rows, C_WA, :], start=True, stop=True)
                else:
                    rows = slice(0, GATE_RANK - P)
                    nc.tensor.matmul(sums, gate_up[:, 0, P * c:P * c + P], pin[:, C_G, :], start=True, stop=False)
                    last = nc.tensor.matmul(sums, gate_up[rows, 1, P * c:P * c + P], pin[rows, C_GI, :], start=False, stop=True)
                last.then_inc(ranked, 1)

    k_squared, k_summed, k_rooted = sem("kk_squared"), sem("kk_summed"), sem("kk_rooted")
    bonus_ready, bonus_summed = sem("bonus_ready"), sem("bonus_summed")
    cum_ready, before_ready, exp_ready, taken = sem("cum_ready"), sem("before_ready"), sem("exp_ready"), sem("exp_taken")
    order = Order(sem("prepare_order"))
    r, k, v = pin[:, C_R:C_R + HC, :], pin[:, C_K:C_K + HC, :], pin[:, C_V:C_V + HC, :]
    sums = ps[:, 0:4, :].rearrange("p b (c t) -> p (b c) t", c=2)
    sums_b = ps[:, 4:8, :].rearrange("p b (c t) -> p (b c) t", c=2)

    def by_chunk(x):
        return x.rearrange("p c (n t) -> p (c n) t", t=CH)

    left_a, left_r = (left[:, :, :, i * CH:i * CH + CH].rearrange("p c n t -> p (c n) t") for i in range(2))
    right_b, right_k = (right[:, :, :, i * CH:i * CH + CH].rearrange("p c n t -> p (c n) t") for i in range(2))

    with nc.Block() as block:
        @block.vector
        def _(dve):
            for c in range(HC):
                order.mark(nc.vector.tensor_scalar(kk[:, c, :], pin[:, C_K + c, :], par("k_k", c), None, ALU.mult))
            order.settle(dve)
            order.after(dve, nc.vector.tensor_tensor(t1[:, :, :], kk[:, :, :], kk[:, :, :], ALU.mult))
            dve.sem_inc(k_squared, 1)
            for c in range(HC):
                order.mark(nc.vector.tensor_scalar(t2[:, c, :], icl[:, c, :], -1.0, par("k_a", c), ALU.add, ALU.mult))
            order.settle(dve)
            order.after(dve, nc.vector.scalar_tensor_tensor(k, t2[:, :, :], 1.0, k, ALU.add, ALU.mult))
            for c in range(HC):
                order.mark(nc.vector.scalar_tensor_tensor(t2[:, c, :], pin[:, C_R + c, :], par("r_k", c), pin[:, C_K + c, :], ALU.mult, ALU.mult))
            order.settle(dve)
            dve.sem_inc(bonus_ready, 1)
            dve.wait_ge(k_rooted, 1)
            order.after(dve, nc.vector.tensor_scalar(t1[:, :, :], t1[:, :, :], 1e-12, None, ALU.max))
            order.after(dve, nc.vector.reciprocal(t1[:, :, :], t1[:, :, :]))
            order.after(dve, nc.vector.tensor_tensor(kk[:, :, :], kk[:, :, :], t1[:, :, :], ALU.mult))
            dve.wait_ge(bonus_summed, 1)
            order.mark(nc.vector.tensor_tensor(bonus[:, :, :], sums_b, v, ALU.mult))
            order.after(dve, nc.vector.tensor_scalar(log_decay[:, :, :], log_decay[:, :, :], -EXP_HALF, None, ALU.mult))
            for c in range(HC):
                order.mark(nc.vector.tensor_tensor_scan(t1[:, c, :], cst("scan"), log_decay[:, c, :], 0.0, ALU.mult, ALU.add))
            order.settle(dve)
            order.after(dve, nc.vector.tensor_tensor(t2[:, :, :], t1[:, :, :], log_decay[:, :, :], ALU.subtract))
            dve.sem_inc(cum_ready, 1)
            dve.wait_ge(exp_ready, 1)
            order.after(dve, nc.vector.scalar_tensor_tensor(left_a, by_chunk(kk[:, :, :]), -1.0, by_chunk(t2[:, :, :]), ALU.mult, ALU.mult))
            order.after(dve, nc.vector.tensor_tensor(kk[:, :, :], kk[:, :, :], icl[:, :, :], ALU.mult))
            dve.wait_ge(exp_ready, 2)
            order.mark(nc.vector.tensor_tensor(right_b, by_chunk(kk[:, :, :]), by_chunk(log_decay[:, :, :]), ALU.mult))
            order.mark(nc.vector.tensor_tensor(right_k, by_chunk(k), by_chunk(log_decay[:, :, :]), ALU.mult))
            dve.wait_ge(exp_ready, 3)
            order.mark(nc.vector.tensor_tensor(left_r, by_chunk(r), by_chunk(t1[:, :, :]), ALU.mult))
            order.mark(nc.vector.tensor_copy(chunk_decay[:, :, :], t1[:, :, CH - 1::CH]))

        @block.tensor
        def _(pe):
            pe.wait_ge(k_squared, 1)
            for c in range(HC):
                last = nc.tensor.matmul(sums[:, c, :], cst("heads"), t1[:, c, :], start=True, stop=True)
            last.then_inc(k_summed, 1)
            pe.wait_ge(bonus_ready, 1)
            for c in range(HC):
                last = nc.tensor.matmul(sums_b[:, c, :], cst("heads"), t2[:, c, :], start=True, stop=True)
            last.then_inc(bonus_summed, 1)

        @block.scalar
        def _(act):
            act.wait_ge(k_summed, 1)
            nc.scalar.activation(t1[:, :, :], sums, ACT.Sqrt).then_inc(k_rooted, 1)
            act.wait_ge(cum_ready, 1)
            nc.scalar.activation(t2[:, :, :], t2[:, :, :], ACT.Exp).then_inc(exp_ready, 1)
            nc.scalar.activation(log_decay[:, :, :], t1[:, :, :], ACT.Exp, scale=-1.0).then_inc(exp_ready, 1)
            act.wait_ge(exp_ready, 2)
            nc.scalar.activation(t1[:, :, :], t1[:, :, :], ACT.Exp).then_inc(exp_ready, 1)


def solve_corrections(pin, left, right, pairs, *, nc, sem, sbuf, cst, ps, scratch):
    space = pin[:, C_Q:C_Q + 12, :].rearrange("p c t -> p (c t)")
    low, inverse, tmp = (space[:, CH * CH * i:CH * CH * (i + 1)].rearrange("p (j t) -> p j t", j=CH) for i in range(3))
    paired, masked = sem("paired"), sem("masked")
    out1, in1, out2, in2 = sem("low_out"), sem("low_in"), sem("inverse_out"), sem("inverse_in")
    solved = sem("solved")
    order = Order(sem("solve_order"))
    with nc.Block() as block:
        @block.tensor
        def _(pe):
            for n in range(NCH):
                for e in range(2):
                    rows = slice(64 * e, 64 * e + 64)
                    bank = (2 * n + e) % 8
                    if 2 * n + e >= 8:
                        pe.wait_ge(masked, 2 * n + e - 7)
                    for c in range(HC):
                        last = nc.tensor.matmul(ps[0:64, bank, 64 * c:64 * c + 64], right[rows, c, n, :], left[rows, c, n, :],
                                                start=True, stop=True)
                    last.then_inc(paired, 1)

        @block.vector
        def _(dve):
            mask = cst("decay_mask")[0:64, :].unsqueeze(1).to_broadcast([64, HC, 2 * CH])
            order.mark(nc.vector.memset(inverse, 0.0))
            for n in range(2 * NCH):
                dve.wait_ge(paired, n + 1)
                nc.vector.tensor_tensor(pairs[:, n // 2, n % 2, :, :], ps[0:64, n % 8, :].rearrange("p (c t) -> p c t", c=HC), mask,
                                        ALU.mult).then_inc(masked, 1)
            order.settle(dve)
            order.after(dve, nc.vector.memset(space[:, CH * CH:2 * CH * CH:CH + 1], 1.0))
            dve.wait_ge(in1, 16)
            for t in range(1, CH):
                by_s = low[:, 0:t, t].unsqueeze(1).to_broadcast([P, t, t])
                order.after(dve, nc.vector.tensor_tensor(tmp[:, 0:t, 0:t], inverse[:, 0:t, 0:t], by_s, ALU.mult))
                order.after(dve, nc.vector.tensor_reduce(inverse[:, 0:t, t], tmp[:, 0:t, 0:t], AX, ALU.add))
            dve.sem_inc(solved, 1)

        @block.sync
        def _(sp):
            sp.wait_ge(masked, 2 * NCH)
            block_ab = pairs[0:CH, :, :, :, 0:CH].rearrange("j n e c t -> j (n e c) t")
            sp.dma_start(scratch["solve_in"].rearrange("m j t -> j m t"), block_ab).then_inc(out1, 16)
            sp.wait_ge(out1, 16)
            sp.dma_start(low, scratch["solve_in"]).then_inc(in1, 16)
            sp.wait_ge(solved, 1)
            sp.dma_start(scratch["solve_out"], inverse).then_inc(out2, 16)
            sp.wait_ge(out2, 16)
            sp.dma_start(block_ab, scratch["solve_out"].rearrange("m j t -> j m t")).then_inc(in2, 16)
            sp.wait_ge(in2, 16)


def recur(pin, left, right, pairs, chunk_decay, y, *, nc, sem, sbuf, cst, ps):
    flat = pin[:, :, :].rearrange("p c t -> p (c t)")
    W = H * HD
    sv = pin[0:2 * CH, 0:8, :].rearrange("p (b c) t -> p b (c t)", b=2)
    wt = pin[0:2 * CH, 8:16, :].rearrange("p (b c) t -> p b (c t)", b=2)
    rhs = pin[0:CH, C_Q:C_Q + 4, :].rearrange("p c t -> p (c t)")
    state = pin[:, C_Q + 4:C_Q + 8, :].rearrange("p c t -> p (c t)").rearrange("p (c e v) -> p c e v", c=HC, e=2)
    v_bank, w_bank = ps[0:64, 0:2, :].rearrange("p b t -> p (b t)"), ps[0:64, 2:4, :].rearrange("p b t -> p (b t)")
    x_bank = ps[:, 4:6, :].rearrange("p b t -> p (b t)")
    s_bank = ps[:, 6:8, :].rearrange("p b t -> p (b t)")
    turned, v_copied, w_copied, cleared = sem("vw_turned"), sem("v_copied"), sem("w_copied"), sem("corrections_cleared")
    x_made, x_copied, s_made, s_copied = sem("rhs_made"), sem("rhs_copied"), sem("corrections_made"), sem("corrections_copied")
    st_made, st_added, st_done, y_made, y_copied = sem("state_made"), sem("state_added"), sem("state_done"), sem("y_made"), sem("y_copied")
    with nc.Block() as block:
        @block.tensor
        def _(pe):
            def turn(n):
                if n >= 1:
                    pe.wait_ge(v_copied, n)
                    pe.wait_ge(w_copied, n)
                for c in range(HC):
                    at = (C_V + c) * T + CH * (n - 1)
                    nc.tensor.transpose(v_bank[:, P * c:P * c + P], flat[:, at:at + 2 * CH], cst("ident"))
                    last = nc.tensor.transpose(w_bank[:, P * c:P * c + P], right[:, c, n, :], cst("ident"))
                last.then_inc(turned, 1)

            turn(0)
            for n in range(NCH):
                b = n % 2
                pe.wait_ge(v_copied, n + 1)
                pe.wait_ge(cleared, n + 1)
                pe.wait_ge(st_done, 2 * n + 1)
                for c in range(HC):
                    nc.tensor.matmul(x_bank[0:CH, P * c:P * c + P], left[:, c, n, 0:CH],
                                     state[:, c, :, :].rearrange("p e v -> p (e v)"), start=True, stop=True)
                    for e in range(2):
                        at = P * c + HD * e
                        last = nc.tensor.matmul(x_bank[0:CH, at:at + HD], pairs[:, n, e, c, 0:CH], sv[:, b, at:at + HD],
                                                start=False, stop=True, skip_group_check=True)
                last.then_inc(x_made, 1)
                if n + 1 < NCH:
                    turn(n + 1)
                pe.wait_ge(x_copied, n + 1)
                if n >= 1:
                    pe.wait_ge(y_copied, n)
                for c in range(HC):
                    for e in range(2):
                        at = P * c + HD * e
                        last = nc.tensor.matmul(s_bank[0:CH, at:at + HD], pairs[0:CH, n, e, c, 0:CH], rhs[:, at:at + HD],
                                                start=True, stop=True)
                last.then_inc(s_made, 1)
                pe.wait_ge(s_copied, n + 1)
                pe.wait_ge(w_copied, n + 1)
                if n + 1 < NCH:
                    for c in range(HC):
                        last = nc.tensor.matmul(x_bank[:, P * c:P * c + P], wt[:, b, P * c:P * c + P], sv[:, b, P * c:P * c + P],
                                                start=True, stop=True)
                    last.then_inc(st_made, 1)
                for c in range(HC):
                    to = s_bank[:, CH * c:CH * c + CH]
                    nc.tensor.matmul(to, state[:, c, :, :].rearrange("p e v -> p (e v)"), left[:, c, n, CH:2 * CH],
                                     start=True, stop=True)
                    for e in range(2):
                        at = P * c + HD * e
                        last = nc.tensor.matmul(to[64 * e:64 * e + 64, :], sv[:, b, at:at + HD], pairs[:, n, e, c, CH:2 * CH],
                                                start=False, stop=True, skip_group_check=True)
                last.then_inc(y_made, 1)

        @block.scalar
        def _(act):
            def take_v(n):
                act.wait_ge(turned, n + 1)
                if n >= 2:
                    act.wait_ge(y_made, n - 1)
                nc.scalar.activation(sv[CH:2 * CH, n % 2, :], v_bank[CH:2 * CH, :], ACT.Copy).then_inc(v_copied, 1)

            take_v(0)
            for n in range(NCH):
                act.wait_ge(x_made, n + 1)
                if n >= 1:
                    act.wait_ge(s_made, n)
                nc.scalar.activation(rhs, x_bank[0:CH, :], ACT.Copy).then_inc(x_copied, 1)
                if n + 1 < NCH:
                    take_v(n + 1)
                act.wait_ge(y_made, n + 1)
                nc.scalar.activation(y[:, :, CH * n:CH * n + CH], s_bank[:, 0:HC * CH].rearrange("p (c t) -> p c t", c=HC),
                                     ACT.Copy).then_inc(y_copied, 1)

        @block.vector
        def _(dve):
            nc.vector.memset(state, 0.0).then_inc(st_done, 1)
            for n in range(NCH):
                b = n % 2
                dve.wait_ge(turned, n + 1)
                if n >= 2:
                    dve.wait_ge(y_made, n - 1)
                nc.vector.memset(sv[0:CH, b, :], 0.0).then_inc(cleared, 1)
                nc.vector.tensor_copy(wt[:, b, :], w_bank).then_inc(w_copied, 1)
                dve.wait_ge(s_made, n + 1)
                nc.vector.tensor_copy(sv[0:CH, b, :], s_bank[0:CH, :]).then_inc(s_copied, 1)
                if n + 1 < NCH:
                    dve.wait_ge(st_made, n + 1)
                    dve.wait_ge(y_made, n + 1)
                    if n >= 1:
                        dve.wait_ge(st_done, 2 * n + 1)
                    for e in range(2):
                        rows = slice(64 * e, 64 * e + 64)
                        add = x_bank[rows, :].rearrange("p (c e v) -> p c e v", c=HC, e=2)[:, :, e, :]
                        nc.vector.tensor_tensor(state[rows, :, e, :], state[rows, :, e, :], add, ALU.add).then_inc(st_added, 1)
                    dve.wait_ge(st_added, 2 * n + 2)
                    for e in range(2):
                        rows = slice(64 * e, 64 * e + 64)
                        nc.vector.tensor_tensor(state[rows, :, e, :], state[rows, :, e, :],
                                                chunk_decay[rows, :, n].unsqueeze(2).to_broadcast([64, HC, HD]), ALU.mult).then_inc(st_done, 1)


def finish_rwkv(scope, y, gate, bonus, *, nc, sem, sbuf, par, cst, ps):
    sq = sbuf(scope, "y_squared", [HC, T])
    meaned, centered, summed, rooted = sem("y_meaned"), sem("y_centered"), sem("y_summed"), sem("y_rooted")
    order = Order(sem("finish_order"))
    means = ps[:, 0:4, :].rearrange("p b (c t) -> p (b c) t", c=2)
    sums = ps[:, 4:8, :].rearrange("p b (c t) -> p (b c) t", c=2)
    with nc.Block() as block:
        @block.tensor
        def _(pe):
            for c in range(HC):
                last = nc.tensor.matmul(means[:, c, :], cst("heads"), y[:, c, :], start=True, stop=True)
            last.then_inc(meaned, 1)
            pe.wait_ge(centered, 1)
            for c in range(HC):
                last = nc.tensor.matmul(sums[:, c, :], cst("heads"), sq[:, c, :], start=True, stop=True)
            last.then_inc(summed, 1)

        @block.scalar
        def _(act):
            act.wait_ge(summed, 1)
            nc.scalar.activation(sq[:, :, :], sums, ACT.Sqrt, bias=cst("eps_gn"), scale=1.0 / HD).then_inc(rooted, 1)

        @block.vector
        def _(dve):
            dve.wait_ge(meaned, 1)
            order.after(dve, nc.vector.scalar_tensor_tensor(y[:, :, :], means, -1.0 / HD, y[:, :, :], ALU.mult, ALU.add))
            nc.vector.tensor_tensor(sq[:, :, :], y[:, :, :], y[:, :, :], ALU.mult).then_inc(centered, 1)
            dve.wait_ge(rooted, 1)
            order.after(dve, nc.vector.reciprocal(sq[:, :, :], sq[:, :, :]))
            order.after(dve, nc.vector.tensor_tensor(y[:, :, :], y[:, :, :], sq[:, :, :], ALU.mult))
            for c in range(HC):
                order.mark(nc.vector.tensor_scalar(y[:, c, :], y[:, c, :], par("ln_x_w", c), par("ln_x_b", c), ALU.mult, ALU.add))
            order.settle(dve)
            order.after(dve, nc.vector.tensor_tensor(y[:, :, :], y[:, :, :], bonus[:, :, :], ALU.add))
            nc.vector.tensor_tensor(y[:, :, :], y[:, :, :], gate[:, :, :], ALU.mult)


def mix_branches(gates, mixed, xn, y_rwkv, y_dsa, *, nc, d, sem, ring, ps, **_):
    def to_gates(act, g, sums, half):
        nc.scalar.activation(gates[:, bass.ds(4 * g, 4), :], sums, ACT.Sigmoid).then_inc(ring.evacuated, 1)

    def first(dve, g, sums, half):
        nc.vector.tensor_tensor(mixed[:, bass.ds(4 * g, 4), :], sums, gates[:, bass.ds(4 * g, 4), :], ALU.mult).then_inc(ring.evacuated, 1)

    gated = sem("branch_gated")

    def second(dve, g, sums, half):
        b = gates[:, bass.ds(DC + 4 * g, 4), :]
        nc.vector.tensor_tensor(b, sums, b, ALU.mult).then_inc(ring.evacuated, 1)
        dve.wait_ge(ring.evacuated, ring.groups + g + 1)
        m = mixed[:, bass.ds(4 * g, 4), :]
        nc.vector.tensor_tensor(m, m, b, ALU.add).then_inc(gated, 1)

    linear(nc, ring, ps, d["w_gates"], 2 * DC, xn, dict(scalar=to_gates), d["w_branch_rwkv"])
    linear(nc, ring, ps, d["w_branch_rwkv"], DC, y_rwkv, dict(vector=first), d["w_branch_dsa"])
    linear(nc, ring, ps, d["w_branch_dsa"], DC, y_dsa, dict(vector=second), d["w_out"])


def add_mixed(mixed, h, *, nc, d, sem, ring, ps, **_):
    x_in = sem("x_again")
    with nc.Block() as block:
        @block.sync
        def _(sp):
            sp.dma_start(h[:, :, :], d["x"]).then_inc(x_in, 16)
            sp.wait_ge(x_in, 16)

    def add(dve, g, sums, half):
        to = h[:, bass.ds(4 * g, 4), :]
        nc.vector.tensor_tensor(to, sums, to, ALU.add).then_inc(ring.evacuated, 1)

    linear(nc, ring, ps, d["w_out"], DC, mixed, dict(vector=add))


def peer(h, x1, *, nc, d, sem, sbuf, par, par_at, cst, ps, ring, **_):
    with ExitStack() as scope:
        h_tok = sbuf(scope, "h_tok", [TT, D])
        tmp = sbuf(scope, "ffn_rms", [T])
        expert = sbuf(scope, "expert", [TT, PK_SEL], U32)
        weight = sbuf(scope, "weight", [TT, PK_SEL])
        with ExitStack() as inner:
            hn = sbuf(inner, "hn", [DC, T])
            query = sbuf(inner, "query", [DC, T])
            rmsnorm(nc, sem, cst, ps, h[:, :, :], hn[:, :, :], par("norm_ffn", 0, DC), tmp[:, :], DC, "eps_rms",
                    lambda sp: ring.prefetch(sp, d["w_query"], ring.parts))
            linear(nc, ring, ps, d["w_query"], DC, hn, dict(scalar=copy_out(nc, ring, query)))
            choose_experts(query, hn, h_tok, expert, weight, nc=nc, d=d, sem=sem, sbuf=sbuf, cst=cst, ps=ps)
        run_experts(h, h_tok, expert, weight, nc=nc, d=d, sem=sem, sbuf=sbuf, cst=cst, ps=ps)
        rmsnorm(nc, sem, cst, ps, h[:, :, :], x1[:, :, :], par("norm_final", 0, DC), tmp[:, :], DC, "eps_rms",
                lambda sp: ring.prefetch(sp, d["a_w_z"], ring.parts))


def choose_experts(query, hn, h_tok, expert, weight, *, nc, d, sem, sbuf, cst, ps):
    S = 2 * PK_HEADS
    K = PK_TOP
    with ExitStack() as scope:
        keys = sbuf(scope, "keys", [S, PK_KEYS])
        score = sbuf(scope, "key_score", [S, PK_KEYS])
        rest = sbuf(scope, "key_rest", [S, PK_KEYS])
        best = sbuf(scope, "best", [S, K])
        best_at = sbuf(scope, "best_at", [S, K], U32)
        best_f = sbuf(scope, "best_f", [S, K])
        cand = sbuf(scope, "cand", [PK_HEADS, K * K])
        cand_rest = sbuf(scope, "cand_rest", [PK_HEADS, K * K])
        top = sbuf(scope, "top_sum", [PK_HEADS, K])
        top_at = sbuf(scope, "top_sum_at", [PK_HEADS, K], U32)
        part = sbuf(scope, "part", [2, PK_HEADS, K], U32)
        part_f = sbuf(scope, "part_f", [2, PK_HEADS, K])
        half_id = sbuf(scope, "half_id", [2, PK_HEADS, K])
        total = sbuf(scope, "gate_total", [PK_HEADS])
        keys_in, turned, h_copied = sem("keys_in"), sem("h_turned"), sem("h_copied")
        scored, s_copied, searched = sem("keys_scored"), sem("keys_copied"), sem("keys_searched")
        shifted, exped = sem("gate_shifted"), sem("gate_exped")
        order = Order(sem("choose_order"))

        def top16(dve, jobs):
            V = nc.vector
            for x, _, v, _ in jobs:
                order.mark(V.max(v[:, 0:8], x))
            order.settle(dve)
            for x, r, v, at in jobs:
                order.mark(V.max_index(at[:, 0:8], v[:, 0:8], x))
                order.mark(V.match_replace(r, v[:, 0:8], x, TAKEN))
            order.settle(dve)
            for _, r, v, _ in jobs:
                order.mark(V.max(v[:, 8:16], r))
            order.settle(dve)
            for _, r, v, at in jobs:
                order.mark(V.max_index(at[:, 8:16], v[:, 8:16], r))
            order.settle(dve)

        with nc.Block() as block:
            @block.sync
            def _(sp):
                sp.dma_start(keys[:, :, :], d["sub_keys"]).then_inc(keys_in, 16)

            @block.tensor
            def _(pe):
                pe.wait_ge(keys_in, 16)
                for i in range(TT):
                    if i:
                        pe.wait_ge(s_copied, i)
                    for s in range(S):
                        last = nc.tensor.matmul(ps[:, s // 4, PK_KEYS * (s % 4):PK_KEYS * (s % 4) + PK_KEYS],
                                                query[:, s, P * i:P * i + P], keys[:, s, :], start=True, stop=True)
                    last.then_inc(scored, 1)
                    if i:
                        pe.wait_ge(h_copied, i)
                    for c in range(DC):
                        last = nc.tensor.transpose(ps[:, 4 + c // 4, P * (c % 4):P * (c % 4) + P], hn[:, c, P * i:P * i + P], cst("ident"))
                    last.then_inc(turned, 1)

            @block.scalar
            def _(act):
                for i in range(TT):
                    act.wait_ge(scored, i + 1)
                    if i:
                        act.wait_ge(searched, i)
                    nc.scalar.activation(score[:, :, :], ps[:, 0:4, :].rearrange("p b (s n) -> p (b s) n", s=4), ACT.Copy).then_inc(s_copied, 1)
                    act.wait_ge(turned, i + 1)
                    nc.scalar.activation(h_tok[:, i, :], ps[:, 4:8, :].rearrange("p b n -> p (b n)"), ACT.Copy).then_inc(h_copied, 1)
                    act.wait_ge(shifted, i + 1)
                    w = weight[:, i, :]
                    nc.scalar.activation(w, w, ACT.Exp).then_inc(exped, 1)

            @block.vector
            def _(dve):
                V = nc.vector
                wide = [P, PK_HEADS, K, K]
                for i in range(TT):
                    dve.wait_ge(s_copied, i + 1)
                    top16(dve, [(score[:, s, :], rest[:, s, :], best[:, s, :], best_at[:, s, :]) for s in range(S)])
                    dve.sem_inc(searched, 1)
                    order.mark(V.tensor_copy(best_f[:, :, :], best_at[:, :, :]))
                    c4 = cand[:, :, :].rearrange("p h (a b) -> p h a b", a=K)
                    order.after(dve, V.tensor_tensor(c4, best[:, 0::2, :].unsqueeze(3).to_broadcast(wide),
                                                     best[:, 1::2, :].unsqueeze(2).to_broadcast(wide), ALU.add))
                    top16(dve, [(cand[:, h, :], cand_rest[:, h, :], top[:, h, :], top_at[:, h, :]) for h in range(PK_HEADS)])
                    w = weight[:, i, :].rearrange("p (h k) -> p h k", h=PK_HEADS)
                    V.tensor_tensor(w, top[:, :, :], top[:, :, 0:1].to_broadcast([P, PK_HEADS, K]), ALU.subtract).then_inc(shifted, 1)
                    order.mark(V.tensor_scalar(part[:, 0, :, :], top_at[:, :, :], 4, None, ALU.logical_shift_right))
                    order.mark(V.tensor_scalar(part[:, 1, :, :], top_at[:, :, :], 15, None, ALU.bitwise_and))
                    order.settle(dve)
                    order.after(dve, V.tensor_copy(part_f[:, :, :, :], part[:, :, :, :]))
                    for half in range(2):
                        order.after(dve, V.tensor_tensor(c4, part_f[:, half, :, :].unsqueeze(3).to_broadcast(wide),
                                                         cst("iota").unsqueeze(1).unsqueeze(1).to_broadcast(wide), ALU.is_equal))
                        order.after(dve, V.tensor_tensor(c4, c4, best_f[:, half::2, :].unsqueeze(2).to_broadcast(wide), ALU.mult))
                        order.after(dve, V.tensor_reduce(half_id[:, half, :, :], c4, AX, ALU.add))
                    e = half_id[:, 0, :, :]
                    order.after(dve, V.scalar_tensor_tensor(e, e, float(PK_KEYS), half_id[:, 1, :, :], ALU.mult, ALU.add))
                    order.mark(V.tensor_copy(expert[:, i, :].rearrange("p (h k) -> p h k", h=PK_HEADS), e))
                    dve.wait_ge(exped, i + 1)
                    order.after(dve, V.tensor_reduce(total[:, :], w, AX, ALU.add))
                    order.after(dve, V.reciprocal(total[:, :], total[:, :]))
                    order.after(dve, V.tensor_tensor(w, w, total[:, :].unsqueeze(2).to_broadcast([P, PK_HEADS, K]), ALU.mult))


def run_experts(h, h_tok, expert, weight, *, nc, d, sem, sbuf, cst, ps):
    SLOTS = 8
    BY_VECTOR = (3, 7)
    BY_TENSOR = [s for s in range(SLOTS) if s not in BY_VECTOR]
    TURNS = PK_SEL // SLOTS
    with ExitStack() as scope:
        row = sbuf(scope, "row", [SLOTS, D])
        index = sbuf(scope, "index", [SLOTS], U32)
        product = sbuf(scope, "product", [D])
        dot = sbuf(scope, "dot", [2, SLOTS])
        act_in = sbuf(scope, "act_in", [TT, PK_SEL])
        diag = sbuf(scope, "diag", [SLOTS, P])
        zero = sbuf(scope, "zero", [P])
        partial = sbuf(scope, "partial", [TT, D])
        index_set = sem("index_set")
        index_seen = sem("index_seen")
        arrived = [sem(f"row_arrived{s}") for s in range(SLOTS)]
        row_free = [sem(f"row_free{s}") for s in range(SLOTS)]
        diag_ready = [sem(f"diag_ready{s}") for s in range(SLOTS)]
        dotted, collected, gelued, weighted, zeroed = sem("dotted8"), sem("collected"), sem("gelued"), sem("weighted"), sem("zeroed")
        summed, sum_copied, turned_back = sem("experts_summed"), sem("sum_copied"), sem("turned_back")
        partial_added, sum_whole = sem("partial_added"), sem("sum_whole")
        with nc.Block() as block:
            @block.gpsimd
            def _(pool):
                for i in range(2 * TT):
                    table = d["peer_u"] if i < TT else d["peer_v"]
                    with pool.Fori(0, TURNS) as t:
                        for s in range(SLOTS):
                            at = TURNS * i + t
                            pool.wait_ge(row_free[s], at + 1)
                            nc.gpsimd.tensor_copy(index[:, s:s + 1], expert[:, i % TT, bass.ds(SLOTS * t + s, 1)]).then_inc(index_set, 1)
                            pool.wait_ge(index_set, SLOTS * at + s + 1)
                            pool.sem_inc(index_seen, 1)
                            nc.gpsimd.indirect_dma_start(row[:, s, :], None, table, bass.IndirectOffsetOnAxis(ap=index[:, s:s + 1], axis=0)).then_inc(arrived[s], 16)

            @block.vector
            def _(dve):
                V = nc.vector
                V.memset(zero[:, :], 0.0).then_inc(zeroed, 1)
                V.memset(partial[:, :, :], 0.0).then_inc(partial_added, 1)
                for s in range(SLOTS):
                    dve.sem_inc(row_free[s], 1)
                for i in range(TT):
                    with dve.Fori(0, TURNS) as t:
                        at = TURNS * i + t
                        for s in range(SLOTS):
                            dve.wait_ge(arrived[s], 16 * at + 16)
                            V.tensor_tensor_reduce(product[:, :], row[:, s, :], h_tok[:, i, :], 1.0, 0.0, ALU.mult, ALU.add,
                                                   dot[:, 0, s:s + 1]).then_inc(row_free[s], 1)
                            dve.wait_ge(row_free[s], at + 2)
                        V.tensor_copy(act_in[:, i, bass.ds(SLOTS * t, SLOTS)], dot[:, 0, :]).then_inc(collected, 1)
                        dve.wait_ge(collected, at + 1)
                for i in range(TT):
                    dve.wait_ge(gelued, i + 1)
                    V.tensor_tensor(weight[:, i, :], weight[:, i, :], act_in[:, i, :], ALU.mult).then_inc(weighted, 1)
                dve.wait_ge(weighted, TT)
                for i in range(TT):
                    with dve.Fori(0, TURNS) as t:
                        at = TURNS * i + t
                        for s in BY_TENSOR:
                            dve.wait_ge(row_free[s], TT * TURNS + at + 1)
                            V.tensor_scalar(diag[:, s, :], cst("ident"), weight[:, i, bass.ds(SLOTS * t + s, 1)], None, ALU.mult).then_inc(diag_ready[s], 1)
                        for n, s in enumerate(BY_VECTOR):
                            dve.wait_ge(arrived[s], 16 * (TT * TURNS + at) + 16)
                            dve.wait_ge(partial_added, len(BY_VECTOR) * at + n + 1)
                            V.scalar_tensor_tensor(partial[:, i, :], row[:, s, :], weight[:, i, bass.ds(SLOTS * t + s, 1)], partial[:, i, :],
                                                   ALU.mult, ALU.add).then_inc(partial_added, 1)
                            dve.wait_ge(partial_added, len(BY_VECTOR) * at + n + 2)
                            dve.sem_inc(row_free[s], 1)
                for i in range(TT):
                    dve.wait_ge(sum_copied, i + 1)
                    V.tensor_tensor(h_tok[:, i, :], h_tok[:, i, :], partial[:, i, :], ALU.add).then_inc(sum_whole, 1)
                for i in range(TT):
                    for q in range(4):
                        dve.wait_ge(turned_back, 4 * i + q + 1)
                        to = h[:, 4 * q:4 * q + 4, P * i:P * i + P]
                        V.tensor_tensor(to, to, ps[:, 4 * i + q, :].rearrange("p (c t) -> p c t", c=4), ALU.add)

            @block.scalar
            def _(act):
                for i in range(TT):
                    act.wait_ge(collected, TURNS * (i + 1))
                    nc.scalar.activation(act_in[:, i, :], act_in[:, i, :], ACT.Gelu).then_inc(gelued, 1)
                for i in range(TT):
                    act.wait_ge(summed, i + 1)
                    nc.scalar.activation(h_tok[:, i, :], ps[:, 4 * i:4 * i + 4, :].rearrange("p b n -> p (b n)"), ACT.Copy).then_inc(sum_copied, 1)

            @block.tensor
            def _(pe):
                pe.wait_ge(zeroed, 1)
                for i in range(TT):
                    for q in range(4):
                        nc.tensor.matmul(ps[:, 4 * i + q, :], zero[:, :], h_tok[:, i, 512 * q:512 * q + 512],
                                         start=True, stop=False)
                    with pe.Fori(0, TURNS) as t:
                        at = TURNS * i + t
                        for s in BY_TENSOR:
                            pe.wait_ge(arrived[s], 16 * (TT * TURNS + at) + 16)
                            pe.wait_ge(diag_ready[s], at + 1)
                            for q in range(4):
                                last = nc.tensor.matmul(ps[:, 4 * i + q, :], diag[:, s, :], row[:, s, 512 * q:512 * q + 512],
                                                        start=False, stop=False)
                            last.then_inc(row_free[s], 1)
                    for q in range(4):
                        last = nc.tensor.matmul(ps[:, 4 * i + q, :], zero[:, :], h_tok[:, i, 512 * q:512 * q + 512], start=False, stop=True)
                    last.then_inc(summed, 1)
                for i in range(TT):
                    pe.wait_ge(sum_whole, i + 1)
                    for q in range(4):
                        for c in range(4):
                            at = P * (4 * q + c)
                            last = nc.tensor.transpose(ps[:, 4 * i + q, P * c:P * c + P], h_tok[:, i, at:at + P], cst("ident"))
                        last.then_inc(turned_back, 1)


def mamba(x1, x2, z, xbc, recycle, *, nc, d, sem, sbuf, par, par_at, cst, ps, ring, **_):
    with ExitStack() as scope:
        dt = sbuf(scope, "dt", [2, T])
        with ExitStack() as inner:
            project_mamba(inner, x1, z, xbc, dt, nc=nc, d=d, sem=sem, sbuf=sbuf, par=par, par_at=par_at, cst=cst, ps=ps, ring=ring)
        with ExitStack() as inner:
            ssd(inner, xbc, dt, nc=nc, sem=sem, sbuf=sbuf, par=par, cst=cst, ps=ps)
        with ExitStack() as inner:
            gate_groups(inner, xbc, z, nc=nc, sem=sem, sbuf=sbuf, par=par, cst=cst, ps=ps,
                        prefetch=lambda sp: ring.prefetch(sp, d["a_w_out"], ring.parts))

        def add(dve, g, sums, half):
            nc.vector.scalar_tensor_tensor(x2[:, bass.ds(4 * g, 4), :], x1[:, bass.ds(4 * g, 4), :], ALPHA, sums,
                                           ALU.mult, ALU.add).then_inc(ring.evacuated, 1)

        linear(nc, ring, ps, d["a_w_out"], DC, xbc[:, 0:ZC, :], dict(vector=add), d["w_k"])
    layernorm(x2, 0, nc=nc, sem=sem, sbuf=sbuf, par=par, cst=cst, ps=ps)


def layernorm(x, layer, *, nc, sem, sbuf, par, cst, ps):
    with ExitStack() as scope:
        sq = sbuf(scope, f"ln_squared{layer}", [DC, T])
        rstd = sbuf(scope, f"ln_rstd{layer}", [T])
        mean = sbuf(scope, f"ln_mean{layer}", [T])
        meaned, centered, squared, summed, rooted = (sem("ln_meaned"), sem("ln_centered"), sem("ln_squared"),
                                                     sem("ln_summed"), sem("ln_rooted"))
        order = Order(sem("ln_order"))
        with nc.Block() as block:
            @block.tensor
            def _(pe):
                sum_over_channels(pe, nc, cst("ones"), x, ps[:, 0, 0:T], DC).then_inc(meaned, 1)
                pe.wait_ge(squared, 1)
                sum_over_channels(pe, nc, cst("ones"), sq, ps[:, 1, 0:T], DC).then_inc(summed, 1)

            @block.scalar
            def _(act):
                act.wait_ge(centered, 1)
                nc.scalar.activation(sq[:, :, :], x[:, :, :], ACT.Square).then_inc(squared, 1)
                act.wait_ge(summed, 1)
                nc.scalar.activation(rstd[:, :], ps[:, 1, 0:T], ACT.Sqrt, bias=cst("eps_2"), scale=1.0 / D).then_inc(rooted, 1)

            @block.vector
            def _(dve):
                dve.wait_ge(meaned, 1)
                order.after(dve, nc.vector.tensor_scalar(mean[:, :], ps[:, 0, 0:T], 1.0 / D, None, ALU.mult))
                nc.vector.tensor_tensor(x[:, :, :], x[:, :, :], mean[:, :].unsqueeze(1).to_broadcast([P, DC, T]), ALU.subtract).then_inc(centered, 1)
                dve.wait_ge(centered, 1)
                dve.wait_ge(rooted, 1)
                order.after(dve, nc.vector.reciprocal(rstd[:, :], rstd[:, :]))
                for c in range(DC):
                    order.mark(nc.vector.scalar_tensor_tensor(x[:, c, :], x[:, c, :], par("ln_g", DC * layer + c), rstd[:, :],
                                                              ALU.mult, ALU.mult))
                order.settle(dve)
                for c in range(DC):
                    nc.vector.tensor_scalar(x[:, c, :], x[:, c, :], par("ln_b", DC * layer + c), None, ALU.add)


def project_mamba(scope, x1, z, xbc, dt, *, nc, d, sem, sbuf, par, par_at, cst, ps, ring):
    TAPS = 4
    raw = sbuf(scope, "conv_raw", [2, 4, TAPS - 1 + T])
    cleared = sem("conv_cleared")
    with nc.Block() as block:
        @block.vector
        def _(dve):
            nc.vector.memset(raw[:, :, :, 0:TAPS - 1], 0.0).then_inc(cleared, 1)

    def silu_z(act, g, sums, half):
        nc.scalar.activation(z[:, bass.ds(4 * g, 4), :], sums, ACT.Silu).then_inc(ring.evacuated, 1)

    linear(nc, ring, ps, d["a_w_z"], ZC, x1, dict(scalar=silu_z), d["a_w_conv"])

    raw_ready, tapped, activated = sem("conv_raw_ready"), sem("conv_tapped"), sem("conv_activated")

    def activate(act, g):
        act.wait_ge(tapped, TAPS * g + TAPS)
        to = xbc[:, bass.ds(4 * g, 4), :]
        nc.scalar.activation(to, to, ACT.Silu).then_inc(activated, 1)

    def evac(act, g, sums, half):
        if not isinstance(g, int) or g > 0:
            activate(act, g - 1)
        nc.scalar.activation(raw[:, half, :, TAPS - 1:TAPS - 1 + T], sums, ACT.Copy).then_inc(ring.evacuated, 1)

    g0 = ring.groups

    def conv(dve, g, sums, half):
        dve.wait_ge(ring.evacuated, g0 + g + 1)
        for n in range(4):
            last = nc.vector.tensor_scalar(xbc[:, bass.ds(4 * g + n, 1), :], raw[:, half, n:n + 1, TAPS - 1:TAPS - 1 + T],
                                           par_at("conv_w", 3 * CONVC + 4 * g + n), par_at("conv_b", 4 * g + n), ALU.mult, ALU.add)
        last.then_inc(tapped, 1)
        for tap in range(TAPS - 1):
            dve.wait_ge(tapped, TAPS * g + tap + 1)
            for n in range(4):
                to = xbc[:, bass.ds(4 * g + n, 1), :]
                last = nc.vector.scalar_tensor_tensor(to, raw[:, half, n:n + 1, tap:tap + T], par_at("conv_w", tap * CONVC + 4 * g + n), to,
                                                      ALU.mult, ALU.add)
            last.then_inc(tapped, 1)

    linear(nc, ring, ps, d["a_w_conv"], CONVC, x1, dict(scalar=evac, vector=conv), d["a_w_dt"])

    def take_dt(act, g, sums, half):
        activate(act, CONVC // 4 - 1)
        nc.scalar.activation(dt[0:SSM_H, 0, :], sums[0:SSM_H, 0, :], ACT.Copy).then_inc(ring.evacuated, 1)

    linear(nc, ring, ps, d["a_w_dt"], 1, x1, dict(scalar=take_dt))


def ssd(scope, xbc, dt, *, nc, sem, sbuf, par, cst, ps):
    heads_a = GROUPS
    cum = sbuf(scope, "cum", [T])
    a = sbuf(scope, "a", [1])
    dt_tok = sbuf(scope, "dt_tok", [TT, SSM_H])
    cum_tok = sbuf(scope, "cum_tok", [TT, SSM_H])
    last_tok = sbuf(scope, "last_tok", [SSM_H])
    xdt = sbuf(scope, "xdt", [2, TT, 512])
    xst = sbuf(scope, "xst", [512])
    b_tok = sbuf(scope, "b_tok", [P])
    cb = sbuf(scope, "cb", [2, P])
    pair = sbuf(scope, "pair", [2, 8, P])
    off_side = sbuf(scope, "off_side", [8, P])
    state = sbuf(scope, "state", [512])
    tmp = sbuf(scope, "ssd_tmp", [T])
    order = Order(sem("ssd_order"))
    act_order = Order(sem("ssd_act_order"))
    dt_done, cum_done, dt_turned, tok_copied, last_made = (sem("dt_done"), sem("cum_done"), sem("dt_turned"), sem("tok_copied"),
                                                           sem("last_made"))
    with nc.Block() as block:
        @block.scalar
        def _(act):
            raw, d1, t = dt[0:SSM_H, 0, :], dt[0:SSM_H, 1, :], tmp[0:SSM_H, :]
            act_order.after(act, nc.scalar.activation(raw, raw, ACT.Identity, bias=par("dt_bias")[0:SSM_H]))
            act_order.after(act, nc.scalar.activation(t, raw, ACT.Abs))
            act_order.after(act, nc.scalar.activation(t, t, ACT.Exp, scale=-1.0))
            act_order.after(act, nc.scalar.activation(t, t, ACT.Ln, bias=1.0))
            act_order.after(act, nc.scalar.activation(d1, raw, ACT.Relu))
            nc.scalar.activation(a[0:SSM_H, :], par("a_log")[0:SSM_H], ACT.Exp).then_inc(dt_done, 1)

        @block.vector
        def _(dve):
            V = nc.vector
            d1, t = dt[0:SSM_H, 1, :], tmp[0:SSM_H, :]
            dve.wait_ge(dt_done, 1)
            order.after(dve, V.tensor_tensor(d1, d1, t, ALU.add))
            order.after(dve, V.tensor_scalar(t, d1, a[0:SSM_H, :], -1.0, ALU.mult, ALU.mult))
            ones = cst("ones")[0:SSM_H, :]
            for i in range(TT):
                w = slice(P * i, P * i + P)
                order.mark(V.tensor_tensor_scan(cum[0:SSM_H, w], ones, t[:, w], 0.0, ALU.mult, ALU.add))
            order.settle(dve)
            dve.sem_inc(cum_done, 1)
            dve.wait_ge(dt_turned, 1)
            order.mark(V.tensor_copy(dt_tok[:, :, :], ps[:, 0, 0:P].rearrange("p (i h) -> p i h", i=TT)))
            order.mark(V.tensor_copy(cum_tok[:, :, :], ps[:, 1, 0:P].rearrange("p (i h) -> p i h", i=TT)))
            order.settle(dve)
            dve.wait_ge(last_made, 1)
            order.mark(V.tensor_tensor(last_tok[:, :], ps[:, 2, 0:SSM_H], cum_tok[:, 0, :], ALU.subtract))
            order.settle(dve)
            dve.sem_inc(tok_copied, 1)

        @block.tensor
        def _(pe):
            pe.wait_ge(cum_done, 1)
            ident = cst("ident")[0:SSM_H, 0:SSM_H]
            for i in range(TT):
                w = slice(P * i, P * i + P)
                nc.tensor.transpose(ps[:, 0, SSM_H * i:SSM_H * i + SSM_H], dt[0:SSM_H, 1, w], ident)
                last = nc.tensor.transpose(ps[:, 1, SSM_H * i:SSM_H * i + SSM_H], cum[0:SSM_H, w], ident)
            last.then_inc(dt_turned, 1)
            nc.tensor.matmul(ps[:, 2, 0:SSM_H], cum[0:SSM_H, P - 1:P].to_broadcast([SSM_H, P]), ident, start=True, stop=True).then_inc(last_made, 1)

    with nc.Block() as block:
        @block.scalar
        def _(act):
            nc.scalar.activation(last_tok[:, :], last_tok[:, :], ACT.Exp)

    x_turned, xdt_made, xst_made, b_turned, b_copied = sem("x_turned"), sem("xdt_made"), sem("xst_made"), sem("b_turned"), sem("b_copied")
    cb_made, cb_masked, spread, differed, decayed, pair_made = (sem("cb_made"), sem("cb_masked"), sem("cum_spread"), sem("differed"),
                                                              sem("decayed"), sem("pair_made"))
    grown, off_made, state_made, state_copied = sem("grown"), sem("off_made"), sem("state_copied_p"), sem("ssm_state_copied")
    y_made, y_added = sem("ssm_y_made"), sem("ssm_y_added")
    UNITS = GROUPS * TT
    b_chunk, c_chunk = ZC, ZC + GROUPS
    masks = sbuf(scope, "causal", [P])
    masked_ready = sem("causal_ready")

    def xd(g):
        return xdt[:, g % 2, :, :]

    with nc.Block() as block:
        @block.gpsimd
        def _(pool):
            nc.gpsimd.affine_select(out=masks[:, :], in_=cst("ones"), compare_op=ALU.is_ge, fill=0.0, base=0, pattern=[[1, P]],
                                    channel_multiplier=-1).then_inc(masked_ready, 1)

        @block.tensor
        def _(pe):
            for g in range(GROUPS):
                if g:
                    pe.wait_ge(y_added, 2 * g)
                for i in range(TT):
                    for c in range(4):
                        last = nc.tensor.transpose(ps[:, i, P * c:P * c + P], xbc[:, 4 * g + c, P * i:P * i + P], cst("ident"))
                    last.then_inc(x_turned, 1)
                if g:
                    pe.wait_ge(state_copied, g)
                    pe.wait_ge(cb_masked, 2 * g)
                nc.tensor.transpose(ps[:, 3, 0:P], xbc[:, b_chunk + g, 0:P], cst("ident")).then_inc(b_turned, 1)
                for i in range(TT):
                    w = slice(P * i, P * i + P)
                    nc.tensor.matmul(ps[:, 2, P * i:P * i + P], xbc[:, b_chunk + g, w], xbc[:, c_chunk + g, w],
                                     start=True, stop=True).then_inc(cb_made, 1)
                if g:
                    pe.wait_ge(differed, 2 * g)
                    pe.wait_ge(grown, g)
                for i in range(TT):
                    for e in range(8):
                        h = 8 * g + e
                        last = nc.tensor.matmul(ps[:, 4 + 2 * i + e // 4, P * (e % 4):P * (e % 4) + P],
                                                cst("ident")[0:SSM_H, h:h + 1].to_broadcast([SSM_H, P]), cum[0:SSM_H, P * i:P * i + P],
                                                start=True, stop=True)
                    last.then_inc(spread, 1)
                pe.wait_ge(b_copied, g + 1)
                pe.wait_ge(xst_made, g + 1)
                nc.tensor.matmul(ps[:, 3, :], b_tok[:, :], xst[:, :], start=True, stop=True).then_inc(state_made, 1)
                pe.wait_ge(xdt_made, 2 * g + 2)
                for i in range(TT):
                    pe.wait_ge(pair_made, 2 * g + i + 1)
                    if i:
                        pe.wait_ge(state_copied, g + 1)
                        pe.wait_ge(off_made, g + 1)
                    for e in range(8):
                        rows = slice(64 * (e % 2), 64 * (e % 2) + 64)
                        to = ps[rows, i, P * (e // 2):P * (e // 2) + P]
                        last = nc.tensor.matmul(to, xd(g)[:, i, HD * e:HD * e + HD], pair[:, i, e, :], start=True, stop=(i == 0))
                        if i:
                            last = nc.tensor.matmul(to, state[:, HD * e:HD * e + HD], off_side[:, e, :], start=False, stop=True)
                    last.then_inc(y_made, 1)

        @block.scalar
        def _(act):
            for g in range(GROUPS):
                act.wait_ge(b_turned, g + 1)
                if g:
                    act.wait_ge(state_made, g)
                nc.scalar.activation(b_tok[:, :], ps[:, 3, 0:P], ACT.Copy).then_inc(b_copied, 1)
                act.wait_ge(spread, 2 * g + 2)
                if g:
                    act.wait_ge(y_made, 2 * g)
                nc.scalar.activation(off_side[:, :, :], ps[:, 6:8, :].rearrange("p b (e q) -> p (b e) q", e=4), ACT.Exp).then_inc(grown, 1)
                for i in range(TT):
                    act.wait_ge(differed, 2 * g + i + 1)
                    nc.scalar.activation(pair[:, i, :, :], pair[:, i, :, :], ACT.Exp).then_inc(decayed, 1)
                act.wait_ge(state_made, g + 1)
                nc.scalar.activation(state[:, :], ps[:, 3, :], ACT.Copy).then_inc(state_copied, 1)

        @block.vector
        def _(dve):
            V = nc.vector
            dve.wait_ge(masked_ready, 1)
            by_q = [P, 8, P]
            for g in range(GROUPS):
                hs = slice(8 * g, 8 * g + 8)
                for i in range(TT):
                    dve.wait_ge(x_turned, 2 * g + i + 1)
                    V.tensor_tensor(xd(g)[:, i, :].rearrange("p (e v) -> p e v", e=8), ps[:, i, :].rearrange("p (e v) -> p e v", e=8),
                                    dt_tok[:, i, hs].unsqueeze(2).to_broadcast([P, 8, HD]), ALU.mult).then_inc(xdt_made, 1)
                dve.wait_ge(xdt_made, 2 * g + 1)
                if g:
                    dve.wait_ge(state_made, g)
                V.tensor_tensor(xst[:, :].rearrange("p (e v) -> p e v", e=8), xd(g)[:, 0, :].rearrange("p (e v) -> p e v", e=8),
                                last_tok[:, hs].unsqueeze(2).to_broadcast([P, 8, HD]), ALU.mult).then_inc(xst_made, 1)
                for i in range(TT):
                    dve.wait_ge(cb_made, 2 * g + 2)
                    V.tensor_tensor(cb[:, i, :], ps[:, 2, P * i:P * i + P], masks[:, :], ALU.mult).then_inc(cb_masked, 1)
                for i in range(TT):
                    dve.wait_ge(spread, 2 * g + i + 1)
                    if i:
                        dve.wait_ge(grown, g + 1)
                    if g:
                        dve.wait_ge(y_made, 2 * g - 1 + i)
                    order.after(dve, V.tensor_tensor(pair[:, i, :, :], ps[:, 4 + 2 * i:6 + 2 * i, :].rearrange("p b (e q) -> p (b e) q", e=4),
                                                     cum_tok[:, i, hs].unsqueeze(2).to_broadcast(by_q), ALU.subtract))
                    V.tensor_scalar(pair[:, i, :, :], pair[:, i, :, :], 0.0, None, ALU.min).then_inc(differed, 1)
                V.tensor_tensor(off_side[:, :, :], off_side[:, :, :], xbc[:, c_chunk + g, P:T].unsqueeze(1).to_broadcast(by_q), ALU.mult).then_inc(off_made, 1)
                for i in range(TT):
                    dve.wait_ge(decayed, 2 * g + i + 1)
                    dve.wait_ge(cb_masked, 2 * g + i + 1)
                    V.tensor_tensor(pair[:, i, :, :], pair[:, i, :, :], cb[:, i, :].unsqueeze(1).to_broadcast(by_q), ALU.mult).then_inc(pair_made, 1)
                for i in range(TT):
                    dve.wait_ge(y_made, 2 * g + i + 1)
                    for c in range(4):
                        to = xbc[:, 4 * g + c, P * i:P * i + P]
                        last = V.scalar_tensor_tensor(to, to, par("a_d", 4 * g + c), ps[:, i, P * c:P * c + P], ALU.mult, ALU.add)
                    last.then_inc(y_added, 1)


def gate_groups(scope, y, z, *, nc, sem, sbuf, par, cst, ps, prefetch):
    sq = sbuf(scope, "group_squared", [2, 4, T])
    rms = sbuf(scope, "group_rms", [4, T])
    gated, squared, summed, rooted, inverted = (sem("group_gated"), sem("group_sq_ready"), sem("group_summed"), sem("group_rooted"),
                                                sem("group_inverted"))
    with nc.Block() as block:
        @block.sync
        def _(sp):
            prefetch(sp)

        @block.vector
        def _(dve):
            V = nc.vector

            def scale(g):
                dve.wait_ge(rooted, g + 1)
                V.reciprocal(rms[:, g % 4, :], rms[:, g % 4, :]).then_inc(inverted, 1)
                dve.wait_ge(inverted, g + 1)
                for c in range(4 * g, 4 * g + 4):
                    V.scalar_tensor_tensor(y[:, c, :], y[:, c, :], par("a_norm", c), rms[:, g % 4, :], ALU.mult, ALU.mult)

            for g in range(GROUPS):
                to = y[:, 4 * g:4 * g + 4, :]
                V.tensor_tensor(to, to, z[:, 4 * g:4 * g + 4, :], ALU.mult).then_inc(gated, 1)
                if g >= 2:
                    scale(g - 2)
            scale(GROUPS - 2)
            scale(GROUPS - 1)

        @block.scalar
        def _(act):
            def root(g):
                act.wait_ge(summed, g + 1)
                if g >= 4:
                    act.wait_ge(inverted, g - 3)
                nc.scalar.activation(rms[:, g % 4, :], ps[:, g, 0:T], ACT.Sqrt, bias=cst("eps_2"), scale=1.0 / 512).then_inc(rooted, 1)

            for g in range(GROUPS):
                act.wait_ge(gated, g + 1)
                if g >= 2:
                    act.wait_ge(summed, g - 1)
                nc.scalar.activation(sq[:, g % 2, :, :], y[:, 4 * g:4 * g + 4, :], ACT.Square).then_inc(squared, 1)
                if g >= 1:
                    root(g - 1)
            root(GROUPS - 1)

        @block.tensor
        def _(pe):
            for g in range(GROUPS):
                pe.wait_ge(squared, g + 1)
                sum_over_channels(pe, nc, cst("ones"), sq[:, g % 2, :, :], ps[:, g, 0:T], 4).then_inc(summed, 1)


def attention(x2, x3, z, out, *, nc, d, sem, sbuf, par, par_at, cst, ps, ring, **_):
    with ExitStack() as scope:
        query, gate = z[:, 0:QH // 2, :], z[:, QH // 2:QH, :]
        key = sbuf(scope, "swa_k", [KVH, T])
        value = sbuf(scope, "swa_v", [TT, KVH * HD])
        cos = sbuf(scope, "rope_cos", [T])
        sin = sbuf(scope, "rope_sin", [T])
        mask = sbuf(scope, "window", [3 * P])
        sinks = sbuf(scope, "sinks_all", [QH])

        def take_keys(act, g, sums, half):
            for n in range(KVH):
                last = nc.scalar.activation(key[:, n, :], sums[:, n, :], ACT.Identity, bias=par("k_bias", n))
            last.then_inc(ring.evacuated, 1)

        def take_query(act, g, sums, half):
            for n in range(4):
                last = nc.scalar.activation(query[:, bass.ds(4 * g + n, 1), :], sums[:, n:n + 1, :], ACT.Identity, bias=par_at("q_bias", 4 * g + n))
            last.then_inc(ring.evacuated, 1)

        def take_gate(act, g, sums, half):
            nc.scalar.activation(gate[:, bass.ds(4 * g, 4), :], sums, ACT.Silu).then_inc(ring.evacuated, 1)

        linear(nc, ring, ps, d["w_k"], KVH, x2, dict(scalar=take_keys), d["b_w_in"][0:4])
        linear(nc, ring, ps, d["b_w_in"][0:4], QH // 2, x2, dict(scalar=take_query), d["b_w_in"][4:8])
        linear(nc, ring, ps, d["b_w_in"][4:8], QH // 2, x2, dict(scalar=take_gate))
        with ExitStack() as inner:
            make_tables(inner, x2, value, cos, sin, mask, sinks, nc=nc, d=d, sem=sem, sbuf=sbuf, cst=cst, ps=ps)
        rotate(query, key, cos, sin, nc=nc, sem=sem, sbuf=sbuf, cst=cst, ps=ps)
        with ExitStack() as inner:
            window_attention(inner, query, key, value, mask, sinks, gate, nc=nc, sem=sem, sbuf=sbuf, cst=cst, ps=ps)

        def add(dve, g, sums, half):
            nc.vector.scalar_tensor_tensor(x3[:, bass.ds(4 * g, 4), :], x2[:, bass.ds(4 * g, 4), :], ALPHA, sums,
                                           ALU.mult, ALU.add).then_inc(ring.evacuated, 1)

        linear(nc, ring, ps, d["b_w_out"], DC, gate, dict(vector=add))
    layernorm(x3, 1, nc=nc, sem=sem, sbuf=sbuf, par=par, cst=cst, ps=ps)
    stored = sem("stored")
    with nc.Block() as block:
        @block.sync
        def _(sp):
            sp.dma_start(out, x3[:, :, :]).then_inc(stored, 16)
            sp.wait_ge(stored, 16)


def make_tables(scope, x2, value, cos, sin, mask, sinks, *, nc, d, sem, sbuf, cst, ps):
    w_v = sbuf(scope, "w_v", [DC, KVH * HD])
    v_bias = scope.enter_context(nc.sbuf_tensor("v_bias", [1, KVH * HD], F32))
    pos = sbuf(scope, "pos", [T], I32)
    angle = sbuf(scope, "angle", [T])
    turns = sbuf(scope, "turns", [2, T])
    pos_in, w_in, sinks_in = sem("pos_in"), sem("w_v_in"), sem("sinks_in")
    reduced, valued, masked = sem("angles_reduced"), sem("swa_v_made"), sem("window_made")
    order, pool_order = Order(sem("table_order")), Order(sem("window_order"))
    with nc.Block() as block:
        @block.sync
        def _(sp):
            sp.dma_start(pos[:, :], d["positions"].to_broadcast([P, T])).then_inc(pos_in, 16)
            sp.dma_start(sinks[:, :], d["sinks"].to_broadcast([P, QH])).then_inc(sinks_in, 16)
            sp.dma_start(v_bias[:, :], d["v_bias"]).then_inc(w_in, 16)
            sp.dma_start(w_v[:, :, :], d["w_v"]).then_inc(w_in, 16)
            sp.wait_ge(sinks_in, 16)

        @block.gpsimd
        def _(pool):
            G = nc.gpsimd
            pool_order.after(pool, G.memset(mask[:, :], 0.0))
            pool_order.mark(G.affine_select(out=mask[:, 0:P], in_=mask[:, 0:P], compare_op=ALU.is_ge, fill=NEG, base=0,
                                            pattern=[[-1, P]], channel_multiplier=1))
            pool_order.mark(G.affine_select(out=mask[:, P:2 * P], in_=mask[:, P:2 * P], compare_op=ALU.is_gt, fill=NEG, base=0,
                                            pattern=[[1, P]], channel_multiplier=-1))
            pool_order.mark(G.affine_select(out=mask[:, 2 * P:3 * P], in_=mask[:, 2 * P:3 * P], compare_op=ALU.is_ge, fill=NEG, base=0,
                                            pattern=[[-1, P]], channel_multiplier=1))

        @block.vector
        def _(dve):
            V = nc.vector
            dve.wait_ge(pos_in, 16)
            order.after(dve, V.tensor_copy(angle[:, :], pos[:, :]))
            order.after(dve, V.tensor_scalar(angle[:, :], angle[:, :], cst("freq"), None, ALU.mult))
            for i, (to, quarter, ahead) in enumerate(((sin, 0.0, 0.0), (cos, 0.25, np.pi / 2))):
                n = turns[:, i, :]
                order.after(dve, V.tensor_scalar(n, angle[:, :], 1 / TWO_PI, quarter, ALU.mult, ALU.add))
                order.after(dve, V.tensor_scalar(n, n, ROUND, None, ALU.add))
                order.after(dve, V.tensor_scalar(n, n, -ROUND, None, ALU.add))
                order.after(dve, V.scalar_tensor_tensor(to[:, :], n, -PI_A, angle[:, :], ALU.mult, ALU.add))
                order.after(dve, V.scalar_tensor_tensor(to[:, :], n, -PI_B, to[:, :], ALU.mult, ALU.add))
                order.after(dve, V.scalar_tensor_tensor(to[:, :], n, -PI_C, to[:, :], ALU.mult, ALU.add))
                order.after(dve, V.tensor_scalar(to[:, :], to[:, :], float(ahead), PI_LOW, ALU.add, ALU.min))
                V.tensor_scalar(to[:, :], to[:, :], -PI_LOW, None, ALU.max).then_inc(reduced, 1)

        @block.scalar
        def _(act):
            for i, to in enumerate((sin, cos)):
                act.wait_ge(reduced, i + 1)
                nc.scalar.activation(to[:, :], to[:, :], ACT.Sin)
            for i in range(TT):
                act.wait_ge(valued, i + 1)
                nc.scalar.activation(value[:, i, :], ps[:, i, 0:T], ACT.Copy)

        @block.tensor
        def _(pe):
            pe.wait_ge(w_in, 32)
            for i in range(TT):
                for c in range(DC):
                    nc.tensor.matmul(ps[:, i, 0:T], x2[:, c, P * i:P * i + P], w_v[:, c, :], start=(c == 0), stop=False)
                nc.tensor.matmul(ps[:, i, 0:T], cst("ones")[0:1, :], v_bias[:, :], start=False, stop=True).then_inc(valued, 1)


def rotate(query, key, cos, sin, *, nc, sem, sbuf, cst, ps):
    jobs = [query[:, 4 * g:4 * g + 4, :] for g in range(4)] + [key[:, :, :]]
    by_t = [P, 4, T]
    turned, multiplied = sem("rope_turned"), sem("rope_multiplied")
    order = Order(sem("rope_order"))
    with ExitStack() as scope:
        part = sbuf(scope, "rope_part", [2, 4, T])
        with nc.Block() as block:
            @block.tensor
            def _(pe):
                for n, x in enumerate(jobs):
                    if n >= 4:
                        pe.wait_ge(multiplied, n - 3)
                    for c in range(4):
                        last = nc.tensor.matmul(ps[:, 2 * (n % 4) + c // 2, T * (c % 2):T * (c % 2) + T], cst("turn"), x[:, c, :],
                                                start=True, stop=True)
                    last.then_inc(turned, 1)

            @block.vector
            def _(dve):
                V = nc.vector
                for n, x in enumerate(jobs):
                    dve.wait_ge(turned, n + 1)
                    sums = ps[:, 2 * (n % 4):2 * (n % 4) + 2, :].rearrange("p b (c t) -> p (b c) t", c=2)
                    V.tensor_tensor(part[:, n % 2, :, :], sums, sin[:, :].unsqueeze(1).to_broadcast(by_t), ALU.mult).then_inc(multiplied, 1)
                    order.mark(V.tensor_tensor(x, x, cos[:, :].unsqueeze(1).to_broadcast(by_t), ALU.mult))
                    dve.wait_ge(multiplied, n + 1)
                    order.settle(dve)
                    order.after(dve, V.tensor_tensor(x, x, part[:, n % 2, :, :], ALU.add))


def window_attention(scope, query, key, value, mask, sinks, gate, *, nc, sem, sbuf, cst, ps):
    G, N = KVH, QH // KVH
    logits = sbuf(scope, "swa_logits", [2, N, 3 * P])
    p_t = sbuf(scope, "swa_p_t", [2, 3 * P])
    peak = sbuf(scope, "swa_peak", [2, 2, N])
    total = sbuf(scope, "swa_total", [2, 2, N])
    sunk = sbuf(scope, "swa_sunk", [2, 2, N])
    dotted, added, shifted, exped, scaled = sem("swa_dotted"), sem("swa_added"), sem("swa_shifted"), sem("swa_exped"), sem("swa_scaled")
    turned, copied, valued, gated = sem("swa_turned"), sem("swa_p_copied"), sem("swa_valued"), sem("swa_gated")
    order = Order(sem("swa_order"))
    with nc.Block() as block:
        @block.tensor
        def _(pe):
            def dots(g):
                for e in range(N):
                    h = N * g + e
                    rows = slice(64 * (h % 2), 64 * (h % 2) + 64)
                    if h >= 4:
                        pe.wait_ge(added, h - 3)
                    nc.tensor.matmul(ps[:, h % 4, 0:P], query[rows, h // 2, 0:P], key[rows, g, 0:P], start=True, stop=True)
                    nc.tensor.matmul(ps[:, h % 4, P:3 * P], query[rows, h // 2, P:T], key[rows, g, :], start=True, stop=True).then_inc(dotted, 1)

            def values(h):
                rows = slice(64 * (h % 2), 64 * (h % 2) + 64)
                pe.wait_ge(copied, h + 1)
                if h >= 2:
                    pe.wait_ge(gated, h - 1)
                v = [value[:, s, HD * (h // N):HD * (h // N) + HD] for s in range(TT)]
                p = [p_t[:, h % 2, P * s:P * s + P] for s in range(3)]
                bank = ps[rows, 6 + h % 2, :]
                nc.tensor.matmul(bank[:, 0:P], v[0], p[0], start=True, stop=True)
                nc.tensor.matmul(bank[:, P:T], v[0], p[1], start=True, stop=False)
                nc.tensor.matmul(bank[:, P:T], v[1], p[2], start=False, stop=True).then_inc(valued, 1)

            dots(0)
            for g in range(G):
                if g + 1 < G:
                    dots(g + 1)
                pe.wait_ge(scaled, g + 1)
                for h in range(N * g, N * g + N):
                    if h >= 2:
                        pe.wait_ge(copied, h - 1)
                    for s in range(3):
                        last = nc.tensor.transpose(ps[:, 4 + h % 2, P * s:P * s + P], logits[:, g % 2, h % N, P * s:P * s + P], cst("ident"))
                    last.then_inc(turned, 1)
                    if h > N * g:
                        values(h - 1)
                values(N * g + N - 1)

        @block.vector
        def _(dve):
            V = nc.vector

            def soften(g):
                b = g % 2
                for e in range(N):
                    h = N * g + e
                    dve.wait_ge(dotted, h + 1)
                    if g >= 2:
                        dve.wait_ge(turned, N * (g - 1))
                    V.scalar_tensor_tensor(logits[:, b, e, :], ps[:, h % 4, 0:3 * P], SA_SCALE, mask[:, :], ALU.mult, ALU.add).then_inc(added, 1)
                dve.wait_ge(added, N * (g + 1))
                order.mark(V.tensor_reduce(peak[:, b, 0, :], logits[:, b, :, 0:P], AX, ALU.max))
                order.mark(V.tensor_reduce(peak[:, b, 1, :], logits[:, b, :, P:3 * P], AX, ALU.max))
                order.settle(dve)
                sink = sinks[:, N * g:N * g + N].unsqueeze(1).to_broadcast([P, 2, N])
                order.after(dve, V.tensor_tensor(peak[:, b, :, :], peak[:, b, :, :], sink, ALU.max))
                order.after(dve, V.tensor_scalar(peak[:, b, :, :], peak[:, b, :, :], -1.0, None, ALU.mult))
                V.tensor_tensor(sunk[:, b, :, :], peak[:, b, :, :], sink, ALU.add).then_inc(shifted, 1)

            def gates(h):
                dve.wait_ge(valued, h + 1)
                rows = slice(64 * (h % 2), 64 * (h % 2) + 64)
                to = gate[rows, h // 2, :]
                V.tensor_tensor(to, to, ps[rows, 6 + h % 2, 0:T], ALU.mult).then_inc(gated, 1)

            soften(0)
            for g in range(G):
                b = g % 2
                if g + 1 < G:
                    soften(g + 1)
                dve.wait_ge(exped, g + 1)
                order.after(dve, V.tensor_tensor(total[:, b, :, :], total[:, b, :, :], sunk[:, b, :, :], ALU.add))
                order.after(dve, V.reciprocal(total[:, b, :, :], total[:, b, :, :]))
                for i, w in enumerate((slice(0, P), slice(P, 3 * P))):
                    order.mark(V.tensor_tensor(logits[:, b, :, w], logits[:, b, :, w],
                                               total[:, b, i, :].unsqueeze(2).to_broadcast([P, N, w.stop - w.start]), ALU.mult))
                order.settle(dve)
                dve.sem_inc(scaled, 1)
                for h in range(N * g, N * g + N):
                    gates(h)

        @block.scalar
        def _(act):
            def exps(g):
                b = g % 2
                act.wait_ge(shifted, g + 1)
                for i, w in enumerate((slice(0, P), slice(P, 3 * P))):
                    for e in range(N):
                        nc.scalar.activation(logits[:, b, e, w], logits[:, b, e, w], ACT.Exp, bias=peak[:, b, i, e:e + 1],
                                             accum_out=total[:, b, i, e:e + 1])
                nc.scalar.activation(sunk[:, b, :, :], sunk[:, b, :, :], ACT.Exp).then_inc(exped, 1)

            exps(0)
            for g in range(G):
                if g + 1 < G:
                    exps(g + 1)
                for h in range(N * g, N * g + N):
                    act.wait_ge(turned, h + 1)
                    if h >= 2:
                        act.wait_ge(valued, h - 1)
                    nc.scalar.activation(p_t[:, h % 2, :], ps[:, 4 + h % 2, 0:3 * P], ACT.Copy).then_inc(copied, 1)


def pack_params(np, v):
    def chunks(a, n):
        a = np.asarray(a).reshape(-1)
        full = np.zeros(n * P, np.float32)
        full[:a.size] = a
        return full.reshape(n, P).T

    mix = v["shift_mix"][0]
    conv = v["a_conv_w_2"][0].reshape(4 * CONVC, P).T
    kb = np.repeat(v["kv_b_2"][:256].reshape(4, 1, 64), 2, axis=1)
    ab = np.concatenate
    cols = dict(
        norm_mix=chunks(v["norm_mix_g"], 16), mix=chunks(mix, 27), w0=chunks(v["w0"], 8), a0=chunks(v["a0"], 8),
        k_k=chunks(v["k_k"], 8), k_a=chunks(v["k_a"], 8), r_k=chunks(v["r_k"], 8), ln_x_w=chunks(v["ln_x_w"], 8),
        ln_x_b=chunks(v["ln_x_b"], 8), kv_norm=chunks(v["kv_norm_g"], 2), norm_ffn=chunks(v["norm_ffn_g"], 16),
        norm_final=chunks(v["norm_final_g"], 16), ln_g=chunks(v["ln_g_2"], 32), ln_b=chunks(v["ln_b_2"], 32),
        conv_w=conv, conv_b=chunks(v["a_conv_b_2"], CONVC), dt_bias=chunks(v["a_dt_bias_2"], 1),
        a_log=chunks(v["a_log_2"], 1), a_d=chunks(np.repeat(v["a_d_2"][0], 64), 32), a_norm=chunks(v["a_norm_w_2"], 32),
        q_bias=chunks(v["b_q_bias_2"], 16), k_bias=chunks(kb, 4))
    return np.ascontiguousarray(ab([cols[n] for n in PARAM_COLS], axis=1))


def make_const(np):
    j, t = np.arange(2 * CH)[:, None], np.arange(2 * CH)[None, :]
    mask = np.zeros((P, 2 * CH), np.float32)
    mask[:2 * CH] = np.where(t < CH, j % CH < t % CH, j % CH <= t % CH)
    heads = np.kron(np.eye(2), np.ones((64, 64)))
    turn = np.zeros((P, P), np.float32)
    freq = np.zeros((P, 1), np.float32)
    f = (np.float32(500000.0) ** (-np.arange(0, 16, 2, dtype=np.float32) / np.float32(16))).astype(np.float32)
    for base in (0, 64):
        for i in range(8):
            turn[base + i + 8, base + i] = -1.0
            turn[base + i, base + i + 8] = 1.0
            freq[base + i] = freq[base + i + 8] = f[i]
    scan = np.tile((np.arange(T) % CH != 0).astype(np.float32), (P, 1))
    full = lambda x: np.full((P, 1), x, np.float32)
    cols = dict(ident=np.eye(P), ones=np.ones((P, P)), heads=heads, flip=np.eye(P)[::-1], decay_mask=mask, scan=scan, turn=turn, freq=freq,
                iota=np.tile(np.arange(16), (P, 1)), eps_rms=full(EPS_RMS), eps_gn=full(EPS_GN), eps_2=full(EPS_2))
    return np.ascontiguousarray(np.concatenate([cols[n] for n in CONST_COLS], axis=1).astype(np.float32))


def make_buckets(np):
    rel = np.arange(2 * T) - (T - 1)
    n = np.abs(rel)
    large = 8 + (np.log(np.maximum(n, 1).astype(np.float32) / np.float32(8)).astype(np.float32)
                 / np.float32(np.log(1024 / 8)) * np.float32(8)).astype(np.int32)
    bucket = (rel > 0) * 16 + np.where(n < 8, n, np.minimum(large, 15))
    return np.ascontiguousarray((np.arange(32)[:, None] == bucket[None, :]).astype(np.float32))


def kernel(**inputs):
    import concourse.bacc as bacc
    from concourse.bass_utils import run_bass_kernel_spmd

    v = {k: np.asarray(a) for k, a in inputs.items()}

    def rows(w):
        return np.ascontiguousarray(w.reshape(w.shape[0] // P, P, w.shape[1]).transpose(1, 0, 2))

    def pack(w):
        k, n = w.shape
        g = (n + 511) // 512
        full = np.zeros((k, g * 512), w.dtype)
        full[:, :n] = w
        return np.ascontiguousarray(full.reshape(k // P, P, g, 512).transpose(2, 1, 0, 3))

    w_in = v["w_in"][0]
    rw = w_in[:, :3360]
    q, ckv, iq, ik, iw, gates = np.split(w_in[:, 3360:], np.cumsum([1024, 256, 512, 64, 8]), axis=1)
    blank = np.zeros((D, P - IW_ROW - IDX_HEADS), np.float32)
    kv = v["kv_w_2"]
    k_twice = np.repeat(kv[:, :256].reshape(D, 4, 1, 64), 2, axis=2).reshape(D, 512)
    up = v["w_gate_up"][0]
    gate_up = np.zeros((2, P, H * HD), np.float32)
    gate_up[0] = up[:P]
    gate_up[1, :GATE_RANK - P] = up[P:]
    data = dict(
        x=rows(v["x"][0].T), params=pack_params(np, v), const=make_const(np), bucket_hot=make_buckets(np),
        w_in=pack(np.concatenate([rw, iw, blank, q, ckv, iq, ik, ik], axis=1)), w_gates=pack(gates),
        lora=np.ascontiguousarray(np.concatenate([v["w_decay_up"][0], v["w_icl_up"][0]], axis=0)),
        gate_up=np.ascontiguousarray(gate_up.transpose(1, 0, 2)), rel_bias=np.ascontiguousarray(v["rel_bias"]),
        w_uk=rows(v["w_uk"][0].transpose(1, 0, 2).reshape(256, 1024)),
        w_uv=rows(v["w_uv"][0].transpose(1, 0, 2).reshape(256, 1024)),
        w_branch_rwkv=pack(v["w_branch_rwkv"][0]), w_branch_dsa=pack(v["w_branch_dsa"][0]), w_out=pack(v["w_out"][0]),
        w_query=pack(v["w_peer_query"][0]),
        sub_keys=np.ascontiguousarray(v["peer_sub_keys"][0].transpose(3, 0, 1, 2).reshape(P, 16, P)),
        peer_u=np.ascontiguousarray(v["peer_u"][0]), peer_v=np.ascontiguousarray(v["peer_v"][0]),
        a_w_z=pack(v["a_w_in_2"][0][:, :4096]), a_w_conv=pack(v["a_w_in_2"][0][:, 4096:10240]),
        a_w_dt=pack(v["a_w_in_2"][0][:, 10240:]), a_w_out=pack(v["a_w_out_2"][0]),
        w_k=pack(k_twice), w_v=rows(np.ascontiguousarray(kv[:, 256:])),
        v_bias=np.ascontiguousarray(v["kv_b_2"][256:].reshape(1, 256)),
        sinks=np.ascontiguousarray(v["b_sinks_2"].reshape(1, QH)),
        positions=np.ascontiguousarray(v["positions_2"].reshape(1, T)),
        b_w_in=pack(v["b_w_in_2"][0]), b_w_out=pack(v["b_w_out_2"][0]),
    )
    nc = bacc.Bacc("TRN2", target_bir_lowering=False, num_devices=1)
    d = {n: nc.dram_tensor(f"in_{n}", a.shape, mybir.dt.from_np(a.dtype), kind="ExternalInput").ap()
         for n, a in data.items()}
    out = nc.dram_tensor("out_t", [P, DC, T], F32, kind="ExternalOutput").ap()
    build(nc, d, out)
    got = run_bass_kernel_spmd(nc, [{f"in_{n}": a for n, a in data.items()}], core_ids=[0]).results[0]["out_t"]
    return np.ascontiguousarray(got.transpose(2, 1, 0).reshape(1, T, D))
```

```python
from contextlib import ExitStack

import concourse.bass as bass
import numpy as np
from concourse import mybir

F32 = mybir.dt.float32
F32R = mybir.dt.float32r
U32 = mybir.dt.uint32
I32 = mybir.dt.int32
ACT = mybir.ActivationFunctionType
ALU = mybir.AluOpType
AX = mybir.AxisListType.X

P = 128
T = 256
TT = T // P
D = 2048
DC = D // P
H = 16
HD = 64
HC = H * HD // P
GATE_RANK = 160
IDX_HEADS = 8
IDX_SCALE = (IDX_HEADS * 64) ** -0.5
SA_SCALE = HD ** -0.5
KV_CHUNKS = 2
TOPK = 64
CH = 32
NCH = T // CH
EXP_HALF = float(np.float32(np.exp(-0.5)))
PK_HEADS, PK_KEYS, PK_TOP = 8, 128, 16
PK_SEL = PK_HEADS * PK_TOP
NEG = -1.0e30
DROPPED, TAKEN = -1.0e38, -3.0e38
SSM_H, GROUPS = 64, 8
ZC, CONVC = 32, 48
ALPHA = 4.0 ** 0.25
EPS_RMS, EPS_GN, EPS_2 = 1e-6, 64e-5, 1e-5
QH, KVH = 32, 4
TWO_PI = 2 * np.pi
PI_A = 6.28125
PI_B = 0.0019350051879882812
PI_C = float(TWO_PI - PI_A - PI_B)
PI_LOW = 3.1415925
ROUND = 12582912.0

C_R, C_K, C_V, C_WA, C_G, C_GI, C_Q, C_KV, C_IQ, C_IK = 0, 8, 16, 24, 25, 26, 27, 35, 37, 41
C_IN = 42
IW_ROW = 32

PARAM_COLS = dict(
    norm_mix=16, mix=27, w0=8, a0=8, k_k=8, k_a=8, r_k=8, ln_x_w=8, ln_x_b=8, kv_norm=2, norm_ffn=16,
    norm_final=16, ln_g=32, ln_b=32, conv_w=4 * CONVC, conv_b=CONVC, dt_bias=1, a_log=1, a_d=32, a_norm=32,
    q_bias=16, k_bias=4)
CONST_COLS = dict(ident=128, ones=128, heads=128, flip=128, decay_mask=64, turn=128, freq=1, iota=16, eps_rms=1,
                  eps_gn=1, eps_2=1)


def columns(sizes):
    at, out = 0, {}
    for name, n in sizes.items():
        out[name] = (at, n)
        at += n
    return out, at


PARAM_AT, N_PARAM = columns(PARAM_COLS)
CONST_AT, N_CONST = columns(CONST_COLS)


class Order:

    def __init__(self, sem):
        self.sem, self.n = sem, 0

    def mark(self, ins):
        self.n += 1
        ins.then_inc(self.sem, 1)
        return self.n

    def settle(self, eng):
        eng.wait_ge(self.sem, self.n)

    def after(self, eng, ins):
        self.mark(ins)
        self.settle(eng)


class Ring:

    SLOTS = 4

    def __init__(self, nc, ctx):
        self.buf = ctx.enter_context(nc.sbuf_tensor("weights", [P, self.SLOTS, 4, 512], F32))
        self.loaded = [ctx.enter_context(nc.semaphore(f"weights_loaded{q}")) for q in range(self.SLOTS)]
        self.high = ctx.enter_context(nc.semaphore("part_high"))
        self.split = ctx.enter_context(nc.semaphore("part_split"))
        self.used = ctx.enter_context(nc.semaphore("part_used"))
        self.evacuated = ctx.enter_context(nc.semaphore("evacuated"))
        self.parts = 0
        self.groups = 0
        self.ahead = False

    def load(self, sp, w, g, q, part, columns=512):
        slot = q % self.SLOTS if w.shape[2] >= 16 else q
        if not isinstance(part, int) or part >= self.SLOTS:
            sp.wait_ge(self.split, part - self.SLOTS + 1)
        rows = 4 * (q % (w.shape[2] // 4))
        src = w[bass.ds(g, 1), :, rows:rows + 4, 0:columns].rearrange("a p k n -> (a p) k n")
        sp.dma_start(self.buf[:, slot, :, 0:columns], src).then_inc(self.loaded[slot], 16)

    def prefetch(self, sp, w, part):
        parts = w.shape[2] // 4
        for s in range(self.SLOTS):
            self.load(sp, w, s // parts, s, part + s)
        self.ahead = True


class Product:

    def __init__(self, w, chunks, rhs, evac, ready=None, alongside=None):
        self.w, self.rhs, self.evac, self.ready, self.alongside = w, rhs, evac, ready, alongside
        self.parts = w.shape[2] // 4
        self.groups = (chunks + 3) // 4
        self.live = [min(4, chunks - 4 * g) for g in range(self.groups)]
        self.pairs = sum(n == 4 for n in self.live) // 2
        self.new_rhs = True

    def each_group(self, eng, group):
        def at(g, half, first):
            group(eng, g, (self.half0 + half) % 2, first, 4)

        if self.pairs:
            for half in range(2):
                at(half, half, self.p0 + half * self.parts)
        if self.pairs > 1:
            with eng.Fori(1, self.pairs) as j:
                for half in range(2):
                    at(2 * j + half, half, self.p0 + half * self.parts + 2 * self.parts * j)
        for g in range(2 * self.pairs, self.groups):
            group(eng, g, (self.half0 + g) % 2, self.p0 + g * self.parts, self.live[g])


def linear(nc, ring, ps, products, next_w=None):
    S = ring.SLOTS
    start, ahead, ring.ahead = ring.parts, ring.ahead, False
    part, group = ring.parts, ring.groups
    for i, m in enumerate(products):
        m.p0, m.g0, m.half0 = part, group, (group - ring.groups) % 2
        m.new_rhs = i == 0 or m.rhs is not products[i - 1].rhs
        part += m.groups * m.parts
        group += m.groups

    with ExitStack() as scope:
        kept = max(m.parts for m in products)
        w_half = scope.enter_context(nc.sbuf_tensor(f"w_half{start}", [P, 2, 2, 4, 512], F32R))
        x_half = scope.enter_context(nc.sbuf_tensor(f"x_half{start}", [P, kept, 2, 4, T], F32R))

        with nc.Block() as block:
            @block.sync
            def _(sp):
                if not ahead:
                    ring.prefetch(sp, products[0].w, start)
                    ring.ahead = False
                for m in products:
                    if m.alongside:
                        m.alongside(sp)

                    def load(sp, g, half, part, n_live, m=m):
                        for q in range(m.parts):
                            if isinstance(part, int) and part + q < start + S:
                                continue
                            ring.load(sp, m.w, g, ((half - m.half0) % 2 * m.parts + q) % max(S, m.parts), part + q, P * n_live)

                    m.each_group(sp, load)
                if next_w is not None:
                    ring.prefetch(sp, next_w, part)

            @block.tensor
            def _(pe):
                for m in products:
                    def multiply(pe, g, half, part, n_live, m=m):
                        if not isinstance(g, int) or m.g0 + g > ring.groups + 1:
                            pe.wait_ge(ring.evacuated, m.g0 + g - 1)
                        for q in range(m.parts):
                            pe.wait_ge(ring.split, part + q + 1)
                            for n in range(n_live):
                                for k in range(4):
                                    for i, (wh, xh) in enumerate(((0, 0), (0, 1), (1, 0))):
                                        last = nc.tensor.matmul(
                                            ps[:, 4 * half + n, 0:T], w_half[:, q % 2, wh, k, P * n:P * n + P], x_half[:, q, xh, k, :],
                                            start=(q == 0 and k == 0 and i == 0), stop=(q == m.parts - 1 and k == 3 and i == 2))
                            last.then_inc(ring.used, 1)

                    m.each_group(pe, multiply)

            def parts_and_sums(eng, one, name):
                def sums(m, g, half, part, n_live):
                    if m.evac.get(name):
                        eng.wait_ge(ring.used, part + m.parts)
                        m.evac[name](eng, g, ps[:, 4 * half:4 * half + n_live, 0:T], half, m.g0 + g)

                def last_group(m):
                    sums(m, m.groups - 1, (m.half0 + m.groups - 1) % 2, m.p0 + (m.groups - 1) * m.parts, m.live[-1])

                for before, m in zip([None] + products, products):
                    def halves(eng, g, half, part, n_live):
                        for q in range(m.parts):
                            one(eng, m, q, g, ((half - m.half0) % 2 * m.parts + q) % S, part + q, P * n_live)
                            if q == 1:
                                if not isinstance(g, int) or g > 0:
                                    sums(m, g - 1, 1 - half, part - m.parts, 4)
                                elif before:
                                    last_group(before)

                    m.each_group(eng, halves)
                last_group(products[-1])

            @block.scalar
            def _(act):
                def high(act, m, q, g, slot, part, columns):
                    act.wait_ge(ring.loaded[slot], 4 * (part - slot) + 16)
                    if not isinstance(part, int) or part >= start + 2:
                        act.wait_ge(ring.used, part - 1)
                    if isinstance(g, int) and g == 0 and m.new_rhs:
                        if m.ready:
                            act.wait_ge(m.ready, q + 1)
                        nc.scalar.activation(x_half[:, q, 0, :, :], m.rhs[:, 4 * q:4 * q + 4, :], ACT.Copy)
                    nc.scalar.activation(w_half[:, q % 2, 0, :, 0:columns], ring.buf[:, slot, :, 0:columns], ACT.Copy).then_inc(ring.high, 1)

                parts_and_sums(act, high, "scalar")

            @block.vector
            def _(dve):
                def low(dve, m, q, g, slot, part, columns):
                    dve.wait_ge(ring.high, part + 1)
                    if isinstance(g, int) and g == 0 and m.new_rhs:
                        nc.vector.tensor_tensor(x_half[:, q, 1, :, :], m.rhs[:, 4 * q:4 * q + 4, :], x_half[:, q, 0, :, :].bitcast(F32), ALU.subtract)
                    nc.vector.tensor_tensor(w_half[:, q % 2, 1, :, 0:columns], ring.buf[:, slot, :, 0:columns],
                                            w_half[:, q % 2, 0, :, 0:columns].bitcast(F32), ALU.subtract).then_inc(ring.split, 1)

                parts_and_sums(dve, low, "vector")
    ring.parts, ring.groups = part, group


def sum_over_channels(pe, nc, ones, sq, out, chunks):
    for c in range(chunks):
        last = nc.tensor.matmul(out, ones, sq[:, c, :], start=(c == 0), stop=(c == chunks - 1))
    return last


def rmsnorm(nc, sem, cst, ps, src, dst, gain, tmp, chunks, eps, prefetch=None):
    squared, summed, rooted = sem("squared"), sem("summed"), sem("rooted")
    order = Order(sem("norm_order"))
    with nc.Block() as block:
        if prefetch:
            @block.sync
            def _(sp):
                prefetch(sp)

        @block.scalar
        def _(act):
            nc.scalar.activation(dst, src, ACT.Square).then_inc(squared, 1)
            act.wait_ge(summed, 1)
            nc.scalar.activation(tmp, ps[:, 0, 0:T], ACT.Sqrt, bias=cst(eps), scale=1.0 / (P * chunks)).then_inc(rooted, 1)

        @block.tensor
        def _(pe):
            pe.wait_ge(squared, 1)
            sum_over_channels(pe, nc, cst("ones"), dst, ps[:, 0, 0:T], chunks).then_inc(summed, 1)

        @block.vector
        def _(dve):
            dve.wait_ge(rooted, 1)
            order.after(dve, nc.vector.reciprocal(tmp, tmp))
            for c in range(chunks):
                nc.vector.scalar_tensor_tensor(dst[:, c, :], src[:, c, :], gain[:, c:c + 1], tmp, ALU.mult, ALU.mult)


def build(nc, d, out):
    ctx = ExitStack()
    made = {}

    in_use = []

    def sem(name):
        made[name] = made.get(name, 0) + 1
        in_use.append(nc.alloc_semaphore(f"{name}_{made[name]}"))
        return in_use[-1]

    def recycle():
        nc.clear_and_free_semaphores(list(in_use))
        nc.all_engine_barrier()
        in_use.clear()

    def sbuf(scope, name, shape, dt=F32):
        return scope.enter_context(nc.sbuf_tensor(name, [P] + shape, dt))

    with ctx:
        params = sbuf(ctx, "params", [N_PARAM])
        const = sbuf(ctx, "const", [N_CONST])
        ps = ctx.enter_context(nc.psum_tensor("ps", [P, 8, 512], F32))
        ring = Ring(nc, ctx)

        def par(name, i=0, n=1):
            return params[:, PARAM_AT[name][0] + i:PARAM_AT[name][0] + i + n]

        def par_at(name, i):
            return params[:, bass.ds(PARAM_AT[name][0] + i, 1)]

        def cst(name):
            at, n = CONST_AT[name]
            return const[:, at:at + n]

        scratch = {n: nc.dram_tensor(n, s, F32, kind="Internal").ap() for n, s in dict(
            solve_in=[P, CH, CH], solve_out=[P, CH, CH], bias_rows=[H, 2 * T]).items()}
        env = dict(nc=nc, d=d, sem=sem, sbuf=sbuf, par=par, par_at=par_at, cst=cst, ps=ps, ring=ring, scratch=scratch)

        x1 = sbuf(ctx, "x1", [DC, T])
        y_rwkv, y_dsa = x1[:, 0:HC, :], x1[:, HC:2 * HC, :]
        with ExitStack() as scope:
            xn = sbuf(scope, "xn", [DC, T])
            with ExitStack() as mix:
                pin = sbuf(mix, "pin", [C_IN, T])
                load_and_norm(mix, xn, params, const, **env)
                linear(nc, ring, ps, [Product(d["w_in"], C_IN, xn, dict(scalar=copy_out(nc, ring, pin)))])
                shift_tokens(pin, **env)
                sparse_attention(pin, y_dsa, **env)
                recycle()
                rwkv(pin, y_rwkv, **env)
                recycle()
            with ExitStack() as mix:
                gates = sbuf(mix, "gates", [2 * DC, T])
                mixed = sbuf(mix, "mixed", [DC, T])
                mix_branches(gates, mixed, xn, y_rwkv, y_dsa, **env)
            recycle()
            peer(xn, x1, **env)
        recycle()
        with ExitStack() as scope:
            z = sbuf(scope, "z", [ZC, T])
            xbc = sbuf(scope, "xbc", [CONVC, T])
            x2 = xbc[:, ZC:CONVC, :]
            mamba(x1, x2, z, xbc, recycle, **env)
            recycle()
            attention(x2, x1, z, out, **env)


def copy_out(nc, ring, dst):
    def f(act, g, sums, half, before):
        nc.scalar.activation(dst[:, bass.ds(4 * g, sums.shape[1]), :], sums, ACT.Copy).then_inc(ring.evacuated, 1)
    return f


def load_and_norm(scope, xn, params, const, *, nc, d, sem, sbuf, par, cst, ps, ring, **_):
    with ExitStack() as inner:
        x = sbuf(inner, "x_in", [DC, T])
        tmp = sbuf(inner, "rms", [T])
        arrived = [sem("params_arrived"), sem("const_arrived"), sem("x_arrived")]
        with nc.Block() as block:
            @block.sync
            def _(sp):
                sp.dma_start(x[:, :, :], d["x"]).then_inc(arrived[2], 16)
                sp.dma_start(params[:, :], d["params"]).then_inc(arrived[0], 16)
                sp.dma_start(const[:, :], d["const"]).then_inc(arrived[1], 16)
                ring.prefetch(sp, d["w_in"], 0)
                for a in arrived:
                    sp.wait_ge(a, 16)
        rmsnorm(nc, sem, cst, ps, x[:, :, :], xn[:, :, :], par("norm_mix", 0, DC), tmp[:, :], DC, "eps_rms")


def shift_tokens(pin, *, nc, sem, sbuf, par, cst, **_):
    n = C_GI + 1
    order = Order(sem("shift_order"))
    with ExitStack() as inner:
        diff = sbuf(inner, "diff", [n, T])
        with nc.Block() as block:
            @block.vector
            def _(dve):
                order.mark(nc.vector.tensor_tensor(diff[:, :, 1:T], pin[:, 0:n, 0:T - 1], pin[:, 0:n, 1:T], ALU.subtract))
                order.mark(nc.vector.tensor_scalar(diff[:, :, 0], pin[:, 0:n, 0], -1.0, None, ALU.mult))
                order.settle(dve)
                for c in range(n):
                    nc.vector.scalar_tensor_tensor(pin[:, c, :], diff[:, c, :], par("mix", c), pin[:, c, :], ALU.mult, ALU.add)


def sparse_attention(pin, y, *, nc, d, sem, sbuf, par, cst, ps, ring, scratch, **_):
    with ExitStack() as scope:
        k_t = sbuf(scope, "k_t", [HC, T])
        v_tok = sbuf(scope, "v_tok", [TT, H * HD])
        logits = sbuf(scope, "logits", [TT, H, T])
        with ExitStack() as inner:
            latent = sbuf(inner, "latent", [KV_CHUNKS, T])
            tmp = sbuf(inner, "latent_rms", [T])
            w_uk = sbuf(inner, "w_uk", [KV_CHUNKS, H * HD])
            w_uv = sbuf(inner, "w_uv", [KV_CHUNKS, H * HD])
            rel = inner.enter_context(nc.sbuf_tensor("rel", [32, H], F32))
            hot = inner.enter_context(nc.sbuf_tensor("hot", [32, 2 * T], F32))
            rows = inner.enter_context(nc.sbuf_tensor("rows", [H, 2 * T], F32))
            up_in, rel_in, rows_out, bias_in = sem("up_in"), sem("rel_in"), sem("rows_out"), sem("bias_in")
            made, rows_ready, keys_made, values_made, copied, normed = (sem("rows_made"), sem("rows_ready"),
                sem("keys_made"), sem("values_made"), sem("kv_copied"), sem("latent_ready"))
            rmsnorm(nc, sem, cst, ps, pin[:, C_KV:C_KV + 2, :], latent[:, :, :], par("kv_norm", 0, 2), tmp[:, :],
                    KV_CHUNKS, "eps_rms")
            with nc.Block() as block:
                @block.sync
                def _(sp):
                    sp.dma_start(rel[:, :], d["rel_bias"]).then_inc(rel_in, 16)
                    sp.dma_start(hot[:, :], d["bucket_hot"]).then_inc(rel_in, 16)
                    sp.dma_start(w_uk[:, :, :], d["w_uk"]).then_inc(up_in, 16)
                    sp.dma_start(w_uv[:, :, :], d["w_uv"]).then_inc(up_in, 16)
                    sp.wait_ge(rows_ready, 1)
                    sp.dma_start(scratch["bias_rows"], rows[:, :]).then_inc(rows_out, 16)
                    sp.wait_ge(rows_out, 16)
                    for i in range(TT):
                        src = bass.AP(scratch["bias_rows"].tensor, P - P * i, [[1, P], [2 * T, H], [1, T]])
                        sp.dma_start(logits[:, i, :, :], src).then_inc(bias_in, 16)
                    sp.wait_ge(bias_in, 16 * TT)

                @block.tensor
                def _(pe):
                    pe.wait_ge(rel_in, 32)
                    nc.tensor.matmul(ps[0:H, 7, :], rel[:, :], hot[:, :], start=True, stop=True).then_inc(made, 1)
                    pe.wait_ge(up_in, 32)
                    for c in range(HC):
                        if c == 7:
                            pe.wait_ge(rows_ready, 1)
                        for k in range(KV_CHUNKS):
                            last = nc.tensor.matmul(ps[:, c, 0:T], w_uk[:, k, P * c:P * c + P], latent[:, k, :],
                                                    start=(k == 0), stop=(k == 1))
                        last.then_inc(keys_made, 1)
                    for i in range(TT):
                        for n in range(2):
                            b = 2 * i + n
                            pe.wait_ge(copied, b + 1)
                            for k in range(KV_CHUNKS):
                                last = nc.tensor.matmul(ps[:, b, :], latent[:, k, P * i:P * i + P],
                                                        w_uv[:, k, 512 * n:512 * n + 512], start=(k == 0), stop=(k == 1))
                            last.then_inc(values_made, 1)

                @block.vector
                def _(dve):
                    dve.wait_ge(made, 1)
                    nc.vector.tensor_copy(rows[:, :], ps[0:H, 7, :]).then_inc(rows_ready, 1)

                @block.scalar
                def _(act):
                    for c in range(HC):
                        act.wait_ge(keys_made, c + 1)
                        nc.scalar.activation(k_t[:, c, :], ps[:, c, 0:T], ACT.Copy, scale=SA_SCALE).then_inc(copied, 1)
                    for b in range(4):
                        act.wait_ge(values_made, b + 1)
                        nc.scalar.activation(v_tok[:, b // 2, 512 * (b % 2):512 * (b % 2) + 512], ps[:, b, :], ACT.Copy)
        score = sbuf(scope, "score", [TT, T])
        index_scores(pin, score, nc=nc, sem=sem, sbuf=sbuf, cst=cst, ps=ps)
        softmax_heads(pin, k_t, v_tok, logits, score, y, nc=nc, sem=sem, sbuf=sbuf, cst=cst, ps=ps)


def index_scores(pin, score, *, nc, sem, sbuf, cst, ps):
    with ExitStack() as inner:
        iw = sbuf(inner, "iw", [TT, IDX_HEADS])
        relu = sbuf(inner, "relu", [4, T])
        top = sbuf(inner, "top", [TT, 8])
        turned, scored, rectified, added = sem("iw_turned"), sem("scored"), sem("rectified"), sem("score_added")
        order = Order(sem("score_order"))
        with nc.Block() as block:
            @block.tensor
            def _(pe):
                for i in range(TT):
                    nc.tensor.transpose(ps[:, 7, P * i:P * i + P], pin[:, C_GI, P * i:P * i + P], cst("ident")).then_inc(turned, 1)
                for n in range(TT * IDX_HEADS):
                    i, h = n // IDX_HEADS, n % IDX_HEADS
                    rows = slice(64 * (h % 2), 64 * (h % 2) + 64)
                    if n >= 4:
                        pe.wait_ge(rectified, n - 3)
                    nc.tensor.matmul(ps[:, n % 4, 0:T], pin[rows, C_IQ + h // 2, P * i:P * i + P], pin[rows, C_IK, :],
                                     start=True, stop=True).then_inc(scored, 1)

            @block.scalar
            def _(act):
                for n in range(TT * IDX_HEADS):
                    act.wait_ge(scored, n + 1)
                    if n >= 4:
                        act.wait_ge(added, n - 3)
                    nc.scalar.activation(relu[:, n % 4, :], ps[:, n % 4, 0:T], ACT.Relu).then_inc(rectified, 1)

            @block.vector
            def _(dve):
                dve.wait_ge(turned, 2)
                for i in range(TT):
                    order.mark(nc.vector.tensor_scalar(iw[:, i, :], ps[:, 7, P * i + IW_ROW:P * i + IW_ROW + IDX_HEADS],
                                                       IDX_SCALE, None, ALU.mult))
                order.settle(dve)
                for n in range(TT * IDX_HEADS):
                    i, h = n // IDX_HEADS, n % IDX_HEADS
                    dve.wait_ge(rectified, n + 1)
                    if h == 0:
                        nc.vector.tensor_scalar(score[:, i, :], relu[:, n % 4, :], iw[:, i, h:h + 1], None, ALU.mult).then_inc(added, 1)
                    else:
                        dve.wait_ge(added, n)
                        nc.vector.scalar_tensor_tensor(score[:, i, :], relu[:, n % 4, :], iw[:, i, h:h + 1], score[:, i, :],
                                                       ALU.mult, ALU.add).then_inc(added, 1)
                dve.wait_ge(added, TT * IDX_HEADS)
                for q in range(T // 64 - 1):
                    order.mark(nc.vector.memset(score[64 * (q % 2):64 * (q % 2) + 64, q // 2, 64 * q + 64:T], DROPPED))
                order.settle(dve)
                for _ in range(TOPK // 8):
                    for i in range(TT):
                        order.mark(nc.vector.max(top[:, i, :], score[:, i, :]))
                    order.settle(dve)
                    for i in range(TT):
                        order.mark(nc.vector.match_replace(score[:, i, :], top[:, i, :], score[:, i, :], TAKEN))
                    order.settle(dve)
                nc.vector.tensor_scalar(score[:, :, :], score[:, :, :], (DROPPED + TAKEN) / 2, NEG, ALU.is_gt, ALU.mult)


def softmax_heads(pin, k_t, v_tok, logits, mask, y, *, nc, sem, sbuf, cst, ps):
    with ExitStack() as inner:
        p_t = sbuf(inner, "p_t", [2, TT, T])
        peak = sbuf(inner, "peak", [TT, H])
        total = sbuf(inner, "total", [TT, H])
        dotted, added, peaked, exped, scaled = sem("dotted"), sem("logit_added"), sem("peaked"), sem("exped"), sem("scaled")
        turned, p_copied, valued, y_copied = sem("p_turned"), sem("p_copied"), sem("valued"), sem("y_copied")
        order = Order(sem("softmax_order"))
        with nc.Block() as block:
            def values(pe, h):
                base = 64 * (h % 2)
                pe.wait_ge(p_copied, h + 1)
                if h >= 2:
                    pe.wait_ge(y_copied, h - 1)
                for s in range(TT):
                    last = nc.tensor.matmul(ps[base:base + 64, 6 + h % 2, 0:T], v_tok[:, s, HD * h:HD * h + HD],
                                            p_t[:, h % 2, s, :], start=(s == 0), stop=(s == 1))
                last.then_inc(valued, 1)

            @block.tensor
            def _(pe):
                for n in range(TT * H):
                    i, h = n // H, n % H
                    rows = slice(64 * (h % 2), 64 * (h % 2) + 64)
                    if n >= 4:
                        pe.wait_ge(added, n - 3)
                    nc.tensor.matmul(ps[:, n % 4, 0:T], cst("flip"), logits[:, i, h, :], start=True, stop=False)
                    nc.tensor.matmul(ps[:, n % 4, 0:T], pin[rows, C_Q + h // 2, P * i:P * i + P], k_t[rows, h // 2, :],
                                     start=False, stop=True).then_inc(dotted, 1)
                pe.wait_ge(scaled, TT)
                for h in range(H):
                    if h >= 2:
                        pe.wait_ge(p_copied, h - 1)
                    for i in range(TT):
                        for s in range(TT):
                            last = nc.tensor.transpose(ps[:, 4 + h % 2, T * s + P * i:T * s + P * i + P],
                                                       logits[:, i, h, P * s:P * s + P], cst("ident"))
                    last.then_inc(turned, 1)
                    if h >= 1:
                        values(pe, h - 1)
                values(pe, H - 1)

            @block.vector
            def _(dve):
                for n in range(TT * H):
                    i, h = n // H, n % H
                    dve.wait_ge(dotted, n + 1)
                    nc.vector.tensor_tensor(logits[:, i, h, :], ps[:, n % 4, 0:T], mask[:, i, :], ALU.add).then_inc(added, 1)
                    if h == H - 1:
                        dve.wait_ge(added, n + 1)
                        nc.vector.tensor_reduce(peak[:, i, :], logits[:, i, :, :], AX, ALU.max, negate=True).then_inc(peaked, 1)
                for i in range(TT):
                    dve.wait_ge(exped, H * (i + 1))
                    order.after(dve, nc.vector.reciprocal(total[:, i, :], total[:, i, :]))
                    nc.vector.tensor_tensor(logits[:, i, :, :], logits[:, i, :, :],
                                            total[:, i, :].unsqueeze(2).to_broadcast([P, H, T]), ALU.mult).then_inc(scaled, 1)
                for h in range(H):
                    base = 64 * (h % 2)
                    dve.wait_ge(valued, h + 1)
                    nc.vector.tensor_copy(y[base:base + 64, h // 2, :], ps[base:base + 64, 6 + h % 2, 0:T]).then_inc(y_copied, 1)

            @block.scalar
            def _(act):
                for n in range(TT * H):
                    i, h = n // H, n % H
                    if h == 0:
                        act.wait_ge(peaked, i + 1)
                    nc.scalar.activation(logits[:, i, h, :], logits[:, i, h, :], ACT.Exp, bias=peak[:, i, h:h + 1],
                                         accum_out=total[:, i, h:h + 1]).then_inc(exped, 1)
                for h in range(H):
                    act.wait_ge(turned, h + 1)
                    if h >= 2:
                        act.wait_ge(valued, h - 1)
                    nc.scalar.activation(p_t[:, h % 2, :, :].rearrange("p s q -> p (s q)"), ps[:, 4 + h % 2, :], ACT.Copy).then_inc(p_copied, 1)


def rwkv(pin, y, *, nc, d, sem, sbuf, par, cst, ps, ring, scratch, **_):
    with ExitStack() as scope:
        left = sbuf(scope, "left", [HC, NCH, 2 * CH])
        right = sbuf(scope, "right", [HC, NCH, 2 * CH])
        gate = sbuf(scope, "gate", [HC, T])
        bonus = sbuf(scope, "bonus", [HC, T])
        chunk_decay = sbuf(scope, "chunk_decay", [HC, NCH])
        with ExitStack() as inner:
            prepare_recurrence(inner, pin, left, right, gate, bonus, chunk_decay, nc=nc, d=d, sem=sem, sbuf=sbuf,
                               par=par, cst=cst, ps=ps)
        with ExitStack() as inner:
            pairs = inner.enter_context(nc.sbuf_tensor("pairs", [2 * CH, NCH, 2, HC, 2 * CH], F32))
            solve_corrections(pin, left, right, pairs, nc=nc, sem=sem, sbuf=sbuf, cst=cst, ps=ps, scratch=scratch)
            recur(pin, left, right, pairs, chunk_decay, y, nc=nc, sem=sem, sbuf=sbuf, cst=cst, ps=ps)
        with ExitStack() as inner:
            finish_rwkv(inner, y, gate, bonus, nc=nc, sem=sem, sbuf=sbuf, par=par, cst=cst, ps=ps)


def prepare_recurrence(scope, pin, left, right, gate, bonus, chunk_decay, *, nc, d, sem, sbuf, par, cst, ps):
    log_decay = sbuf(scope, "log_decay", [HC, T])
    icl = sbuf(scope, "icl", [HC, T])
    kk = sbuf(scope, "kk", [HC, T])
    t1 = sbuf(scope, "t1", [HC, T])
    t2 = sbuf(scope, "t2", [HC, T])
    kept = sbuf(scope, "scan_kept", [T])
    lora = t1[:, 0:4, :].rearrange("p a b -> p (a b)")
    gate_up = t2[:, :, :].rearrange("p (k a) b -> p k (a b)", k=2)
    lora_in, squashed, ranked, unranked = sem("lora_in"), sem("squashed"), sem("ranked"), sem("unranked")
    with nc.Block() as block:
        @block.sync
        def _(sp):
            sp.dma_start(lora, d["lora"]).then_inc(lora_in, 16)
            sp.dma_start(gate_up, d["gate_up"]).then_inc(lora_in, 16)

        @block.scalar
        def _(act):
            nc.scalar.activation(pin[0:64, C_WA, :], pin[0:64, C_WA, :], ACT.Tanh).then_inc(squashed, 1)
            nc.scalar.activation(pin[:, C_G, :], pin[:, C_G, :], ACT.Sigmoid).then_inc(squashed, 1)
            nc.scalar.activation(pin[0:GATE_RANK - P, C_GI, :], pin[0:GATE_RANK - P, C_GI, :], ACT.Sigmoid).then_inc(squashed, 1)
            for n in range(3 * HC):
                c, kind = n // 3, n % 3
                act.wait_ge(ranked, n + 1)
                if kind < 2:
                    to, bias = (log_decay, par("w0", c)) if kind == 0 else (icl, par("a0", c))
                    nc.scalar.activation(to[:, c, :], ps[:, n % 8, 0:T], ACT.Sigmoid, bias=bias).then_inc(unranked, 1)
                else:
                    nc.scalar.activation(gate[:, c, :], ps[:, n % 8, 0:T], ACT.Copy).then_inc(unranked, 1)

        @block.tensor
        def _(pe):
            pe.wait_ge(lora_in, 32)
            pe.wait_ge(squashed, 3)
            for n in range(3 * HC):
                c, kind = n // 3, n % 3
                if n >= 8:
                    pe.wait_ge(unranked, n - 7)
                sums = ps[:, n % 8, 0:T]
                if kind < 2:
                    rows = slice(64 * kind, 64 * kind + 64)
                    last = nc.tensor.matmul(sums, lora[rows, P * c:P * c + P], pin[rows, C_WA, :], start=True, stop=True)
                else:
                    rows = slice(0, GATE_RANK - P)
                    nc.tensor.matmul(sums, gate_up[:, 0, P * c:P * c + P], pin[:, C_G, :], start=True, stop=False)
                    last = nc.tensor.matmul(sums, gate_up[rows, 1, P * c:P * c + P], pin[rows, C_GI, :], start=False, stop=True)
                last.then_inc(ranked, 1)

    k_squared, k_summed, k_rooted = sem("kk_squared"), sem("kk_summed"), sem("kk_rooted")
    bonus_ready, bonus_summed = sem("bonus_ready"), sem("bonus_summed")
    cum_ready, before_ready, exp_ready, taken = sem("cum_ready"), sem("before_ready"), sem("exp_ready"), sem("exp_taken")
    order = Order(sem("prepare_order"))
    r, k, v = pin[:, C_R:C_R + HC, :], pin[:, C_K:C_K + HC, :], pin[:, C_V:C_V + HC, :]
    sums = ps[:, 0:4, :].rearrange("p b (c t) -> p (b c) t", c=2)
    sums_b = ps[:, 4:8, :].rearrange("p b (c t) -> p (b c) t", c=2)

    def by_chunk(x):
        return x.rearrange("p c (n t) -> p (c n) t", t=CH)

    left_a, left_r = (left[:, :, :, i * CH:i * CH + CH].rearrange("p c n t -> p (c n) t") for i in range(2))
    right_b, right_k = (right[:, :, :, i * CH:i * CH + CH].rearrange("p c n t -> p (c n) t") for i in range(2))

    with nc.Block() as block:
        @block.vector
        def _(dve):
            order.after(dve, nc.vector.memset(kept[:, :], 1.0))
            order.mark(nc.vector.memset(kept[:, ::CH], 0.0))
            for c in range(HC):
                order.mark(nc.vector.tensor_scalar(kk[:, c, :], pin[:, C_K + c, :], par("k_k", c), None, ALU.mult))
            order.settle(dve)
            order.after(dve, nc.vector.tensor_tensor(t1[:, :, :], kk[:, :, :], kk[:, :, :], ALU.mult))
            dve.sem_inc(k_squared, 1)
            for c in range(HC):
                order.mark(nc.vector.tensor_scalar(t2[:, c, :], icl[:, c, :], -1.0, par("k_a", c), ALU.add, ALU.mult))
            order.settle(dve)
            order.after(dve, nc.vector.scalar_tensor_tensor(k, t2[:, :, :], 1.0, k, ALU.add, ALU.mult))
            for c in range(HC):
                order.mark(nc.vector.scalar_tensor_tensor(t2[:, c, :], pin[:, C_R + c, :], par("r_k", c), pin[:, C_K + c, :], ALU.mult, ALU.mult))
            order.settle(dve)
            dve.sem_inc(bonus_ready, 1)
            dve.wait_ge(k_rooted, 1)
            order.after(dve, nc.vector.tensor_scalar(t1[:, :, :], t1[:, :, :], 1e-12, None, ALU.max))
            order.after(dve, nc.vector.reciprocal(t1[:, :, :], t1[:, :, :]))
            order.after(dve, nc.vector.tensor_tensor(kk[:, :, :], kk[:, :, :], t1[:, :, :], ALU.mult))
            dve.wait_ge(bonus_summed, 1)
            order.mark(nc.vector.tensor_tensor(bonus[:, :, :], sums_b, v, ALU.mult))
            order.after(dve, nc.vector.tensor_scalar(log_decay[:, :, :], log_decay[:, :, :], -EXP_HALF, None, ALU.mult))
            for c in range(HC):
                order.mark(nc.vector.tensor_tensor_scan(t1[:, c, :], kept[:, :], log_decay[:, c, :], 0.0, ALU.mult, ALU.add))
            order.settle(dve)
            order.after(dve, nc.vector.tensor_tensor(t2[:, :, :], t1[:, :, :], log_decay[:, :, :], ALU.subtract))
            dve.sem_inc(cum_ready, 1)
            dve.wait_ge(exp_ready, 1)
            order.after(dve, nc.vector.scalar_tensor_tensor(left_a, by_chunk(kk[:, :, :]), -1.0, by_chunk(t2[:, :, :]), ALU.mult, ALU.mult))
            order.after(dve, nc.vector.tensor_tensor(kk[:, :, :], kk[:, :, :], icl[:, :, :], ALU.mult))
            dve.wait_ge(exp_ready, 2)
            order.mark(nc.vector.tensor_tensor(right_b, by_chunk(kk[:, :, :]), by_chunk(log_decay[:, :, :]), ALU.mult))
            order.mark(nc.vector.tensor_tensor(right_k, by_chunk(k), by_chunk(log_decay[:, :, :]), ALU.mult))
            dve.wait_ge(exp_ready, 3)
            order.mark(nc.vector.tensor_tensor(left_r, by_chunk(r), by_chunk(t1[:, :, :]), ALU.mult))
            order.mark(nc.vector.tensor_copy(chunk_decay[:, :, :], t1[:, :, CH - 1::CH]))

        @block.tensor
        def _(pe):
            pe.wait_ge(k_squared, 1)
            for c in range(HC):
                last = nc.tensor.matmul(sums[:, c, :], cst("heads"), t1[:, c, :], start=True, stop=True)
            last.then_inc(k_summed, 1)
            pe.wait_ge(bonus_ready, 1)
            for c in range(HC):
                last = nc.tensor.matmul(sums_b[:, c, :], cst("heads"), t2[:, c, :], start=True, stop=True)
            last.then_inc(bonus_summed, 1)

        @block.scalar
        def _(act):
            act.wait_ge(k_summed, 1)
            nc.scalar.activation(t1[:, :, :], sums, ACT.Sqrt).then_inc(k_rooted, 1)
            act.wait_ge(cum_ready, 1)
            nc.scalar.activation(t2[:, :, :], t2[:, :, :], ACT.Exp).then_inc(exp_ready, 1)
            nc.scalar.activation(log_decay[:, :, :], t1[:, :, :], ACT.Exp, scale=-1.0).then_inc(exp_ready, 1)
            act.wait_ge(exp_ready, 2)
            nc.scalar.activation(t1[:, :, :], t1[:, :, :], ACT.Exp).then_inc(exp_ready, 1)


def solve_corrections(pin, left, right, pairs, *, nc, sem, sbuf, cst, ps, scratch):
    space = pin[:, C_Q:C_Q + 12, :].rearrange("p c t -> p (c t)")
    low, inverse, tmp = (space[:, CH * CH * i:CH * CH * (i + 1)].rearrange("p (j t) -> p j t", j=CH) for i in range(3))
    paired, masked = sem("paired"), sem("masked")
    out1, in1, out2, in2 = sem("low_out"), sem("low_in"), sem("inverse_out"), sem("inverse_in")
    solved = sem("solved")
    order = Order(sem("solve_order"))
    with nc.Block() as block:
        @block.tensor
        def _(pe):
            for n in range(NCH):
                for e in range(2):
                    rows = slice(64 * e, 64 * e + 64)
                    bank = (2 * n + e) % 8
                    if 2 * n + e >= 8:
                        pe.wait_ge(masked, 2 * n + e - 7)
                    for c in range(HC):
                        last = nc.tensor.matmul(ps[0:64, bank, 64 * c:64 * c + 64], right[rows, c, n, :], left[rows, c, n, :],
                                                start=True, stop=True)
                    last.then_inc(paired, 1)

        @block.vector
        def _(dve):
            mask = cst("decay_mask")[0:64, :].unsqueeze(1).to_broadcast([64, HC, 2 * CH])
            order.mark(nc.vector.memset(inverse, 0.0))
            for n in range(2 * NCH):
                dve.wait_ge(paired, n + 1)
                nc.vector.tensor_tensor(pairs[:, n // 2, n % 2, :, :], ps[0:64, n % 8, :].rearrange("p (c t) -> p c t", c=HC), mask,
                                        ALU.mult).then_inc(masked, 1)
            order.settle(dve)
            order.after(dve, nc.vector.memset(space[:, CH * CH:2 * CH * CH:CH + 1], 1.0))
            dve.wait_ge(in1, 16)
            for t in range(1, CH):
                by_s = low[:, 0:t, t].unsqueeze(1).to_broadcast([P, t, t])
                order.after(dve, nc.vector.tensor_tensor(tmp[:, 0:t, 0:t], inverse[:, 0:t, 0:t], by_s, ALU.mult))
                order.after(dve, nc.vector.tensor_reduce(inverse[:, 0:t, t], tmp[:, 0:t, 0:t], AX, ALU.add))
            dve.sem_inc(solved, 1)

        @block.sync
        def _(sp):
            sp.wait_ge(masked, 2 * NCH)
            block_ab = pairs[0:CH, :, :, :, 0:CH].rearrange("j n e c t -> j (n e c) t")
            sp.dma_start(scratch["solve_in"].rearrange("m j t -> j m t"), block_ab).then_inc(out1, 16)
            sp.wait_ge(out1, 16)
            sp.dma_start(low, scratch["solve_in"]).then_inc(in1, 16)
            sp.wait_ge(solved, 1)
            sp.dma_start(scratch["solve_out"], inverse).then_inc(out2, 16)
            sp.wait_ge(out2, 16)
            sp.dma_start(block_ab, scratch["solve_out"].rearrange("m j t -> j m t")).then_inc(in2, 16)
            sp.wait_ge(in2, 16)


def recur(pin, left, right, pairs, chunk_decay, y, *, nc, sem, sbuf, cst, ps):
    flat = pin[:, :, :].rearrange("p c t -> p (c t)")
    W = H * HD
    sv = pin[0:2 * CH, 0:8, :].rearrange("p (b c) t -> p b (c t)", b=2)
    wt = pin[0:2 * CH, 8:16, :].rearrange("p (b c) t -> p b (c t)", b=2)
    rhs = pin[0:CH, C_Q:C_Q + 4, :].rearrange("p c t -> p (c t)")
    states = [pin[:, at:at + 4, :].rearrange("p c t -> p (c t)").rearrange("p (c e v) -> p c e v", c=HC, e=2) for at in (C_Q + 4, C_Q + 8)]
    v_bank, w_bank = ps[0:64, 0:2, :].rearrange("p b t -> p (b t)"), ps[0:64, 2:4, :].rearrange("p b t -> p (b t)")
    x_bank = ps[:, 4:6, :].rearrange("p b t -> p (b t)")
    s_bank = ps[:, 6:8, :].rearrange("p b t -> p (b t)")
    v_turned, w_turned = sem("v_turned"), sem("w_turned")
    v_copied, w_copied, cleared = sem("v_copied"), sem("w_copied"), sem("corrections_cleared")
    x_made, x_copied, s_made, s_copied = sem("rhs_made"), sem("rhs_copied"), sem("corrections_made"), sem("corrections_copied")
    st_made, st_added, st_done, y_made, y_copied = sem("state_made"), sem("state_added"), sem("state_done"), sem("y_made"), sem("y_copied")
    with nc.Block() as block:
        @block.tensor
        def _(pe):
            def turn_v(n):
                if n >= 1:
                    pe.wait_ge(v_copied, n)
                for c in range(HC):
                    at = (C_V + c) * T + CH * (n - 1)
                    last = nc.tensor.transpose(v_bank[:, P * c:P * c + P], flat[:, at:at + 2 * CH], cst("ident"))
                last.then_inc(v_turned, 1)

            def turn_w(n):
                if n >= 1:
                    pe.wait_ge(w_copied, n)
                for c in range(HC):
                    last = nc.tensor.transpose(w_bank[:, P * c:P * c + P], right[:, c, n, :], cst("ident"))
                last.then_inc(w_turned, 1)

            turn_v(0)
            turn_w(0)
            for n in range(NCH):
                b = n % 2
                state = states[b]
                pe.wait_ge(v_copied, n + 1)
                pe.wait_ge(cleared, n + 1)
                pe.wait_ge(st_done, 2 * n + 1)
                for c in range(HC):
                    nc.tensor.matmul(x_bank[0:CH, P * c:P * c + P], left[:, c, n, 0:CH],
                                     state[:, c, :, :].rearrange("p e v -> p (e v)"), start=(c % 4 == 0), stop=True, skip_group_check=(c % 4 > 0))
                for c in range(HC):
                    for e in range(2):
                        at = P * c + HD * e
                        last = nc.tensor.matmul(x_bank[0:CH, at:at + HD], pairs[:, n, e, c, 0:CH], sv[:, b, at:at + HD],
                                                start=False, stop=True, skip_group_check=True)
                last.then_inc(x_made, 1)
                if n + 1 < NCH:
                    turn_v(n + 1)
                pe.wait_ge(x_copied, n + 1)
                if n >= 1:
                    pe.wait_ge(y_copied, n)
                for c in range(HC):
                    for e in range(2):
                        at = P * c + HD * e
                        last = nc.tensor.matmul(s_bank[0:CH, at:at + HD], pairs[0:CH, n, e, c, 0:CH], rhs[:, at:at + HD],
                                                start=True, stop=True)
                last.then_inc(s_made, 1)
                if n + 1 < NCH:
                    turn_w(n + 1)
                pe.wait_ge(s_copied, n + 1)
                if n + 1 < NCH:
                    for c in range(HC):
                        last = nc.tensor.matmul(x_bank[:, P * c:P * c + P], wt[:, b, P * c:P * c + P], sv[:, b, P * c:P * c + P],
                                                start=True, stop=True)
                    last.then_inc(st_made, 1)
                for c in range(HC):
                    nc.tensor.matmul(s_bank[:, CH * c:CH * c + CH], state[:, c, :, :].rearrange("p e v -> p (e v)"), left[:, c, n, CH:2 * CH],
                                     start=(c == 0), stop=True, skip_group_check=(c > 0))
                for c in range(HC):
                    for e in range(2):
                        at = P * c + HD * e
                        last = nc.tensor.matmul(s_bank[64 * e:64 * e + 64, CH * c:CH * c + CH], sv[:, b, at:at + HD],
                                                pairs[:, n, e, c, CH:2 * CH], start=False, stop=True, skip_group_check=True)
                last.then_inc(y_made, 1)

        @block.scalar
        def _(act):
            def take_v(n):
                act.wait_ge(v_turned, n + 1)
                if n >= 2:
                    act.wait_ge(y_made, n - 1)
                nc.scalar.activation(sv[CH:2 * CH, n % 2, :], v_bank[CH:2 * CH, :], ACT.Copy).then_inc(v_copied, 1)

            take_v(0)
            for n in range(NCH):
                act.wait_ge(x_made, n + 1)
                if n >= 1:
                    act.wait_ge(s_made, n)
                nc.scalar.activation(rhs, x_bank[0:CH, :], ACT.Copy).then_inc(x_copied, 1)
                if n + 1 < NCH:
                    take_v(n + 1)
                act.wait_ge(y_made, n + 1)
                nc.scalar.activation(y[:, :, CH * n:CH * n + CH], s_bank[:, 0:HC * CH].rearrange("p (c t) -> p c t", c=HC),
                                     ACT.Copy).then_inc(y_copied, 1)

        @block.vector
        def _(dve):
            def clear(n):
                if n >= 2:
                    dve.wait_ge(y_made, n - 1)
                nc.vector.memset(sv[0:CH, n % 2, :], 0.0).then_inc(cleared, 1)

            def take_w(n):
                dve.wait_ge(w_turned, n + 1)
                nc.vector.tensor_copy(wt[:, n % 2, :], w_bank).then_inc(w_copied, 1)

            nc.vector.memset(pin[:, C_Q + 4:C_Q + 12, :], 0.0).then_inc(st_done, 1)
            clear(0)
            take_w(0)
            for n in range(NCH):
                if n + 1 < NCH:
                    clear(n + 1)
                dve.wait_ge(s_made, n + 1)
                dve.wait_ge(cleared, n + 1)
                nc.vector.tensor_copy(sv[0:CH, n % 2, :], s_bank[0:CH, :]).then_inc(s_copied, 1)
                if n + 1 < NCH:
                    take_w(n + 1)
                    dve.wait_ge(st_made, n + 1)
                    if n >= 1:
                        dve.wait_ge(st_done, 2 * n + 1)
                        dve.wait_ge(y_made, n)
                    for e in range(2):
                        rows = slice(64 * e, 64 * e + 64)
                        add = x_bank[rows, :].rearrange("p (c e v) -> p c e v", c=HC, e=2)[:, :, e, :]
                        nc.vector.tensor_tensor(states[(n + 1) % 2][rows, :, e, :], states[n % 2][rows, :, e, :], add, ALU.add).then_inc(st_added, 1)
                    dve.wait_ge(st_added, 2 * n + 2)
                    for e in range(2):
                        rows = slice(64 * e, 64 * e + 64)
                        to = states[(n + 1) % 2][rows, :, e, :]
                        nc.vector.tensor_tensor(to, to, chunk_decay[rows, :, n].unsqueeze(2).to_broadcast([64, HC, HD]),
                                                ALU.mult).then_inc(st_done, 1)


def finish_rwkv(scope, y, gate, bonus, *, nc, sem, sbuf, par, cst, ps):
    sq = sbuf(scope, "y_squared", [HC, T])
    meaned, centered, summed, rooted = sem("y_meaned"), sem("y_centered"), sem("y_summed"), sem("y_rooted")
    order = Order(sem("finish_order"))
    means = ps[:, 0:4, :].rearrange("p b (c t) -> p (b c) t", c=2)
    sums = ps[:, 4:8, :].rearrange("p b (c t) -> p (b c) t", c=2)
    with nc.Block() as block:
        @block.tensor
        def _(pe):
            for c in range(HC):
                last = nc.tensor.matmul(means[:, c, :], cst("heads"), y[:, c, :], start=True, stop=True)
            last.then_inc(meaned, 1)
            pe.wait_ge(centered, 1)
            for c in range(HC):
                last = nc.tensor.matmul(sums[:, c, :], cst("heads"), sq[:, c, :], start=True, stop=True)
            last.then_inc(summed, 1)

        @block.scalar
        def _(act):
            act.wait_ge(summed, 1)
            nc.scalar.activation(sq[:, :, :], sums, ACT.Sqrt, bias=cst("eps_gn"), scale=1.0 / HD).then_inc(rooted, 1)

        @block.vector
        def _(dve):
            dve.wait_ge(meaned, 1)
            order.after(dve, nc.vector.scalar_tensor_tensor(y[:, :, :], means, -1.0 / HD, y[:, :, :], ALU.mult, ALU.add))
            nc.vector.tensor_tensor(sq[:, :, :], y[:, :, :], y[:, :, :], ALU.mult).then_inc(centered, 1)
            dve.wait_ge(rooted, 1)
            order.after(dve, nc.vector.reciprocal(sq[:, :, :], sq[:, :, :]))
            order.after(dve, nc.vector.tensor_tensor(y[:, :, :], y[:, :, :], sq[:, :, :], ALU.mult))
            for c in range(HC):
                order.mark(nc.vector.tensor_scalar(y[:, c, :], y[:, c, :], par("ln_x_w", c), par("ln_x_b", c), ALU.mult, ALU.add))
            order.settle(dve)
            order.after(dve, nc.vector.tensor_tensor(y[:, :, :], y[:, :, :], bonus[:, :, :], ALU.add))
            nc.vector.tensor_tensor(y[:, :, :], y[:, :, :], gate[:, :, :], ALU.mult)


def mix_branches(gates, mixed, xn, y_rwkv, y_dsa, *, nc, d, sem, ring, ps, **_):
    gated, x_in = sem("branch_gated"), sem("x_again")
    first_part = ring.parts

    def to_gates(act, g, sums, half, before):
        nc.scalar.activation(gates[:, bass.ds(4 * g, 4), :], sums, ACT.Sigmoid).then_inc(ring.evacuated, 1)

    def first(dve, g, sums, half, before):
        dve.wait_ge(ring.evacuated, before)
        nc.vector.tensor_tensor(mixed[:, bass.ds(4 * g, 4), :], sums, gates[:, bass.ds(4 * g, 4), :], ALU.mult).then_inc(ring.evacuated, 1)

    def second(dve, g, sums, half, before):
        b = gates[:, bass.ds(DC + 4 * g, 4), :]
        nc.vector.tensor_tensor(b, sums, b, ALU.mult).then_inc(ring.evacuated, 1)
        dve.wait_ge(ring.evacuated, before + 1)
        m = mixed[:, bass.ds(4 * g, 4), :]
        nc.vector.tensor_tensor(m, m, b, ALU.add).then_inc(gated, 1)

    def x_again(sp):
        sp.wait_ge(ring.split, first_part + DC // 4)
        sp.dma_start(xn[:, :, :], d["x"]).then_inc(x_in, 16)

    def add(dve, g, sums, half, before):
        dve.wait_ge(x_in, 16)
        to = xn[:, bass.ds(4 * g, 4), :]
        nc.vector.tensor_tensor(to, sums, to, ALU.add).then_inc(ring.evacuated, 1)

    linear(nc, ring, ps, [
        Product(d["w_gates"], 2 * DC, xn, dict(scalar=to_gates)),
        Product(d["w_branch_rwkv"], DC, y_rwkv, dict(vector=first), alongside=x_again),
        Product(d["w_branch_dsa"], DC, y_dsa, dict(vector=second)),
        Product(d["w_out"], DC, mixed, dict(vector=add), ready=gated)])


def peer(h, x1, *, nc, d, sem, sbuf, par, par_at, cst, ps, ring, **_):
    with ExitStack() as scope:
        h_tok = sbuf(scope, "h_tok", [TT, D])
        tmp = sbuf(scope, "ffn_rms", [T])
        partial = sbuf(scope, "partial", [TT, D])
        hn = partial[:, :, :].rearrange("p i (c t) -> p (i c) t", t=T)
        rmsnorm(nc, sem, cst, ps, h[:, :, :], hn, par("norm_ffn", 0, DC), tmp[:, :], DC, "eps_rms",
                lambda sp: ring.prefetch(sp, d["w_query"], ring.parts))
        product = sbuf(scope, "product", [D])
        keys = product[:, :].rearrange("p (s n) -> p s n", n=PK_KEYS)
        keys_in = sem("keys_in")
        linear(nc, ring, ps, [Product(d["w_query"], DC, hn, dict(scalar=copy_out(nc, ring, x1)),
                                      alongside=lambda sp: sp.dma_start(keys, d["sub_keys"]).then_inc(keys_in, 16))])
        experts(h, x1, hn, h_tok, partial, product, keys, keys_in, nc=nc, d=d, sem=sem, sbuf=sbuf, cst=cst, ps=ps)
        rmsnorm(nc, sem, cst, ps, h[:, :, :], x1[:, :, :], par("norm_final", 0, DC), tmp[:, :], DC, "eps_rms",
                lambda sp: ring.prefetch(sp, d["a_w_z"], ring.parts))


def experts(h, query, hn, h_tok, partial, product, keys, keys_in, *, nc, d, sem, sbuf, cst, ps):
    S = 2 * PK_HEADS
    K = PK_TOP
    SLOTS = 8
    BY_VECTOR = (3, 7)
    BY_TENSOR = [s for s in range(SLOTS) if s not in BY_VECTOR]
    TURNS = PK_SEL // SLOTS
    with ExitStack() as scope:
        expert = sbuf(scope, "expert", [TT, PK_SEL], U32)
        weight = sbuf(scope, "weight", [TT, PK_SEL])
        score = sbuf(scope, "key_score", [S, PK_KEYS])
        rest = sbuf(scope, "key_rest", [S, PK_KEYS])
        best = sbuf(scope, "best", [S, K])
        best_at = sbuf(scope, "best_at", [S, K], U32)
        best_f = sbuf(scope, "best_f", [S, K])
        cand = score[:, :, :].rearrange("p (h s) n -> p h (s n)", h=PK_HEADS)
        cand_rest = rest[:, :, :].rearrange("p (h s) n -> p h (s n)", h=PK_HEADS)
        top = sbuf(scope, "top_sum", [PK_HEADS, K])
        top_at = sbuf(scope, "top_sum_at", [PK_HEADS, K], U32)
        place = sbuf(scope, "place", [2, PK_HEADS, K], U32)
        place_f = sbuf(scope, "place_f", [2, PK_HEADS, K])
        half_id = sbuf(scope, "half_id", [2, PK_HEADS, K])
        total = sbuf(scope, "gate_total", [PK_HEADS])
        row = sbuf(scope, "row", [SLOTS, D])
        index = sbuf(scope, "index", [SLOTS], U32)
        dot = sbuf(scope, "dot", [2, SLOTS])
        act_in = sbuf(scope, "act_in", [TT, PK_SEL])
        diag = sbuf(scope, "diag", [SLOTS, P])
        zero = sbuf(scope, "zero", [P])
        turned, h_copied = sem("h_turned"), sem("h_copied")
        scored, s_copied, searched = sem("keys_scored"), sem("keys_copied"), sem("tile_searched")
        shifted, exped, chosen = sem("gate_shifted"), sem("gate_exped"), sem("tile_chosen")
        order = Order(sem("choose_order"))
        index_set = sem("index_set")
        index_seen = sem("index_seen")
        arrived = [sem(f"row_arrived{s}") for s in range(SLOTS)]
        row_free = [sem(f"row_free{s}") for s in range(SLOTS)]
        diag_ready = [sem(f"diag_ready{s}") for s in range(SLOTS)]
        collected, gelued, weighted, zeroed = sem("collected"), sem("gelued"), sem("weighted"), sem("zeroed")
        summed, sum_copied, turned_back = sem("experts_summed"), sem("sum_copied"), sem("turned_back")
        partial_added, sum_whole = sem("partial_added"), sem("sum_whole")

        def top16(dve, jobs):
            V = nc.vector
            for x, _, v, _ in jobs:
                order.mark(V.max(v[:, 0:8], x))
            order.settle(dve)
            for x, r, v, at in jobs:
                order.mark(V.max_index(at[:, 0:8], v[:, 0:8], x))
                order.mark(V.match_replace(r, v[:, 0:8], x, TAKEN))
            order.settle(dve)
            for _, r, v, _ in jobs:
                order.mark(V.max(v[:, 8:16], r))
            order.settle(dve)
            for _, r, v, at in jobs:
                order.mark(V.max_index(at[:, 8:16], v[:, 8:16], r))
            order.settle(dve)

        def search_keys(dve, i, half):
            dve.wait_ge(s_copied, i + 1)
            top16(dve, [(score[:, s, :], rest[:, s, :], best[:, s, :], best_at[:, s, :]) for s in range(S // 2 * half, S // 2 * half + S // 2)])

        def search_sums(dve, i):
            V = nc.vector
            order.mark(V.tensor_copy(best_f[:, :, :], best_at[:, :, :]))
            order.after(dve, V.tensor_tensor(cand.rearrange("p h (a b) -> p h a b", a=K),
                                             best[:, 0::2, :].unsqueeze(3).to_broadcast([P, PK_HEADS, K, K]),
                                             best[:, 1::2, :].unsqueeze(2).to_broadcast([P, PK_HEADS, K, K]), ALU.add))
            top16(dve, [(cand[:, h, :], cand_rest[:, h, :], top[:, h, :], top_at[:, h, :]) for h in range(PK_HEADS)])
            dve.sem_inc(searched, 1)

        def take_experts(dve, i):
            V = nc.vector
            wide = [P, PK_HEADS, K, K]
            hot = rest[:, :, :].rearrange("p (h s) (a b) -> p h (s a) b", h=PK_HEADS, b=K)
            w = weight[:, i, :].rearrange("p (h k) -> p h k", h=PK_HEADS)
            V.tensor_tensor(w, top[:, :, :], top[:, :, 0:1].to_broadcast([P, PK_HEADS, K]), ALU.subtract).then_inc(shifted, 1)
            order.mark(V.tensor_scalar(place[:, 0, :, :], top_at[:, :, :], 4, None, ALU.logical_shift_right))
            order.mark(V.tensor_scalar(place[:, 1, :, :], top_at[:, :, :], 15, None, ALU.bitwise_and))
            order.settle(dve)
            order.after(dve, V.tensor_copy(place_f[:, :, :, :], place[:, :, :, :]))
            for half in range(2):
                order.after(dve, V.tensor_tensor(hot, place_f[:, half, :, :].unsqueeze(3).to_broadcast(wide),
                                                 cst("iota").unsqueeze(1).unsqueeze(1).to_broadcast(wide), ALU.is_equal))
                order.after(dve, V.tensor_tensor(hot, hot, best_f[:, half::2, :].unsqueeze(2).to_broadcast(wide), ALU.mult))
                order.after(dve, V.tensor_reduce(half_id[:, half, :, :], hot, AX, ALU.add))
            e = half_id[:, 0, :, :]
            order.after(dve, V.scalar_tensor_tensor(e, e, float(PK_KEYS), half_id[:, 1, :, :], ALU.mult, ALU.add))
            V.tensor_copy(expert[:, i, :].rearrange("p (h k) -> p h k", h=PK_HEADS), e).then_inc(chosen, 1)
            dve.wait_ge(exped, i + 1)
            order.after(dve, V.tensor_reduce(total[:, :], w, AX, ALU.add))
            order.after(dve, V.reciprocal(total[:, :], total[:, :]))
            order.after(dve, V.tensor_tensor(w, w, total[:, :].unsqueeze(2).to_broadcast([P, PK_HEADS, K]), ALU.mult))

        def dot_rows(dve, i, t):
            V = nc.vector
            at = TURNS * i + t
            for s in range(SLOTS):
                dve.wait_ge(arrived[s], 16 * at + 16)
                V.tensor_tensor_reduce(product[:, :], row[:, s, :], h_tok[:, i, :], 1.0, 0.0, ALU.mult, ALU.add,
                                       dot[:, 0, s:s + 1]).then_inc(row_free[s], 1)
                dve.wait_ge(row_free[s], at + 2)
            V.tensor_copy(act_in[:, i, bass.ds(SLOTS * t, SLOTS)], dot[:, 0, :]).then_inc(collected, 1)
            dve.wait_ge(collected, at + 1)

        with nc.Block() as block:
            @block.gpsimd
            def _(pool):
                for i in range(2 * TT):
                    table = d["peer_u"] if i < TT else d["peer_v"]
                    if i < TT:
                        pool.wait_ge(chosen, i + 1)
                    with pool.Fori(0, TURNS) as t:
                        for s in range(SLOTS):
                            at = TURNS * i + t
                            pool.wait_ge(row_free[s], at + 1)
                            nc.gpsimd.tensor_copy(index[:, s:s + 1], expert[:, i % TT, bass.ds(SLOTS * t + s, 1)]).then_inc(index_set, 1)
                            pool.wait_ge(index_set, SLOTS * at + s + 1)
                            pool.sem_inc(index_seen, 1)
                            nc.gpsimd.indirect_dma_start(row[:, s, :], None, table, bass.IndirectOffsetOnAxis(ap=index[:, s:s + 1], axis=0)).then_inc(arrived[s], 16)

            @block.vector
            def _(dve):
                V = nc.vector
                V.memset(zero[:, :], 0.0).then_inc(zeroed, 1)
                for s in range(SLOTS):
                    dve.sem_inc(row_free[s], 1)
                for half in range(2):
                    search_keys(dve, 0, half)
                search_sums(dve, 0)
                take_experts(dve, 0)
                search_keys(dve, 1, 0)
                dve.wait_ge(h_copied, TT)
                dve.wait_ge(scored, TT)
                with dve.Fori(0, 2) as t:
                    dot_rows(dve, 0, t)
                search_keys(dve, 1, 1)
                with dve.Fori(2, 4) as t:
                    dot_rows(dve, 0, t)
                search_sums(dve, 1)
                with dve.Fori(4, 6) as t:
                    dot_rows(dve, 0, t)
                take_experts(dve, 1)
                V.memset(partial[:, :, :], 0.0).then_inc(partial_added, 1)
                with dve.Fori(6, TURNS) as t:
                    dot_rows(dve, 0, t)
                with dve.Fori(0, TURNS) as t:
                    dot_rows(dve, 1, t)
                for i in range(TT):
                    dve.wait_ge(gelued, i + 1)
                    V.tensor_tensor(weight[:, i, :], weight[:, i, :], act_in[:, i, :], ALU.mult).then_inc(weighted, 1)
                dve.wait_ge(weighted, TT)
                for i in range(TT):
                    with dve.Fori(0, TURNS) as t:
                        at = TURNS * i + t
                        for s in BY_TENSOR:
                            dve.wait_ge(row_free[s], TT * TURNS + at + 1)
                            V.tensor_scalar(diag[:, s, :], cst("ident"), weight[:, i, bass.ds(SLOTS * t + s, 1)], None, ALU.mult).then_inc(diag_ready[s], 1)
                        for n, s in enumerate(BY_VECTOR):
                            dve.wait_ge(arrived[s], 16 * (TT * TURNS + at) + 16)
                            dve.wait_ge(partial_added, len(BY_VECTOR) * at + n + 1)
                            V.scalar_tensor_tensor(partial[:, i, :], row[:, s, :], weight[:, i, bass.ds(SLOTS * t + s, 1)], partial[:, i, :],
                                                   ALU.mult, ALU.add).then_inc(partial_added, 1)
                            dve.wait_ge(partial_added, len(BY_VECTOR) * at + n + 2)
                            dve.sem_inc(row_free[s], 1)
                for i in range(TT):
                    dve.wait_ge(sum_copied, i + 1)
                    V.tensor_tensor(h_tok[:, i, :], h_tok[:, i, :], partial[:, i, :], ALU.add).then_inc(sum_whole, 1)
                for i in range(TT):
                    for q in range(4):
                        dve.wait_ge(turned_back, 4 * i + q + 1)
                        to = h[:, 4 * q:4 * q + 4, P * i:P * i + P]
                        V.tensor_tensor(to, to, ps[:, 4 * i + q, :].rearrange("p (c t) -> p c t", c=4), ALU.add)

            @block.scalar
            def _(act):
                for i in range(TT):
                    act.wait_ge(scored, i + 1)
                    if i:
                        act.wait_ge(searched, i)
                    nc.scalar.activation(score[:, :, :], ps[:, 0:4, :].rearrange("p b (s n) -> p (b s) n", s=4), ACT.Copy).then_inc(s_copied, 1)
                    act.wait_ge(turned, i + 1)
                    nc.scalar.activation(h_tok[:, i, :], ps[:, 4:8, :].rearrange("p b n -> p (b n)"), ACT.Copy).then_inc(h_copied, 1)
                    act.wait_ge(shifted, i + 1)
                    w = weight[:, i, :]
                    nc.scalar.activation(w, w, ACT.Exp).then_inc(exped, 1)
                for i in range(TT):
                    act.wait_ge(collected, TURNS * (i + 1))
                    nc.scalar.activation(act_in[:, i, :], act_in[:, i, :], ACT.Gelu).then_inc(gelued, 1)
                for i in range(TT):
                    act.wait_ge(summed, i + 1)
                    nc.scalar.activation(h_tok[:, i, :], ps[:, 4 * i:4 * i + 4, :].rearrange("p b n -> p (b n)"), ACT.Copy).then_inc(sum_copied, 1)

            @block.tensor
            def _(pe):
                pe.wait_ge(keys_in, 16)
                for i in range(TT):
                    if i:
                        pe.wait_ge(s_copied, i)
                    for s in range(S):
                        last = nc.tensor.matmul(ps[:, s // 4, PK_KEYS * (s % 4):PK_KEYS * (s % 4) + PK_KEYS],
                                                query[:, s, P * i:P * i + P], keys[:, s, :], start=True, stop=True)
                    last.then_inc(scored, 1)
                    if i:
                        pe.wait_ge(h_copied, i)
                    for c in range(DC):
                        last = nc.tensor.transpose(ps[:, 4 + c // 4, P * (c % 4):P * (c % 4) + P], hn[:, c, P * i:P * i + P], cst("ident"))
                    last.then_inc(turned, 1)
                pe.wait_ge(zeroed, 1)
                pe.wait_ge(s_copied, TT)
                pe.wait_ge(h_copied, TT)
                for i in range(TT):
                    for q in range(4):
                        nc.tensor.matmul(ps[:, 4 * i + q, :], zero[:, :], h_tok[:, i, 512 * q:512 * q + 512],
                                         start=True, stop=False)
                    with pe.Fori(0, TURNS) as t:
                        at = TURNS * i + t
                        for s in BY_TENSOR:
                            pe.wait_ge(arrived[s], 16 * (TT * TURNS + at) + 16)
                            pe.wait_ge(diag_ready[s], at + 1)
                            for q in range(4):
                                last = nc.tensor.matmul(ps[:, 4 * i + q, :], diag[:, s, :], row[:, s, 512 * q:512 * q + 512],
                                                        start=False, stop=False)
                            last.then_inc(row_free[s], 1)
                    for q in range(4):
                        last = nc.tensor.matmul(ps[:, 4 * i + q, :], zero[:, :], h_tok[:, i, 512 * q:512 * q + 512], start=False, stop=True)
                    last.then_inc(summed, 1)
                for i in range(TT):
                    pe.wait_ge(sum_whole, i + 1)
                    for q in range(4):
                        for c in range(4):
                            at = P * (4 * q + c)
                            last = nc.tensor.transpose(ps[:, 4 * i + q, P * c:P * c + P], h_tok[:, i, at:at + P], cst("ident"))
                        last.then_inc(turned_back, 1)


def mamba(x1, x2, z, xbc, recycle, *, nc, d, sem, sbuf, par, par_at, cst, ps, ring, **_):
    with ExitStack() as scope:
        w = d["a_w_out"]
        dt = sbuf(scope, "dt", [2, T])
        with ExitStack() as inner:
            project_mamba(inner, x1, z, xbc, dt, nc=nc, d=d, sem=sem, sbuf=sbuf, par=par, par_at=par_at, cst=cst, ps=ps, ring=ring)
        with ExitStack() as inner:
            ssd(inner, xbc, dt, nc=nc, sem=sem, sbuf=sbuf, par=par, cst=cst, ps=ps)
        with ExitStack() as inner:
            gate_groups(inner, xbc, z, nc=nc, sem=sem, sbuf=sbuf, par=par, cst=cst, ps=ps,
                        prefetch=lambda sp: ring.prefetch(sp, w[:, :, 0:ZC // 2, :], ring.parts))

        def add(dve, g, sums, half, before):
            nc.vector.scalar_tensor_tensor(x2[:, bass.ds(4 * g, 4), :], x1[:, bass.ds(4 * g, 4), :], ALPHA, sums,
                                           ALU.mult, ALU.add).then_inc(ring.evacuated, 1)

        def add_more(dve, g, sums, half, before):
            dve.wait_ge(ring.evacuated, before)
            to = x2[:, bass.ds(4 * g, 4), :]
            nc.vector.tensor_tensor(to, sums, to, ALU.add).then_inc(ring.evacuated, 1)

        linear(nc, ring, ps, [
            Product(w[:, :, 0:ZC // 2, :], DC, xbc[:, 0:ZC // 2, :], dict(vector=add)),
            Product(w[:, :, ZC // 2:ZC, :], DC, xbc[:, ZC // 2:ZC, :], dict(vector=add_more))], d["w_k"])
    layernorm(x2, 0, nc=nc, sem=sem, sbuf=sbuf, par=par, cst=cst, ps=ps)


def layernorm(x, layer, *, nc, sem, sbuf, par, cst, ps):
    with ExitStack() as scope:
        sq = sbuf(scope, f"ln_squared{layer}", [DC, T])
        rstd = sbuf(scope, f"ln_rstd{layer}", [T])
        mean = sbuf(scope, f"ln_mean{layer}", [T])
        meaned, centered, squared, summed, rooted = (sem("ln_meaned"), sem("ln_centered"), sem("ln_squared"),
                                                     sem("ln_summed"), sem("ln_rooted"))
        order = Order(sem("ln_order"))
        with nc.Block() as block:
            @block.tensor
            def _(pe):
                sum_over_channels(pe, nc, cst("ones"), x, ps[:, 0, 0:T], DC).then_inc(meaned, 1)
                pe.wait_ge(squared, 1)
                sum_over_channels(pe, nc, cst("ones"), sq, ps[:, 1, 0:T], DC).then_inc(summed, 1)

            @block.scalar
            def _(act):
                act.wait_ge(centered, 1)
                nc.scalar.activation(sq[:, :, :], x[:, :, :], ACT.Square).then_inc(squared, 1)
                act.wait_ge(summed, 1)
                nc.scalar.activation(rstd[:, :], ps[:, 1, 0:T], ACT.Sqrt, bias=cst("eps_2"), scale=1.0 / D).then_inc(rooted, 1)

            @block.vector
            def _(dve):
                dve.wait_ge(meaned, 1)
                order.after(dve, nc.vector.tensor_scalar(mean[:, :], ps[:, 0, 0:T], 1.0 / D, None, ALU.mult))
                nc.vector.tensor_tensor(x[:, :, :], x[:, :, :], mean[:, :].unsqueeze(1).to_broadcast([P, DC, T]), ALU.subtract).then_inc(centered, 1)
                dve.wait_ge(centered, 1)
                dve.wait_ge(rooted, 1)
                order.after(dve, nc.vector.reciprocal(rstd[:, :], rstd[:, :]))
                for c in range(DC):
                    order.mark(nc.vector.scalar_tensor_tensor(x[:, c, :], x[:, c, :], par("ln_g", DC * layer + c), rstd[:, :],
                                                              ALU.mult, ALU.mult))
                order.settle(dve)
                for c in range(DC):
                    nc.vector.tensor_scalar(x[:, c, :], x[:, c, :], par("ln_b", DC * layer + c), None, ALU.add)


def project_mamba(scope, x1, z, xbc, dt, *, nc, d, sem, sbuf, par, par_at, cst, ps, ring):
    TAPS = 4
    raw = sbuf(scope, "conv_raw", [2, 4, TAPS - 1 + T])
    cleared = sem("conv_cleared")
    with nc.Block() as block:
        @block.vector
        def _(dve):
            nc.vector.memset(raw[:, :, :, 0:TAPS - 1], 0.0).then_inc(cleared, 1)

    def silu_z(act, g, sums, half, before):
        nc.scalar.activation(z[:, bass.ds(4 * g, 4), :], sums, ACT.Silu).then_inc(ring.evacuated, 1)

    raw_ready, tapped, activated = sem("conv_raw_ready"), sem("conv_tapped"), sem("conv_activated")

    def activate(act, g):
        act.wait_ge(tapped, TAPS * g + TAPS)
        to = xbc[:, bass.ds(4 * g, 4), :]
        nc.scalar.activation(to, to, ACT.Silu).then_inc(activated, 1)

    def evac(act, g, sums, half, before):
        if not isinstance(g, int) or g > 0:
            activate(act, g - 1)
        nc.scalar.activation(raw[:, half, :, TAPS - 1:TAPS - 1 + T], sums, ACT.Copy).then_inc(ring.evacuated, 1)

    def conv(dve, g, sums, half, before):
        dve.wait_ge(ring.evacuated, before + 1)
        for n in range(4):
            last = nc.vector.tensor_scalar(xbc[:, bass.ds(4 * g + n, 1), :], raw[:, half, n:n + 1, TAPS - 1:TAPS - 1 + T],
                                           par_at("conv_w", 3 * CONVC + 4 * g + n), par_at("conv_b", 4 * g + n), ALU.mult, ALU.add)
        last.then_inc(tapped, 1)
        for tap in range(TAPS - 1):
            dve.wait_ge(tapped, TAPS * g + tap + 1)
            for n in range(4):
                to = xbc[:, bass.ds(4 * g + n, 1), :]
                last = nc.vector.scalar_tensor_tensor(to, raw[:, half, n:n + 1, tap:tap + T], par_at("conv_w", tap * CONVC + 4 * g + n), to,
                                                      ALU.mult, ALU.add)
            last.then_inc(tapped, 1)

    def take_dt(act, g, sums, half, before):
        activate(act, CONVC // 4 - 1)
        nc.scalar.activation(dt[0:SSM_H, 0, :], sums[0:SSM_H, 0, :], ACT.Copy).then_inc(ring.evacuated, 1)

    linear(nc, ring, ps, [
        Product(d["a_w_z"], ZC, x1, dict(scalar=silu_z)),
        Product(d["a_w_conv"], CONVC, x1, dict(scalar=evac, vector=conv)),
        Product(d["a_w_dt"], 1, x1, dict(scalar=take_dt))])


def ssd(scope, xbc, dt, *, nc, sem, sbuf, par, cst, ps):
    heads_a = GROUPS
    cum = sbuf(scope, "cum", [T])
    a = sbuf(scope, "a", [1])
    dt_tok = sbuf(scope, "dt_tok", [TT, SSM_H])
    cum_tok = sbuf(scope, "cum_tok", [TT, SSM_H])
    last_tok = sbuf(scope, "last_tok", [SSM_H])
    xdt = sbuf(scope, "xdt", [2, TT, 512])
    xst = sbuf(scope, "xst", [512])
    b_tok = sbuf(scope, "b_tok", [P])
    cb = sbuf(scope, "cb", [2, P])
    pair = sbuf(scope, "pair", [2, 8, P])
    off_side = sbuf(scope, "off_side", [8, P])
    state = sbuf(scope, "state", [512])
    tmp = sbuf(scope, "ssd_tmp", [T])
    order = Order(sem("ssd_order"))
    act_order = Order(sem("ssd_act_order"))
    dt_done, cum_done, dt_turned, tok_copied, last_made = (sem("dt_done"), sem("cum_done"), sem("dt_turned"), sem("tok_copied"),
                                                           sem("last_made"))
    with nc.Block() as block:
        @block.scalar
        def _(act):
            raw, d1, t = dt[0:SSM_H, 0, :], dt[0:SSM_H, 1, :], tmp[0:SSM_H, :]
            act_order.after(act, nc.scalar.activation(raw, raw, ACT.Identity, bias=par("dt_bias")[0:SSM_H]))
            act_order.after(act, nc.scalar.activation(t, raw, ACT.Abs))
            act_order.after(act, nc.scalar.activation(t, t, ACT.Exp, scale=-1.0))
            act_order.after(act, nc.scalar.activation(t, t, ACT.Ln, bias=1.0))
            act_order.after(act, nc.scalar.activation(d1, raw, ACT.Relu))
            nc.scalar.activation(a[0:SSM_H, :], par("a_log")[0:SSM_H], ACT.Exp).then_inc(dt_done, 1)

        @block.vector
        def _(dve):
            V = nc.vector
            d1, t = dt[0:SSM_H, 1, :], tmp[0:SSM_H, :]
            dve.wait_ge(dt_done, 1)
            order.after(dve, V.tensor_tensor(d1, d1, t, ALU.add))
            order.after(dve, V.tensor_scalar(t, d1, a[0:SSM_H, :], -1.0, ALU.mult, ALU.mult))
            ones = cst("ones")[0:SSM_H, :]
            for i in range(TT):
                w = slice(P * i, P * i + P)
                order.mark(V.tensor_tensor_scan(cum[0:SSM_H, w], ones, t[:, w], 0.0, ALU.mult, ALU.add))
            order.settle(dve)
            dve.sem_inc(cum_done, 1)
            dve.wait_ge(dt_turned, 1)
            order.mark(V.tensor_copy(dt_tok[:, :, :], ps[:, 0, 0:P].rearrange("p (i h) -> p i h", i=TT)))
            order.mark(V.tensor_copy(cum_tok[:, :, :], ps[:, 1, 0:P].rearrange("p (i h) -> p i h", i=TT)))
            order.settle(dve)
            dve.wait_ge(last_made, 1)
            order.mark(V.tensor_tensor(last_tok[:, :], ps[:, 2, 0:SSM_H], cum_tok[:, 0, :], ALU.subtract))
            order.settle(dve)
            dve.sem_inc(tok_copied, 1)

        @block.tensor
        def _(pe):
            pe.wait_ge(cum_done, 1)
            ident = cst("ident")[0:SSM_H, 0:SSM_H]
            for i in range(TT):
                w = slice(P * i, P * i + P)
                nc.tensor.transpose(ps[:, 0, SSM_H * i:SSM_H * i + SSM_H], dt[0:SSM_H, 1, w], ident)
                last = nc.tensor.transpose(ps[:, 1, SSM_H * i:SSM_H * i + SSM_H], cum[0:SSM_H, w], ident)
            last.then_inc(dt_turned, 1)
            nc.tensor.matmul(ps[:, 2, 0:SSM_H], cum[0:SSM_H, P - 1:P].to_broadcast([SSM_H, P]), ident, start=True, stop=True).then_inc(last_made, 1)

    with nc.Block() as block:
        @block.scalar
        def _(act):
            nc.scalar.activation(last_tok[:, :], last_tok[:, :], ACT.Exp)

    x_turned, xdt_made, xst_made, b_turned, b_copied = sem("x_turned"), sem("xdt_made"), sem("xst_made"), sem("b_turned"), sem("b_copied")
    cb_made, cb_masked, spread, differed, decayed, pair_made = (sem("cb_made"), sem("cb_masked"), sem("cum_spread"), sem("differed"),
                                                              sem("decayed"), sem("pair_made"))
    grown, off_made, state_made, state_copied = sem("grown"), sem("off_made"), sem("state_copied_p"), sem("ssm_state_copied")
    y_made, y_added = sem("ssm_y_made"), sem("ssm_y_added")
    UNITS = GROUPS * TT
    b_chunk, c_chunk = ZC, ZC + GROUPS
    masks = sbuf(scope, "causal", [P])
    masked_ready = sem("causal_ready")

    def xd(g):
        return xdt[:, g % 2, :, :]

    with nc.Block() as block:
        @block.gpsimd
        def _(pool):
            nc.gpsimd.affine_select(out=masks[:, :], in_=cst("ones"), compare_op=ALU.is_ge, fill=0.0, base=0, pattern=[[1, P]],
                                    channel_multiplier=-1).then_inc(masked_ready, 1)

        @block.tensor
        def _(pe):
            for g in range(GROUPS):
                if g:
                    pe.wait_ge(y_added, 2 * g)
                for i in range(TT):
                    for c in range(4):
                        last = nc.tensor.transpose(ps[:, i, P * c:P * c + P], xbc[:, 4 * g + c, P * i:P * i + P], cst("ident"))
                    last.then_inc(x_turned, 1)
                if g:
                    pe.wait_ge(state_copied, g)
                    pe.wait_ge(cb_masked, 2 * g)
                nc.tensor.transpose(ps[:, 3, 0:P], xbc[:, b_chunk + g, 0:P], cst("ident")).then_inc(b_turned, 1)
                for i in range(TT):
                    w = slice(P * i, P * i + P)
                    nc.tensor.matmul(ps[:, 2, P * i:P * i + P], xbc[:, b_chunk + g, w], xbc[:, c_chunk + g, w],
                                     start=True, stop=True).then_inc(cb_made, 1)
                if g:
                    pe.wait_ge(differed, 2 * g)
                    pe.wait_ge(grown, g)
                for i in range(TT):
                    for e in range(8):
                        h = 8 * g + e
                        last = nc.tensor.matmul(ps[:, 4 + 2 * i + e // 4, P * (e % 4):P * (e % 4) + P],
                                                cst("ident")[0:SSM_H, h:h + 1].to_broadcast([SSM_H, P]), cum[0:SSM_H, P * i:P * i + P],
                                                start=True, stop=True)
                    last.then_inc(spread, 1)
                pe.wait_ge(b_copied, g + 1)
                pe.wait_ge(xst_made, g + 1)
                nc.tensor.matmul(ps[:, 3, :], b_tok[:, :], xst[:, :], start=True, stop=True).then_inc(state_made, 1)
                pe.wait_ge(xdt_made, 2 * g + 2)
                for i in range(TT):
                    pe.wait_ge(pair_made, 2 * g + i + 1)
                    if i:
                        pe.wait_ge(state_copied, g + 1)
                        pe.wait_ge(off_made, g + 1)
                    for e in range(8):
                        rows = slice(64 * (e % 2), 64 * (e % 2) + 64)
                        to = ps[rows, i, P * (e // 2):P * (e // 2) + P]
                        last = nc.tensor.matmul(to, xd(g)[:, i, HD * e:HD * e + HD], pair[:, i, e, :], start=True, stop=(i == 0))
                        if i:
                            last = nc.tensor.matmul(to, state[:, HD * e:HD * e + HD], off_side[:, e, :], start=False, stop=True)
                    last.then_inc(y_made, 1)

        @block.scalar
        def _(act):
            for g in range(GROUPS):
                act.wait_ge(b_turned, g + 1)
                if g:
                    act.wait_ge(state_made, g)
                nc.scalar.activation(b_tok[:, :], ps[:, 3, 0:P], ACT.Copy).then_inc(b_copied, 1)
                act.wait_ge(spread, 2 * g + 2)
                if g:
                    act.wait_ge(y_made, 2 * g)
                nc.scalar.activation(off_side[:, :, :], ps[:, 6:8, :].rearrange("p b (e q) -> p (b e) q", e=4), ACT.Exp).then_inc(grown, 1)
                for i in range(TT):
                    act.wait_ge(differed, 2 * g + i + 1)
                    nc.scalar.activation(pair[:, i, :, :], pair[:, i, :, :], ACT.Exp).then_inc(decayed, 1)
                act.wait_ge(state_made, g + 1)
                nc.scalar.activation(state[:, :], ps[:, 3, :], ACT.Copy).then_inc(state_copied, 1)

        @block.vector
        def _(dve):
            V = nc.vector
            dve.wait_ge(masked_ready, 1)
            by_q = [P, 8, P]
            for g in range(GROUPS):
                hs = slice(8 * g, 8 * g + 8)
                for i in range(TT):
                    dve.wait_ge(x_turned, 2 * g + i + 1)
                    V.tensor_tensor(xd(g)[:, i, :].rearrange("p (e v) -> p e v", e=8), ps[:, i, :].rearrange("p (e v) -> p e v", e=8),
                                    dt_tok[:, i, hs].unsqueeze(2).to_broadcast([P, 8, HD]), ALU.mult).then_inc(xdt_made, 1)
                dve.wait_ge(xdt_made, 2 * g + 1)
                if g:
                    dve.wait_ge(state_made, g)
                V.tensor_tensor(xst[:, :].rearrange("p (e v) -> p e v", e=8), xd(g)[:, 0, :].rearrange("p (e v) -> p e v", e=8),
                                last_tok[:, hs].unsqueeze(2).to_broadcast([P, 8, HD]), ALU.mult).then_inc(xst_made, 1)
                for i in range(TT):
                    dve.wait_ge(cb_made, 2 * g + 2)
                    V.tensor_tensor(cb[:, i, :], ps[:, 2, P * i:P * i + P], masks[:, :], ALU.mult).then_inc(cb_masked, 1)
                for i in range(TT):
                    dve.wait_ge(spread, 2 * g + i + 1)
                    if i:
                        dve.wait_ge(grown, g + 1)
                    if g:
                        dve.wait_ge(y_made, 2 * g - 1 + i)
                    order.after(dve, V.tensor_tensor(pair[:, i, :, :], ps[:, 4 + 2 * i:6 + 2 * i, :].rearrange("p b (e q) -> p (b e) q", e=4),
                                                     cum_tok[:, i, hs].unsqueeze(2).to_broadcast(by_q), ALU.subtract))
                    V.tensor_scalar(pair[:, i, :, :], pair[:, i, :, :], 0.0, None, ALU.min).then_inc(differed, 1)
                V.tensor_tensor(off_side[:, :, :], off_side[:, :, :], xbc[:, c_chunk + g, P:T].unsqueeze(1).to_broadcast(by_q), ALU.mult).then_inc(off_made, 1)
                for i in range(TT):
                    dve.wait_ge(decayed, 2 * g + i + 1)
                    dve.wait_ge(cb_masked, 2 * g + i + 1)
                    V.tensor_tensor(pair[:, i, :, :], pair[:, i, :, :], cb[:, i, :].unsqueeze(1).to_broadcast(by_q), ALU.mult).then_inc(pair_made, 1)
                for i in range(TT):
                    dve.wait_ge(y_made, 2 * g + i + 1)
                    for c in range(4):
                        to = xbc[:, 4 * g + c, P * i:P * i + P]
                        last = V.scalar_tensor_tensor(to, to, par("a_d", 4 * g + c), ps[:, i, P * c:P * c + P], ALU.mult, ALU.add)
                    last.then_inc(y_added, 1)


def gate_groups(scope, y, z, *, nc, sem, sbuf, par, cst, ps, prefetch):
    sq = sbuf(scope, "group_squared", [2, 4, T])
    rms = sbuf(scope, "group_rms", [4, T])
    gated, squared, summed, rooted, inverted = (sem("group_gated"), sem("group_sq_ready"), sem("group_summed"), sem("group_rooted"),
                                                sem("group_inverted"))
    with nc.Block() as block:
        @block.sync
        def _(sp):
            prefetch(sp)

        @block.vector
        def _(dve):
            V = nc.vector

            def scale(g):
                dve.wait_ge(rooted, g + 1)
                V.reciprocal(rms[:, g % 4, :], rms[:, g % 4, :]).then_inc(inverted, 1)
                dve.wait_ge(inverted, g + 1)
                for c in range(4 * g, 4 * g + 4):
                    V.scalar_tensor_tensor(y[:, c, :], y[:, c, :], par("a_norm", c), rms[:, g % 4, :], ALU.mult, ALU.mult)

            for g in range(GROUPS):
                to = y[:, 4 * g:4 * g + 4, :]
                V.tensor_tensor(to, to, z[:, 4 * g:4 * g + 4, :], ALU.mult).then_inc(gated, 1)
                if g >= 2:
                    scale(g - 2)
            scale(GROUPS - 2)
            scale(GROUPS - 1)

        @block.scalar
        def _(act):
            def root(g):
                act.wait_ge(summed, g + 1)
                if g >= 4:
                    act.wait_ge(inverted, g - 3)
                nc.scalar.activation(rms[:, g % 4, :], ps[:, g, 0:T], ACT.Sqrt, bias=cst("eps_2"), scale=1.0 / 512).then_inc(rooted, 1)

            for g in range(GROUPS):
                act.wait_ge(gated, g + 1)
                if g >= 2:
                    act.wait_ge(summed, g - 1)
                nc.scalar.activation(sq[:, g % 2, :, :], y[:, 4 * g:4 * g + 4, :], ACT.Square).then_inc(squared, 1)
                if g >= 1:
                    root(g - 1)
            root(GROUPS - 1)

        @block.tensor
        def _(pe):
            for g in range(GROUPS):
                pe.wait_ge(squared, g + 1)
                sum_over_channels(pe, nc, cst("ones"), sq[:, g % 2, :, :], ps[:, g, 0:T], 4).then_inc(summed, 1)


def attention(x2, x3, z, out, *, nc, d, sem, sbuf, par, par_at, cst, ps, ring, **_):
    with ExitStack() as scope:
        query, gate = z[:, 0:QH // 2, :], z[:, QH // 2:QH, :]
        key = sbuf(scope, "swa_k", [KVH, T])
        value = sbuf(scope, "swa_v", [TT, KVH * HD])
        cos = sbuf(scope, "rope_cos", [T])
        sin = sbuf(scope, "rope_sin", [T])
        mask = sbuf(scope, "window", [3 * P])
        sinks = sbuf(scope, "sinks_all", [QH])

        def take_keys(act, g, sums, half, before):
            for n in range(KVH):
                last = nc.scalar.activation(key[:, n, :], sums[:, n, :], ACT.Identity, bias=par("k_bias", n))
            last.then_inc(ring.evacuated, 1)

        def take_query(act, g, sums, half, before):
            for n in range(4):
                last = nc.scalar.activation(query[:, bass.ds(4 * g + n, 1), :], sums[:, n:n + 1, :], ACT.Identity, bias=par_at("q_bias", 4 * g + n))
            last.then_inc(ring.evacuated, 1)

        def take_gate(act, g, sums, half, before):
            nc.scalar.activation(gate[:, bass.ds(4 * g, 4), :], sums, ACT.Silu).then_inc(ring.evacuated, 1)

        linear(nc, ring, ps, [
            Product(d["w_k"], KVH, x2, dict(scalar=take_keys)),
            Product(d["b_w_in"][0:4], QH // 2, x2, dict(scalar=take_query)),
            Product(d["b_w_in"][4:8], QH // 2, x2, dict(scalar=take_gate))])
        with ExitStack() as inner:
            make_tables(inner, x2, value, cos, sin, mask, sinks, nc=nc, d=d, sem=sem, sbuf=sbuf, cst=cst, ps=ps)
        rotate(query, key, cos, sin, nc=nc, sem=sem, sbuf=sbuf, cst=cst, ps=ps)
        with ExitStack() as inner:
            window_attention(inner, query, key, value, mask, sinks, gate, nc=nc, sem=sem, sbuf=sbuf, cst=cst, ps=ps)

        def add(dve, g, sums, half, before):
            nc.vector.scalar_tensor_tensor(x3[:, bass.ds(4 * g, 4), :], x2[:, bass.ds(4 * g, 4), :], ALPHA, sums,
                                           ALU.mult, ALU.add).then_inc(ring.evacuated, 1)

        linear(nc, ring, ps, [Product(d["b_w_out"], DC, gate, dict(vector=add))])
    layernorm(x3, 1, nc=nc, sem=sem, sbuf=sbuf, par=par, cst=cst, ps=ps)
    stored = sem("stored")
    with nc.Block() as block:
        @block.sync
        def _(sp):
            sp.dma_start(out, x3[:, :, :]).then_inc(stored, 16)
            sp.wait_ge(stored, 16)


def make_tables(scope, x2, value, cos, sin, mask, sinks, *, nc, d, sem, sbuf, cst, ps):
    w_v = sbuf(scope, "w_v", [DC, KVH * HD])
    v_bias = scope.enter_context(nc.sbuf_tensor("v_bias", [1, KVH * HD], F32))
    pos = sbuf(scope, "pos", [T], I32)
    angle = sbuf(scope, "angle", [T])
    turns = sbuf(scope, "turns", [2, T])
    pos_in, w_in, sinks_in = sem("pos_in"), sem("w_v_in"), sem("sinks_in")
    reduced, valued, masked = sem("angles_reduced"), sem("swa_v_made"), sem("window_made")
    order, pool_order = Order(sem("table_order")), Order(sem("window_order"))
    with nc.Block() as block:
        @block.sync
        def _(sp):
            sp.dma_start(pos[:, :], d["positions"].to_broadcast([P, T])).then_inc(pos_in, 16)
            sp.dma_start(sinks[:, :], d["sinks"].to_broadcast([P, QH])).then_inc(sinks_in, 16)
            sp.dma_start(v_bias[:, :], d["v_bias"]).then_inc(w_in, 16)
            sp.dma_start(w_v[:, :, :], d["w_v"]).then_inc(w_in, 16)
            sp.wait_ge(sinks_in, 16)

        @block.gpsimd
        def _(pool):
            G = nc.gpsimd
            pool_order.after(pool, G.memset(mask[:, :], 0.0))
            pool_order.mark(G.affine_select(out=mask[:, 0:P], in_=mask[:, 0:P], compare_op=ALU.is_ge, fill=NEG, base=0,
                                            pattern=[[-1, P]], channel_multiplier=1))
            pool_order.mark(G.affine_select(out=mask[:, P:2 * P], in_=mask[:, P:2 * P], compare_op=ALU.is_gt, fill=NEG, base=0,
                                            pattern=[[1, P]], channel_multiplier=-1))
            pool_order.mark(G.affine_select(out=mask[:, 2 * P:3 * P], in_=mask[:, 2 * P:3 * P], compare_op=ALU.is_ge, fill=NEG, base=0,
                                            pattern=[[-1, P]], channel_multiplier=1))

        @block.vector
        def _(dve):
            V = nc.vector
            dve.wait_ge(pos_in, 16)
            order.after(dve, V.tensor_copy(angle[:, :], pos[:, :]))
            order.after(dve, V.tensor_scalar(angle[:, :], angle[:, :], cst("freq"), None, ALU.mult))
            for i, (to, quarter, ahead) in enumerate(((sin, 0.0, 0.0), (cos, 0.25, np.pi / 2))):
                n = turns[:, i, :]
                order.after(dve, V.tensor_scalar(n, angle[:, :], 1 / TWO_PI, quarter, ALU.mult, ALU.add))
                order.after(dve, V.tensor_scalar(n, n, ROUND, None, ALU.add))
                order.after(dve, V.tensor_scalar(n, n, -ROUND, None, ALU.add))
                order.after(dve, V.scalar_tensor_tensor(to[:, :], n, -PI_A, angle[:, :], ALU.mult, ALU.add))
                order.after(dve, V.scalar_tensor_tensor(to[:, :], n, -PI_B, to[:, :], ALU.mult, ALU.add))
                order.after(dve, V.scalar_tensor_tensor(to[:, :], n, -PI_C, to[:, :], ALU.mult, ALU.add))
                order.after(dve, V.tensor_scalar(to[:, :], to[:, :], float(ahead), PI_LOW, ALU.add, ALU.min))
                V.tensor_scalar(to[:, :], to[:, :], -PI_LOW, None, ALU.max).then_inc(reduced, 1)

        @block.scalar
        def _(act):
            for i, to in enumerate((sin, cos)):
                act.wait_ge(reduced, i + 1)
                nc.scalar.activation(to[:, :], to[:, :], ACT.Sin)
            for i in range(TT):
                act.wait_ge(valued, i + 1)
                nc.scalar.activation(value[:, i, :], ps[:, i, 0:T], ACT.Copy)

        @block.tensor
        def _(pe):
            pe.wait_ge(w_in, 32)
            for i in range(TT):
                for c in range(DC):
                    nc.tensor.matmul(ps[:, i, 0:T], x2[:, c, P * i:P * i + P], w_v[:, c, :], start=(c == 0), stop=False)
                nc.tensor.matmul(ps[:, i, 0:T], cst("ones")[0:1, :], v_bias[:, :], start=False, stop=True).then_inc(valued, 1)


def rotate(query, key, cos, sin, *, nc, sem, sbuf, cst, ps):
    jobs = [query[:, 4 * g:4 * g + 4, :] for g in range(4)] + [key[:, :, :]]
    by_t = [P, 4, T]
    turned, multiplied = sem("rope_turned"), sem("rope_multiplied")
    order = Order(sem("rope_order"))
    with ExitStack() as scope:
        part = sbuf(scope, "rope_part", [2, 4, T])
        with nc.Block() as block:
            @block.tensor
            def _(pe):
                for n, x in enumerate(jobs):
                    if n >= 4:
                        pe.wait_ge(multiplied, n - 3)
                    for c in range(4):
                        last = nc.tensor.matmul(ps[:, 2 * (n % 4) + c // 2, T * (c % 2):T * (c % 2) + T], cst("turn"), x[:, c, :],
                                                start=True, stop=True)
                    last.then_inc(turned, 1)

            @block.vector
            def _(dve):
                V = nc.vector
                for n, x in enumerate(jobs):
                    dve.wait_ge(turned, n + 1)
                    sums = ps[:, 2 * (n % 4):2 * (n % 4) + 2, :].rearrange("p b (c t) -> p (b c) t", c=2)
                    V.tensor_tensor(part[:, n % 2, :, :], sums, sin[:, :].unsqueeze(1).to_broadcast(by_t), ALU.mult).then_inc(multiplied, 1)
                    order.mark(V.tensor_tensor(x, x, cos[:, :].unsqueeze(1).to_broadcast(by_t), ALU.mult))
                    dve.wait_ge(multiplied, n + 1)
                    order.settle(dve)
                    order.after(dve, V.tensor_tensor(x, x, part[:, n % 2, :, :], ALU.add))


def window_attention(scope, query, key, value, mask, sinks, gate, *, nc, sem, sbuf, cst, ps):
    G, N = KVH, QH // KVH
    logits = sbuf(scope, "swa_logits", [2, N, 3 * P])
    p_t = sbuf(scope, "swa_p_t", [2, 3 * P])
    peak = sbuf(scope, "swa_peak", [2, 2, N])
    total = sbuf(scope, "swa_total", [2, 2, N])
    sunk = sbuf(scope, "swa_sunk", [2, 2, N])
    dotted, added, shifted, exped, scaled = sem("swa_dotted"), sem("swa_added"), sem("swa_shifted"), sem("swa_exped"), sem("swa_scaled")
    turned, copied, valued, gated = sem("swa_turned"), sem("swa_p_copied"), sem("swa_valued"), sem("swa_gated")
    order = Order(sem("swa_order"))
    with nc.Block() as block:
        @block.tensor
        def _(pe):
            def dots(g):
                for e in range(N):
                    h = N * g + e
                    rows = slice(64 * (h % 2), 64 * (h % 2) + 64)
                    if h >= 4:
                        pe.wait_ge(added, h - 3)
                    nc.tensor.matmul(ps[:, h % 4, 0:P], query[rows, h // 2, 0:P], key[rows, g, 0:P], start=True, stop=True)
                    nc.tensor.matmul(ps[:, h % 4, P:3 * P], query[rows, h // 2, P:T], key[rows, g, :], start=True, stop=True).then_inc(dotted, 1)

            def values(h):
                rows = slice(64 * (h % 2), 64 * (h % 2) + 64)
                pe.wait_ge(copied, h + 1)
                if h >= 2:
                    pe.wait_ge(gated, h - 1)
                v = [value[:, s, HD * (h // N):HD * (h // N) + HD] for s in range(TT)]
                p = [p_t[:, h % 2, P * s:P * s + P] for s in range(3)]
                bank = ps[rows, 6 + h % 2, :]
                nc.tensor.matmul(bank[:, 0:P], v[0], p[0], start=True, stop=True)
                nc.tensor.matmul(bank[:, P:T], v[0], p[1], start=True, stop=False)
                nc.tensor.matmul(bank[:, P:T], v[1], p[2], start=False, stop=True).then_inc(valued, 1)

            dots(0)
            for g in range(G):
                if g + 1 < G:
                    dots(g + 1)
                pe.wait_ge(scaled, g + 1)
                for h in range(N * g, N * g + N):
                    if h >= 2:
                        pe.wait_ge(copied, h - 1)
                    for s in range(3):
                        last = nc.tensor.transpose(ps[:, 4 + h % 2, P * s:P * s + P], logits[:, g % 2, h % N, P * s:P * s + P], cst("ident"))
                    last.then_inc(turned, 1)
                    if h > N * g:
                        values(h - 1)
                values(N * g + N - 1)

        @block.vector
        def _(dve):
            V = nc.vector

            def soften(g):
                b = g % 2
                for e in range(N):
                    h = N * g + e
                    dve.wait_ge(dotted, h + 1)
                    if g >= 2:
                        dve.wait_ge(turned, N * (g - 1))
                    V.scalar_tensor_tensor(logits[:, b, e, :], ps[:, h % 4, 0:3 * P], SA_SCALE, mask[:, :], ALU.mult, ALU.add).then_inc(added, 1)
                dve.wait_ge(added, N * (g + 1))
                order.mark(V.tensor_reduce(peak[:, b, 0, :], logits[:, b, :, 0:P], AX, ALU.max))
                order.mark(V.tensor_reduce(peak[:, b, 1, :], logits[:, b, :, P:3 * P], AX, ALU.max))
                order.settle(dve)
                sink = sinks[:, N * g:N * g + N].unsqueeze(1).to_broadcast([P, 2, N])
                order.after(dve, V.tensor_tensor(peak[:, b, :, :], peak[:, b, :, :], sink, ALU.max))
                order.after(dve, V.tensor_scalar(peak[:, b, :, :], peak[:, b, :, :], -1.0, None, ALU.mult))
                V.tensor_tensor(sunk[:, b, :, :], peak[:, b, :, :], sink, ALU.add).then_inc(shifted, 1)

            def gates(h):
                dve.wait_ge(valued, h + 1)
                rows = slice(64 * (h % 2), 64 * (h % 2) + 64)
                to = gate[rows, h // 2, :]
                V.tensor_tensor(to, to, ps[rows, 6 + h % 2, 0:T], ALU.mult).then_inc(gated, 1)

            soften(0)
            for g in range(G):
                b = g % 2
                if g + 1 < G:
                    soften(g + 1)
                dve.wait_ge(exped, g + 1)
                order.after(dve, V.tensor_tensor(total[:, b, :, :], total[:, b, :, :], sunk[:, b, :, :], ALU.add))
                order.after(dve, V.reciprocal(total[:, b, :, :], total[:, b, :, :]))
                for i, w in enumerate((slice(0, P), slice(P, 3 * P))):
                    order.mark(V.tensor_tensor(logits[:, b, :, w], logits[:, b, :, w],
                                               total[:, b, i, :].unsqueeze(2).to_broadcast([P, N, w.stop - w.start]), ALU.mult))
                order.settle(dve)
                dve.sem_inc(scaled, 1)
                for h in range(N * g, N * g + N):
                    gates(h)

        @block.scalar
        def _(act):
            def exps(g):
                b = g % 2
                act.wait_ge(shifted, g + 1)
                for i, w in enumerate((slice(0, P), slice(P, 3 * P))):
                    for e in range(N):
                        nc.scalar.activation(logits[:, b, e, w], logits[:, b, e, w], ACT.Exp, bias=peak[:, b, i, e:e + 1],
                                             accum_out=total[:, b, i, e:e + 1])
                nc.scalar.activation(sunk[:, b, :, :], sunk[:, b, :, :], ACT.Exp).then_inc(exped, 1)

            exps(0)
            for g in range(G):
                if g + 1 < G:
                    exps(g + 1)
                for h in range(N * g, N * g + N):
                    act.wait_ge(turned, h + 1)
                    if h >= 2:
                        act.wait_ge(valued, h - 1)
                    nc.scalar.activation(p_t[:, h % 2, :], ps[:, 4 + h % 2, 0:3 * P], ACT.Copy).then_inc(copied, 1)


def pack_params(np, v):
    def chunks(a, n):
        a = np.asarray(a).reshape(-1)
        full = np.zeros(n * P, np.float32)
        full[:a.size] = a
        return full.reshape(n, P).T

    mix = v["shift_mix"][0]
    conv = v["a_conv_w_2"][0].reshape(4 * CONVC, P).T
    kb = np.repeat(v["kv_b_2"][:256].reshape(4, 1, 64), 2, axis=1)
    ab = np.concatenate
    cols = dict(
        norm_mix=chunks(v["norm_mix_g"], 16), mix=chunks(mix, 27), w0=chunks(v["w0"], 8), a0=chunks(v["a0"], 8),
        k_k=chunks(v["k_k"], 8), k_a=chunks(v["k_a"], 8), r_k=chunks(v["r_k"], 8), ln_x_w=chunks(v["ln_x_w"], 8),
        ln_x_b=chunks(v["ln_x_b"], 8), kv_norm=chunks(v["kv_norm_g"], 2), norm_ffn=chunks(v["norm_ffn_g"], 16),
        norm_final=chunks(v["norm_final_g"], 16), ln_g=chunks(v["ln_g_2"], 32), ln_b=chunks(v["ln_b_2"], 32),
        conv_w=conv, conv_b=chunks(v["a_conv_b_2"], CONVC), dt_bias=chunks(v["a_dt_bias_2"], 1),
        a_log=chunks(v["a_log_2"], 1), a_d=chunks(np.repeat(v["a_d_2"][0], 64), 32), a_norm=chunks(v["a_norm_w_2"], 32),
        q_bias=chunks(v["b_q_bias_2"], 16), k_bias=chunks(kb, 4))
    return np.ascontiguousarray(ab([cols[n] for n in PARAM_COLS], axis=1))


def make_const(np):
    j, t = np.arange(2 * CH)[:, None], np.arange(2 * CH)[None, :]
    mask = np.zeros((P, 2 * CH), np.float32)
    mask[:2 * CH] = np.where(t < CH, j % CH < t % CH, j % CH <= t % CH)
    heads = np.kron(np.eye(2), np.ones((64, 64)))
    turn = np.zeros((P, P), np.float32)
    freq = np.zeros((P, 1), np.float32)
    f = (np.float32(500000.0) ** (-np.arange(0, 16, 2, dtype=np.float32) / np.float32(16))).astype(np.float32)
    for base in (0, 64):
        for i in range(8):
            turn[base + i + 8, base + i] = -1.0
            turn[base + i, base + i + 8] = 1.0
            freq[base + i] = freq[base + i + 8] = f[i]
    full = lambda x: np.full((P, 1), x, np.float32)
    cols = dict(ident=np.eye(P), ones=np.ones((P, P)), heads=heads, flip=np.eye(P)[::-1], decay_mask=mask, turn=turn, freq=freq,
                iota=np.tile(np.arange(16), (P, 1)), eps_rms=full(EPS_RMS), eps_gn=full(EPS_GN), eps_2=full(EPS_2))
    return np.ascontiguousarray(np.concatenate([cols[n] for n in CONST_COLS], axis=1).astype(np.float32))


def make_buckets(np):
    rel = np.arange(2 * T) - (T - 1)
    n = np.abs(rel)
    large = 8 + (np.log(np.maximum(n, 1).astype(np.float32) / np.float32(8)).astype(np.float32)
                 / np.float32(np.log(1024 / 8)) * np.float32(8)).astype(np.int32)
    bucket = (rel > 0) * 16 + np.where(n < 8, n, np.minimum(large, 15))
    return np.ascontiguousarray((np.arange(32)[:, None] == bucket[None, :]).astype(np.float32))


def kernel(**inputs):
    import concourse.bacc as bacc
    from concourse.bass_utils import run_bass_kernel_spmd

    v = {k: np.asarray(a) for k, a in inputs.items()}

    def rows(w):
        return np.ascontiguousarray(w.reshape(w.shape[0] // P, P, w.shape[1]).transpose(1, 0, 2))

    def pack(w):
        k, n = w.shape
        g = (n + 511) // 512
        full = np.zeros((k, g * 512), w.dtype)
        full[:, :n] = w
        return np.ascontiguousarray(full.reshape(k // P, P, g, 512).transpose(2, 1, 0, 3))

    w_in = v["w_in"][0]
    rw = w_in[:, :3360]
    q, ckv, iq, ik, iw, gates = np.split(w_in[:, 3360:], np.cumsum([1024, 256, 512, 64, 8]), axis=1)
    blank = np.zeros((D, P - IW_ROW - IDX_HEADS), np.float32)
    kv = v["kv_w_2"]
    k_twice = np.repeat(kv[:, :256].reshape(D, 4, 1, 64), 2, axis=2).reshape(D, 512)
    up = v["w_gate_up"][0]
    gate_up = np.zeros((2, P, H * HD), np.float32)
    gate_up[0] = up[:P]
    gate_up[1, :GATE_RANK - P] = up[P:]
    data = dict(
        x=rows(v["x"][0].T), params=pack_params(np, v), const=make_const(np), bucket_hot=make_buckets(np),
        w_in=pack(np.concatenate([rw, iw, blank, q, ckv, iq, ik, ik], axis=1)), w_gates=pack(gates),
        lora=np.ascontiguousarray(np.concatenate([v["w_decay_up"][0], v["w_icl_up"][0]], axis=0)),
        gate_up=np.ascontiguousarray(gate_up.transpose(1, 0, 2)), rel_bias=np.ascontiguousarray(v["rel_bias"]),
        w_uk=rows(v["w_uk"][0].transpose(1, 0, 2).reshape(256, 1024)),
        w_uv=rows(v["w_uv"][0].transpose(1, 0, 2).reshape(256, 1024)),
        w_branch_rwkv=pack(v["w_branch_rwkv"][0]), w_branch_dsa=pack(v["w_branch_dsa"][0]), w_out=pack(v["w_out"][0]),
        w_query=pack(v["w_peer_query"][0]),
        sub_keys=np.ascontiguousarray(v["peer_sub_keys"][0].transpose(3, 0, 1, 2).reshape(P, 16, P)),
        peer_u=np.ascontiguousarray(v["peer_u"][0]), peer_v=np.ascontiguousarray(v["peer_v"][0]),
        a_w_z=pack(v["a_w_in_2"][0][:, :4096]), a_w_conv=pack(v["a_w_in_2"][0][:, 4096:10240]),
        a_w_dt=pack(v["a_w_in_2"][0][:, 10240:]), a_w_out=pack(v["a_w_out_2"][0]),
        w_k=pack(k_twice), w_v=rows(np.ascontiguousarray(kv[:, 256:])),
        v_bias=np.ascontiguousarray(v["kv_b_2"][256:].reshape(1, 256)),
        sinks=np.ascontiguousarray(v["b_sinks_2"].reshape(1, QH)),
        positions=np.ascontiguousarray(v["positions_2"].reshape(1, T)),
        b_w_in=pack(v["b_w_in_2"][0]), b_w_out=pack(v["b_w_out_2"][0]),
    )
    nc = bacc.Bacc("TRN2", target_bir_lowering=False, num_devices=1)
    d = {n: nc.dram_tensor(f"in_{n}", a.shape, mybir.dt.from_np(a.dtype), kind="ExternalInput").ap()
         for n, a in data.items()}
    out = nc.dram_tensor("out_t", [P, DC, T], F32, kind="ExternalOutput").ap()
    build(nc, d, out)
    got = run_bass_kernel_spmd(nc, [{f"in_{n}": a for n, a in data.items()}], core_ids=[0]).results[0]["out_t"]
    return np.ascontiguousarray(got.transpose(2, 1, 0).reshape(1, T, D))
```

```python
from contextlib import ExitStack

import concourse.bass as bass
import numpy as np
from concourse import mybir

F32 = mybir.dt.float32
F32R = mybir.dt.float32r
U32 = mybir.dt.uint32
I32 = mybir.dt.int32
ACT = mybir.ActivationFunctionType
ALU = mybir.AluOpType
AX = mybir.AxisListType.X

P = 128
T = 256
TT = T // P
D = 2048
DC = D // P
H = 16
HD = 64
HC = H * HD // P
GATE_RANK = 160
IDX_HEADS = 8
IDX_SCALE = (IDX_HEADS * 64) ** -0.5
SA_SCALE = HD ** -0.5
KV_CHUNKS = 2
TOPK = 64
CH = 32
NCH = T // CH
EXP_HALF = float(np.float32(np.exp(-0.5)))
PK_HEADS, PK_KEYS, PK_TOP = 8, 128, 16
PK_SEL = PK_HEADS * PK_TOP
NEG = -1.0e30
DROPPED, TAKEN = -1.0e38, -3.0e38
SSM_H, GROUPS = 64, 8
ZC, CONVC = 32, 48
ALPHA = 4.0 ** 0.25
EPS_RMS, EPS_GN, EPS_2 = 1e-6, 64e-5, 1e-5
QH, KVH = 32, 4
TWO_PI = 2 * np.pi
PI_A = 6.28125
PI_B = 0.0019350051879882812
PI_C = float(TWO_PI - PI_A - PI_B)
PI_LOW = 3.1415925
ROUND = 12582912.0

C_R, C_K, C_V, C_WA, C_G, C_GI, C_Q, C_KV, C_IQ, C_IK = 0, 8, 16, 24, 25, 26, 27, 35, 37, 41
C_IN = 42
IW_ROW = 32

PARAM_COLS = dict(
    norm_mix=16, mix=C_IN, w0=8, a0=8, k_k=8, k_a=8, r_k=8, ln_x_w=8, ln_x_b=8, kv_norm=2, norm_ffn=16,
    norm_final=16, ln_g=32, ln_b=32, conv_w=4 * CONVC, conv_b=CONVC, dt_bias=1, a_log=1, a_d=32, a_norm=32,
    q_bias=16, k_bias=4, v_bias=2)
CONST_COLS = dict(ident=128, ones=128, heads=128, flip=128, decay_mask=64, turn=128, freq=1, iota=16, eps_rms=1,
                  eps_gn=1, eps_2=1)


def columns(sizes):
    at, out = 0, {}
    for name, n in sizes.items():
        out[name] = (at, n)
        at += n
    return out, at


PARAM_AT, N_PARAM = columns(PARAM_COLS)
CONST_AT, N_CONST = columns(CONST_COLS)


class Order:

    def __init__(self, sem):
        self.sem, self.n = sem, 0

    def mark(self, ins):
        self.n += 1
        ins.then_inc(self.sem, 1)
        return self.n

    def settle(self, eng):
        eng.wait_ge(self.sem, self.n)

    def after(self, eng, ins):
        self.mark(ins)
        self.settle(eng)


class Ring:

    SLOTS = 4

    def __init__(self, nc, ctx):
        self.buf = ctx.enter_context(nc.sbuf_tensor("weights", [P, self.SLOTS, 4, 512], F32))
        self.loaded = [ctx.enter_context(nc.semaphore(f"weights_loaded{q}")) for q in range(self.SLOTS)]
        self.high = ctx.enter_context(nc.semaphore("part_high"))
        self.split = ctx.enter_context(nc.semaphore("part_split"))
        self.used = ctx.enter_context(nc.semaphore("part_used"))
        self.evacuated = ctx.enter_context(nc.semaphore("evacuated"))
        self.parts = 0
        self.groups = 0
        self.ahead = False

    def load(self, sp, w, g, q, part, columns=512):
        slot = q % self.SLOTS if w.shape[2] >= 16 else q
        if not isinstance(part, int) or part >= self.SLOTS:
            sp.wait_ge(self.split, part - self.SLOTS + 1)
        rows = 4 * (q % (w.shape[2] // 4))
        src = w[bass.ds(g, 1), :, rows:rows + 4, 0:columns].rearrange("a p k n -> (a p) k n")
        sp.dma_start(self.buf[:, slot, :, 0:columns], src).then_inc(self.loaded[slot], 16)

    def prefetch(self, sp, w, part):
        parts = w.shape[2] // 4
        for s in range(self.SLOTS):
            self.load(sp, w, s // parts, s, part + s)
        self.ahead = True


class Product:

    def __init__(self, w, chunks, rhs, evac, ready=None, alongside=None):
        self.w, self.rhs, self.ready, self.alongside = w, rhs, ready, alongside
        self.evac = {name: f if isinstance(f, tuple) else (f,) for name, f in evac.items()}
        self.parts = w.shape[2] // 4
        self.groups = (chunks + 3) // 4
        self.live = [min(4, chunks - 4 * g) for g in range(self.groups)]
        self.pairs = sum(n == 4 for n in self.live) // 2
        self.new_rhs = True

    def each_group(self, eng, group):
        def at(g, half, first):
            group(eng, g, (self.half0 + half) % 2, first, 4)

        if self.pairs:
            for half in range(2):
                at(half, half, self.p0 + half * self.parts)
        if self.pairs > 1:
            with eng.Fori(1, self.pairs) as j:
                for half in range(2):
                    at(2 * j + half, half, self.p0 + half * self.parts + 2 * self.parts * j)
        for g in range(2 * self.pairs, self.groups):
            group(eng, g, (self.half0 + g) % 2, self.p0 + g * self.parts, self.live[g])


def linear(nc, ring, ps, products, next_w=None):
    S = ring.SLOTS
    start, ahead, ring.ahead = ring.parts, ring.ahead, False
    part, group = ring.parts, ring.groups
    for i, m in enumerate(products):
        m.p0, m.g0, m.half0 = part, group, (group - ring.groups) % 2
        m.new_rhs = i == 0 or m.rhs is not products[i - 1].rhs
        part += m.groups * m.parts
        group += m.groups

    with ExitStack() as scope:
        kept = max(m.parts for m in products)
        w_half = scope.enter_context(nc.sbuf_tensor(f"w_half{start}", [P, 2, 2, 4, 512], F32R))
        x_half = scope.enter_context(nc.sbuf_tensor(f"x_half{start}", [P, kept, 2, 4, T], F32R))

        with nc.Block() as block:
            @block.sync
            def _(sp):
                if not ahead:
                    ring.prefetch(sp, products[0].w, start)
                    ring.ahead = False
                for m in products:
                    if m.alongside:
                        m.alongside(sp)

                    def load(sp, g, half, part, n_live, m=m):
                        for q in range(m.parts):
                            if isinstance(part, int) and part + q < start + S:
                                continue
                            ring.load(sp, m.w, g, ((half - m.half0) % 2 * m.parts + q) % max(S, m.parts), part + q, P * n_live)

                    m.each_group(sp, load)
                if next_w is not None:
                    ring.prefetch(sp, next_w, part)

            @block.tensor
            def _(pe):
                for m in products:
                    def multiply(pe, g, half, part, n_live, m=m):
                        if not isinstance(g, int) or m.g0 + g > ring.groups + 1:
                            pe.wait_ge(ring.evacuated, m.g0 + g - 1)
                        for q in range(m.parts):
                            pe.wait_ge(ring.split, part + q + 1)
                            for n in range(n_live):
                                for k in range(4):
                                    for i, (wh, xh) in enumerate(((0, 0), (0, 1), (1, 0))):
                                        last = nc.tensor.matmul(
                                            ps[:, 4 * half + n, 0:T], w_half[:, q % 2, wh, k, P * n:P * n + P], x_half[:, q, xh, k, :],
                                            start=(q == 0 and k == 0 and i == 0), stop=(q == m.parts - 1 and k == 3 and i == 2))
                            last.then_inc(ring.used, 1)

                    m.each_group(pe, multiply)

            def parts_and_sums(eng, one, name):
                def sums(m, g, half, part, n_live, steps):
                    if steps.start == 0 and m.evac.get(name):
                        eng.wait_ge(ring.used, part + m.parts)
                    for f in m.evac.get(name, ())[steps]:
                        f(eng, g, ps[:, 4 * half:4 * half + n_live, 0:T], half, m.g0 + g)

                def last_group(m, steps):
                    sums(m, m.groups - 1, (m.half0 + m.groups - 1) % 2, m.p0 + (m.groups - 1) * m.parts, m.live[-1], steps)

                for before, m in zip([None] + products, products):
                    def halves(eng, g, half, part, n_live):
                        for q in range(m.parts):
                            one(eng, m, q, g, ((half - m.half0) % 2 * m.parts + q) % S, part + q, P * n_live)
                            if q:
                                steps = slice(q - 1, q if q < m.parts - 1 else None)
                                if not isinstance(g, int) or g > 0:
                                    sums(m, g - 1, 1 - half, part - m.parts, 4, steps)
                                elif before:
                                    last_group(before, steps)

                    m.each_group(eng, halves)
                last_group(products[-1], slice(0, None))

            @block.scalar
            def _(act):
                def high(act, m, q, g, slot, part, columns):
                    act.wait_ge(ring.loaded[slot], 4 * (part - slot) + 16)
                    if not isinstance(part, int) or part >= start + 2:
                        act.wait_ge(ring.used, part - 1)
                    if isinstance(g, int) and g == 0 and m.new_rhs:
                        if m.ready:
                            act.wait_ge(m.ready[0], m.ready[1] * (q + 1))
                        nc.scalar.activation(x_half[:, q, 0, :, :], m.rhs[:, 4 * q:4 * q + 4, :], ACT.Copy)
                    nc.scalar.activation(w_half[:, q % 2, 0, :, 0:columns], ring.buf[:, slot, :, 0:columns], ACT.Copy).then_inc(ring.high, 1)

                parts_and_sums(act, high, "scalar")

            @block.vector
            def _(dve):
                def low(dve, m, q, g, slot, part, columns):
                    dve.wait_ge(ring.high, part + 1)
                    if isinstance(g, int) and g == 0 and m.new_rhs:
                        nc.vector.tensor_tensor(x_half[:, q, 1, :, :], m.rhs[:, 4 * q:4 * q + 4, :], x_half[:, q, 0, :, :].bitcast(F32), ALU.subtract)
                    nc.vector.tensor_tensor(w_half[:, q % 2, 1, :, 0:columns], ring.buf[:, slot, :, 0:columns],
                                            w_half[:, q % 2, 0, :, 0:columns].bitcast(F32), ALU.subtract).then_inc(ring.split, 1)

                parts_and_sums(dve, low, "vector")
    ring.parts, ring.groups = part, group


def sum_over_channels(pe, nc, ones, sq, out, chunks, squared=None):
    for c in range(chunks):
        if squared and c % 4 == 0:
            pe.wait_ge(squared, c // 4 + 1)
        last = nc.tensor.matmul(out, ones, sq[:, c, :], start=(c == 0), stop=(c == chunks - 1))
    return last


def rmsnorm(nc, sem, cst, ps, src, dst, gain, tmp, chunks, eps, prefetch=None):
    squared, summed, rooted = sem("squared"), sem("summed"), sem("rooted")
    order = Order(sem("norm_order"))
    with nc.Block() as block:
        if prefetch:
            @block.sync
            def _(sp):
                prefetch(sp)

        @block.scalar
        def _(act):
            for c in range(0, chunks, 4):
                w = slice(c, min(c + 4, chunks))
                nc.scalar.activation(dst[:, w, :], src[:, w, :], ACT.Square).then_inc(squared, 1)
            act.wait_ge(summed, 1)
            nc.scalar.activation(tmp, ps[:, 0, 0:T], ACT.Sqrt, bias=cst(eps), scale=1.0 / (P * chunks)).then_inc(rooted, 1)

        @block.tensor
        def _(pe):
            sum_over_channels(pe, nc, cst("ones"), dst, ps[:, 0, 0:T], chunks, squared).then_inc(summed, 1)

        @block.vector
        def _(dve):
            dve.wait_ge(rooted, 1)
            order.after(dve, nc.vector.reciprocal(tmp, tmp))
            for c in range(chunks):
                nc.vector.scalar_tensor_tensor(dst[:, c, :], src[:, c, :], gain[:, c:c + 1], tmp, ALU.mult, ALU.mult)


def build(nc, d, out):
    ctx = ExitStack()
    made = {}

    in_use = []

    def sem(name):
        made[name] = made.get(name, 0) + 1
        in_use.append(nc.alloc_semaphore(f"{name}_{made[name]}"))
        return in_use[-1]

    def recycle():
        nc.clear_and_free_semaphores(list(in_use))
        nc.all_engine_barrier()
        in_use.clear()

    def sbuf(scope, name, shape, dt=F32):
        return scope.enter_context(nc.sbuf_tensor(name, [P] + shape, dt))

    with ctx:
        params = sbuf(ctx, "params", [N_PARAM])
        const = sbuf(ctx, "const", [N_CONST])
        ps = ctx.enter_context(nc.psum_tensor("ps", [P, 8, 512], F32))
        ring = Ring(nc, ctx)

        def par(name, i=0, n=1):
            return params[:, PARAM_AT[name][0] + i:PARAM_AT[name][0] + i + n]

        def par_at(name, i):
            return params[:, bass.ds(PARAM_AT[name][0] + i, 1)]

        def cst(name):
            at, n = CONST_AT[name]
            return const[:, at:at + n]

        scratch = {n: nc.dram_tensor(n, s, F32, kind="Internal").ap() for n, s in dict(
            solve_in=[P, CH, CH], solve_out=[P, CH, CH], bias_rows=[H, 2 * T]).items()}
        env = dict(nc=nc, d=d, sem=sem, sbuf=sbuf, par=par, par_at=par_at, cst=cst, ps=ps, ring=ring, scratch=scratch)

        x1 = sbuf(ctx, "x1", [DC, T])
        y_rwkv, y_dsa = x1[:, 0:HC, :], x1[:, HC:2 * HC, :]
        with ExitStack() as scope:
            xn = sbuf(scope, "xn", [DC, T])
            with ExitStack() as branches:
                gate, bonus, rms = (sbuf(branches, n, [HC, T]) for n in ("gate", "bonus", "y_deviation"))
                with ExitStack() as mix:
                    pin = sbuf(mix, "pin", [C_IN, T])
                    load_and_norm(mix, xn, params, const, **env)
                    with ExitStack() as inner:
                        project_in(inner, xn, pin, **env)
                    sparse_attention(pin, y_dsa, **env)
                    recycle()
                    rwkv(pin, y_rwkv, gate, bonus, rms, **env)
                    recycle()
                with ExitStack() as mix:
                    gates = sbuf(mix, "gates", [2 * DC, T])
                    mixed = sbuf(mix, "mixed", [DC, T])
                    mix_branches(gates, mixed, xn, y_rwkv, y_dsa, gate, bonus, rms, **env)
            recycle()
            peer(xn, x1, **env)
        recycle()
        with ExitStack() as scope:
            z = sbuf(scope, "z", [ZC, T])
            xbc = sbuf(scope, "xbc", [CONVC, T])
            x2 = xbc[:, ZC:CONVC, :]
            mamba(x1, x2, z, xbc, recycle, **env)
            recycle()
            attention(x2, x1, z, xbc[:, 0:ZC, :], out, **env)


def copy_out(nc, ring, dst):
    def f(act, g, sums, half, before):
        nc.scalar.activation(dst[:, bass.ds(4 * g, sums.shape[1]), :], sums, ACT.Copy).then_inc(ring.evacuated, 1)
    return f


def load_and_norm(scope, xn, params, const, *, nc, d, sem, sbuf, par, cst, ps, ring, **_):
    with ExitStack() as inner:
        x = sbuf(inner, "x_in", [DC, T])
        tmp = sbuf(inner, "rms", [T])
        arrived = [sem("params_arrived"), sem("const_arrived"), sem("x_arrived")]
        with nc.Block() as block:
            @block.sync
            def _(sp):
                sp.dma_start(x[:, :, :], d["x"]).then_inc(arrived[2], 16)
                sp.dma_start(params[:, :], d["params"]).then_inc(arrived[0], 16)
                sp.dma_start(const[:, :], d["const"]).then_inc(arrived[1], 16)
                ring.prefetch(sp, d["w_in"], 0)
                for a in arrived:
                    sp.wait_ge(a, 16)
        rmsnorm(nc, sem, cst, ps, x[:, :, :], xn[:, :, :], par("norm_mix", 0, DC), tmp[:, :], DC, "eps_rms")


def project_in(scope, xn, pin, *, nc, d, sem, sbuf, par_at, ps, ring, **_):
    diff = sbuf(scope, "diff", [2, 4, T])
    shifted = sem("shifted")

    def shift(dve, g, sums, half, before):
        V = nc.vector
        n_live = sums.shape[1]
        p = pin[:, bass.ds(4 * g, n_live), :]
        dve.wait_ge(ring.evacuated, before + 1)
        V.tensor_tensor(diff[:, half, 0:n_live, 1:T], p[:, :, 0:T - 1], p[:, :, 1:T], ALU.subtract).then_inc(shifted, 1)
        V.tensor_scalar(diff[:, half, 0:n_live, 0], p[:, :, 0], -1.0, None, ALU.mult).then_inc(shifted, 1)
        dve.wait_ge(shifted, 3 * g + 2)
        for n in range(n_live):
            to = pin[:, bass.ds(4 * g + n, 1), :]
            last = V.scalar_tensor_tensor(to, diff[:, half, n:n + 1, :], par_at("mix", 4 * g + n), to, ALU.mult, ALU.add)
        last.then_inc(shifted, 1)

    linear(nc, ring, ps, [Product(d["w_in"], C_IN, xn, dict(scalar=copy_out(nc, ring, pin), vector=shift))])


def sparse_attention(pin, y, *, nc, d, sem, sbuf, par, cst, ps, ring, scratch, **_):
    with ExitStack() as scope:
        k_t = sbuf(scope, "k_t", [HC, T])
        v_tok = sbuf(scope, "v_tok", [TT, H * HD])
        logits = sbuf(scope, "logits", [TT, H, T])
        with ExitStack() as inner:
            latent = sbuf(inner, "latent", [KV_CHUNKS, T])
            tmp = sbuf(inner, "latent_rms", [T])
            w_uk = sbuf(inner, "w_uk", [KV_CHUNKS, H * HD])
            w_uv = sbuf(inner, "w_uv", [KV_CHUNKS, H * HD])
            rel = inner.enter_context(nc.sbuf_tensor("rel", [32, H], F32))
            hot = inner.enter_context(nc.sbuf_tensor("hot", [32, 2 * T], F32))
            rows = inner.enter_context(nc.sbuf_tensor("rows", [H, 2 * T], F32))
            up_in, rel_in, rows_out, bias_in = sem("up_in"), sem("rel_in"), sem("rows_out"), sem("bias_in")
            made, rows_ready, keys_made, values_made, copied, normed = (sem("rows_made"), sem("rows_ready"),
                sem("keys_made"), sem("values_made"), sem("kv_copied"), sem("latent_ready"))
            rmsnorm(nc, sem, cst, ps, pin[:, C_KV:C_KV + 2, :], latent[:, :, :], par("kv_norm", 0, 2), tmp[:, :],
                    KV_CHUNKS, "eps_rms")
            with nc.Block() as block:
                @block.sync
                def _(sp):
                    sp.dma_start(rel[:, :], d["rel_bias"]).then_inc(rel_in, 16)
                    sp.dma_start(hot[:, :], d["bucket_hot"]).then_inc(rel_in, 16)
                    sp.dma_start(w_uk[:, :, :], d["w_uk"]).then_inc(up_in, 16)
                    sp.dma_start(w_uv[:, :, :], d["w_uv"]).then_inc(up_in, 16)
                    sp.wait_ge(rows_ready, 1)
                    sp.dma_start(scratch["bias_rows"], rows[:, :]).then_inc(rows_out, 16)
                    sp.wait_ge(rows_out, 16)
                    for i in range(TT):
                        src = bass.AP(scratch["bias_rows"].tensor, P - P * i, [[1, P], [2 * T, H], [1, T]])
                        sp.dma_start(logits[:, i, :, :], src).then_inc(bias_in, 16)
                    sp.wait_ge(bias_in, 16 * TT)

                @block.tensor
                def _(pe):
                    pe.wait_ge(rel_in, 32)
                    nc.tensor.matmul(ps[0:H, 7, :], rel[:, :], hot[:, :], start=True, stop=True).then_inc(made, 1)
                    pe.wait_ge(up_in, 32)
                    for c in range(HC):
                        if c == 7:
                            pe.wait_ge(rows_ready, 1)
                        for k in range(KV_CHUNKS):
                            last = nc.tensor.matmul(ps[:, c, 0:T], w_uk[:, k, P * c:P * c + P], latent[:, k, :],
                                                    start=(k == 0), stop=(k == 1))
                        last.then_inc(keys_made, 1)
                    for i in range(TT):
                        for n in range(2):
                            b = 2 * i + n
                            pe.wait_ge(copied, b + 1)
                            for k in range(KV_CHUNKS):
                                last = nc.tensor.matmul(ps[:, b, :], latent[:, k, P * i:P * i + P],
                                                        w_uv[:, k, 512 * n:512 * n + 512], start=(k == 0), stop=(k == 1))
                            last.then_inc(values_made, 1)

                @block.vector
                def _(dve):
                    dve.wait_ge(made, 1)
                    nc.vector.tensor_copy(rows[:, :], ps[0:H, 7, :]).then_inc(rows_ready, 1)

                @block.scalar
                def _(act):
                    for c in range(HC):
                        act.wait_ge(keys_made, c + 1)
                        nc.scalar.activation(k_t[:, c, :], ps[:, c, 0:T], ACT.Copy, scale=SA_SCALE).then_inc(copied, 1)
                    for b in range(4):
                        act.wait_ge(values_made, b + 1)
                        nc.scalar.activation(v_tok[:, b // 2, 512 * (b % 2):512 * (b % 2) + 512], ps[:, b, :], ACT.Copy)
        score = sbuf(scope, "score", [TT, T])
        index_scores(pin, score, nc=nc, sem=sem, sbuf=sbuf, cst=cst, ps=ps)
        softmax_heads(pin, k_t, v_tok, logits, score, y, nc=nc, sem=sem, sbuf=sbuf, cst=cst, ps=ps)


def index_scores(pin, score, *, nc, sem, sbuf, cst, ps):
    with ExitStack() as inner:
        iw = sbuf(inner, "iw", [TT, IDX_HEADS])
        relu = sbuf(inner, "relu", [4, T])
        top = sbuf(inner, "top", [TT, 8])
        turned, scored, rectified, added = sem("iw_turned"), sem("scored"), sem("rectified"), sem("score_added")
        order = Order(sem("score_order"))
        with nc.Block() as block:
            @block.tensor
            def _(pe):
                for i in range(TT):
                    nc.tensor.transpose(ps[:, 7, P * i:P * i + P], pin[:, C_GI, P * i:P * i + P], cst("ident")).then_inc(turned, 1)
                for n in range(TT * IDX_HEADS):
                    i, h = n // IDX_HEADS, n % IDX_HEADS
                    rows = slice(64 * (h % 2), 64 * (h % 2) + 64)
                    if n >= 4:
                        pe.wait_ge(rectified, n - 3)
                    nc.tensor.matmul(ps[:, n % 4, 0:T], pin[rows, C_IQ + h // 2, P * i:P * i + P], pin[rows, C_IK, :],
                                     start=True, stop=True).then_inc(scored, 1)

            @block.scalar
            def _(act):
                for n in range(TT * IDX_HEADS):
                    act.wait_ge(scored, n + 1)
                    if n >= 4:
                        act.wait_ge(added, n - 3)
                    nc.scalar.activation(relu[:, n % 4, :], ps[:, n % 4, 0:T], ACT.Relu).then_inc(rectified, 1)

            @block.vector
            def _(dve):
                dve.wait_ge(turned, 2)
                for i in range(TT):
                    order.mark(nc.vector.tensor_scalar(iw[:, i, :], ps[:, 7, P * i + IW_ROW:P * i + IW_ROW + IDX_HEADS],
                                                       IDX_SCALE, None, ALU.mult))
                order.settle(dve)
                for n in range(TT * IDX_HEADS):
                    i, h = n // IDX_HEADS, n % IDX_HEADS
                    dve.wait_ge(rectified, n + 1)
                    if h == 0:
                        nc.vector.tensor_scalar(score[:, i, :], relu[:, n % 4, :], iw[:, i, h:h + 1], None, ALU.mult).then_inc(added, 1)
                    else:
                        dve.wait_ge(added, n)
                        nc.vector.scalar_tensor_tensor(score[:, i, :], relu[:, n % 4, :], iw[:, i, h:h + 1], score[:, i, :],
                                                       ALU.mult, ALU.add).then_inc(added, 1)
                dve.wait_ge(added, TT * IDX_HEADS)
                for q in range(T // 64 - 1):
                    order.mark(nc.vector.memset(score[64 * (q % 2):64 * (q % 2) + 64, q // 2, 64 * q + 64:T], DROPPED))
                order.settle(dve)
                for _ in range(TOPK // 8):
                    for i in range(TT):
                        order.mark(nc.vector.max(top[:, i, :], score[:, i, :]))
                    order.settle(dve)
                    for i in range(TT):
                        order.mark(nc.vector.match_replace(score[:, i, :], top[:, i, :], score[:, i, :], TAKEN))
                    order.settle(dve)
                nc.vector.tensor_scalar(score[:, :, :], score[:, :, :], (DROPPED + TAKEN) / 2, NEG, ALU.is_gt, ALU.mult)


def softmax_heads(pin, k_t, v_tok, logits, mask, y, *, nc, sem, sbuf, cst, ps):
    with ExitStack() as inner:
        p_t = sbuf(inner, "p_t", [2, TT, T])
        peak = sbuf(inner, "peak", [TT, H])
        total = sbuf(inner, "total", [TT, H])
        dotted, added, peaked, exped, scaled = sem("dotted"), sem("logit_added"), sem("peaked"), sem("exped"), sem("scaled")
        turned, p_copied, valued, y_copied = sem("p_turned"), sem("p_copied"), sem("valued"), sem("y_copied")
        order = Order(sem("softmax_order"))
        with nc.Block() as block:
            def values(pe, h):
                base = 64 * (h % 2)
                pe.wait_ge(p_copied, h + 1)
                if h >= 2:
                    pe.wait_ge(y_copied, h - 1)
                for s in range(TT):
                    last = nc.tensor.matmul(ps[base:base + 64, 6 + h % 2, 0:T], v_tok[:, s, HD * h:HD * h + HD],
                                            p_t[:, h % 2, s, :], start=(s == 0), stop=(s == 1))
                last.then_inc(valued, 1)

            @block.tensor
            def _(pe):
                for n in range(TT * H):
                    i, h = n // H, n % H
                    rows = slice(64 * (h % 2), 64 * (h % 2) + 64)
                    if n >= 4:
                        pe.wait_ge(added, n - 3)
                    nc.tensor.matmul(ps[:, n % 4, 0:T], cst("flip"), logits[:, i, h, :], start=True, stop=False)
                    nc.tensor.matmul(ps[:, n % 4, 0:T], pin[rows, C_Q + h // 2, P * i:P * i + P], k_t[rows, h // 2, :],
                                     start=False, stop=True).then_inc(dotted, 1)
                pe.wait_ge(scaled, TT)
                for h in range(H):
                    if h >= 2:
                        pe.wait_ge(p_copied, h - 1)
                    for i in range(TT):
                        for s in range(TT):
                            last = nc.tensor.transpose(ps[:, 4 + h % 2, T * s + P * i:T * s + P * i + P],
                                                       logits[:, i, h, P * s:P * s + P], cst("ident"))
                    last.then_inc(turned, 1)
                    if h >= 1:
                        values(pe, h - 1)
                values(pe, H - 1)

            @block.vector
            def _(dve):
                for n in range(TT * H):
                    i, h = n // H, n % H
                    dve.wait_ge(dotted, n + 1)
                    nc.vector.tensor_tensor(logits[:, i, h, :], ps[:, n % 4, 0:T], mask[:, i, :], ALU.add).then_inc(added, 1)
                    if h == H - 1:
                        dve.wait_ge(added, n + 1)
                        nc.vector.tensor_reduce(peak[:, i, :], logits[:, i, :, :], AX, ALU.max, negate=True).then_inc(peaked, 1)
                for i in range(TT):
                    dve.wait_ge(exped, H * (i + 1))
                    order.after(dve, nc.vector.reciprocal(total[:, i, :], total[:, i, :]))
                    nc.vector.tensor_tensor(logits[:, i, :, :], logits[:, i, :, :],
                                            total[:, i, :].unsqueeze(2).to_broadcast([P, H, T]), ALU.mult).then_inc(scaled, 1)
                for h in range(H):
                    base = 64 * (h % 2)
                    dve.wait_ge(valued, h + 1)
                    nc.vector.tensor_copy(y[base:base + 64, h // 2, :], ps[base:base + 64, 6 + h % 2, 0:T]).then_inc(y_copied, 1)

            @block.scalar
            def _(act):
                for n in range(TT * H):
                    i, h = n // H, n % H
                    if h == 0:
                        act.wait_ge(peaked, i + 1)
                    nc.scalar.activation(logits[:, i, h, :], logits[:, i, h, :], ACT.Exp, bias=peak[:, i, h:h + 1],
                                         accum_out=total[:, i, h:h + 1]).then_inc(exped, 1)
                for h in range(H):
                    act.wait_ge(turned, h + 1)
                    if h >= 2:
                        act.wait_ge(valued, h - 1)
                    nc.scalar.activation(p_t[:, h % 2, :, :].rearrange("p s q -> p (s q)"), ps[:, 4 + h % 2, :], ACT.Copy).then_inc(p_copied, 1)


def rwkv(pin, y, gate, bonus, t1, *, nc, d, sem, sbuf, par, cst, ps, ring, scratch, **_):
    with ExitStack() as scope:
        left = sbuf(scope, "left", [HC, NCH, 2 * CH])
        right = sbuf(scope, "right", [HC, NCH, 2 * CH])
        chunk_decay = sbuf(scope, "chunk_decay", [HC, NCH])
        with ExitStack() as inner:
            prepare_recurrence(inner, pin, left, right, gate, bonus, t1, chunk_decay, nc=nc, d=d, sem=sem, sbuf=sbuf,
                               par=par, cst=cst, ps=ps)
        with ExitStack() as inner:
            pairs = inner.enter_context(nc.sbuf_tensor("pairs", [2 * CH, NCH, 2, HC, 2 * CH], F32))
            solve_corrections(pin, left, right, pairs, nc=nc, sem=sem, sbuf=sbuf, cst=cst, ps=ps, scratch=scratch)
            recur(pin, left, right, pairs, chunk_decay, y, nc=nc, sem=sem, sbuf=sbuf, cst=cst, ps=ps)


def prepare_recurrence(scope, pin, left, right, gate, bonus, t1, chunk_decay, *, nc, d, sem, sbuf, par, cst, ps):
    log_decay = sbuf(scope, "log_decay", [HC, T])
    icl = sbuf(scope, "icl", [HC, T])
    kk = sbuf(scope, "kk", [HC, T])
    t2 = sbuf(scope, "t2", [HC, T])
    kept = sbuf(scope, "scan_kept", [T])
    lora = t1[:, 0:4, :].rearrange("p a b -> p (a b)")
    gate_up = t2[:, :, :].rearrange("p (k a) b -> p k (a b)", k=2)
    lora_in, squashed, ranked, unranked = sem("lora_in"), sem("squashed"), sem("ranked"), sem("unranked")
    with nc.Block() as block:
        @block.sync
        def _(sp):
            sp.dma_start(lora, d["lora"]).then_inc(lora_in, 16)
            sp.dma_start(gate_up, d["gate_up"]).then_inc(lora_in, 16)

        @block.scalar
        def _(act):
            nc.scalar.activation(pin[0:64, C_WA, :], pin[0:64, C_WA, :], ACT.Tanh).then_inc(squashed, 1)
            nc.scalar.activation(pin[:, C_G, :], pin[:, C_G, :], ACT.Sigmoid).then_inc(squashed, 1)
            nc.scalar.activation(pin[0:GATE_RANK - P, C_GI, :], pin[0:GATE_RANK - P, C_GI, :], ACT.Sigmoid).then_inc(squashed, 1)
            for n in range(3 * HC):
                c, kind = n // 3, n % 3
                act.wait_ge(ranked, n + 1)
                if kind < 2:
                    to, bias = (log_decay, par("w0", c)) if kind == 0 else (icl, par("a0", c))
                    nc.scalar.activation(to[:, c, :], ps[:, n % 8, 0:T], ACT.Sigmoid, bias=bias).then_inc(unranked, 1)
                else:
                    nc.scalar.activation(gate[:, c, :], ps[:, n % 8, 0:T], ACT.Copy).then_inc(unranked, 1)

        @block.tensor
        def _(pe):
            pe.wait_ge(lora_in, 32)
            pe.wait_ge(squashed, 3)
            for n in range(3 * HC):
                c, kind = n // 3, n % 3
                if n >= 8:
                    pe.wait_ge(unranked, n - 7)
                sums = ps[:, n % 8, 0:T]
                if kind < 2:
                    rows = slice(64 * kind, 64 * kind + 64)
                    last = nc.tensor.matmul(sums, lora[rows, P * c:P * c + P], pin[rows, C_WA, :], start=True, stop=True)
                else:
                    rows = slice(0, GATE_RANK - P)
                    nc.tensor.matmul(sums, gate_up[:, 0, P * c:P * c + P], pin[:, C_G, :], start=True, stop=False)
                    last = nc.tensor.matmul(sums, gate_up[rows, 1, P * c:P * c + P], pin[rows, C_GI, :], start=False, stop=True)
                last.then_inc(ranked, 1)

    k_squared, k_summed, k_rooted = sem("kk_squared"), sem("kk_summed"), sem("kk_rooted")
    bonus_ready, bonus_summed = sem("bonus_ready"), sem("bonus_summed")
    cum_ready, before_ready, exp_ready, taken = sem("cum_ready"), sem("before_ready"), sem("exp_ready"), sem("exp_taken")
    order = Order(sem("prepare_order"))
    r, k, v = pin[:, C_R:C_R + HC, :], pin[:, C_K:C_K + HC, :], pin[:, C_V:C_V + HC, :]
    sums = ps[:, 0:4, :].rearrange("p b (c t) -> p (b c) t", c=2)
    sums_b = ps[:, 4:8, :].rearrange("p b (c t) -> p (b c) t", c=2)

    def by_chunk(x):
        return x.rearrange("p c (n t) -> p (c n) t", t=CH)

    left_a, left_r = (left[:, :, :, i * CH:i * CH + CH].rearrange("p c n t -> p (c n) t") for i in range(2))
    right_b, right_k = (right[:, :, :, i * CH:i * CH + CH].rearrange("p c n t -> p (c n) t") for i in range(2))

    with nc.Block() as block:
        @block.vector
        def _(dve):
            order.after(dve, nc.vector.memset(kept[:, :], 1.0))
            order.mark(nc.vector.memset(kept[:, ::CH], 0.0))
            for c in range(HC):
                order.mark(nc.vector.tensor_scalar(kk[:, c, :], pin[:, C_K + c, :], par("k_k", c), None, ALU.mult))
            order.settle(dve)
            order.after(dve, nc.vector.tensor_tensor(t1[:, :, :], kk[:, :, :], kk[:, :, :], ALU.mult))
            dve.sem_inc(k_squared, 1)
            for c in range(HC):
                order.mark(nc.vector.tensor_scalar(t2[:, c, :], icl[:, c, :], -1.0, par("k_a", c), ALU.add, ALU.mult))
            order.settle(dve)
            order.after(dve, nc.vector.scalar_tensor_tensor(k, t2[:, :, :], 1.0, k, ALU.add, ALU.mult))
            for c in range(HC):
                order.mark(nc.vector.scalar_tensor_tensor(t2[:, c, :], pin[:, C_R + c, :], par("r_k", c), pin[:, C_K + c, :], ALU.mult, ALU.mult))
            order.settle(dve)
            dve.sem_inc(bonus_ready, 1)
            dve.wait_ge(k_rooted, 1)
            order.after(dve, nc.vector.tensor_scalar(t1[:, :, :], t1[:, :, :], 1e-12, None, ALU.max))
            order.after(dve, nc.vector.reciprocal(t1[:, :, :], t1[:, :, :]))
            order.after(dve, nc.vector.tensor_tensor(kk[:, :, :], kk[:, :, :], t1[:, :, :], ALU.mult))
            dve.wait_ge(bonus_summed, 1)
            order.mark(nc.vector.tensor_tensor(bonus[:, :, :], sums_b, v, ALU.mult))
            order.after(dve, nc.vector.tensor_scalar(log_decay[:, :, :], log_decay[:, :, :], -EXP_HALF, None, ALU.mult))
            for c in range(HC):
                order.mark(nc.vector.tensor_tensor_scan(t1[:, c, :], kept[:, :], log_decay[:, c, :], 0.0, ALU.mult, ALU.add))
            order.settle(dve)
            order.after(dve, nc.vector.tensor_tensor(t2[:, :, :], t1[:, :, :], log_decay[:, :, :], ALU.subtract))
            dve.sem_inc(cum_ready, 1)
            dve.wait_ge(exp_ready, 1)
            order.after(dve, nc.vector.scalar_tensor_tensor(left_a, by_chunk(kk[:, :, :]), -1.0, by_chunk(t2[:, :, :]), ALU.mult, ALU.mult))
            order.after(dve, nc.vector.tensor_tensor(kk[:, :, :], kk[:, :, :], icl[:, :, :], ALU.mult))
            dve.wait_ge(exp_ready, 2)
            order.mark(nc.vector.tensor_tensor(right_b, by_chunk(kk[:, :, :]), by_chunk(log_decay[:, :, :]), ALU.mult))
            order.mark(nc.vector.tensor_tensor(right_k, by_chunk(k), by_chunk(log_decay[:, :, :]), ALU.mult))
            dve.wait_ge(exp_ready, 3)
            order.mark(nc.vector.tensor_tensor(left_r, by_chunk(r), by_chunk(t1[:, :, :]), ALU.mult))
            order.mark(nc.vector.tensor_copy(chunk_decay[:, :, :], t1[:, :, CH - 1::CH]))

        @block.tensor
        def _(pe):
            pe.wait_ge(k_squared, 1)
            for c in range(HC):
                last = nc.tensor.matmul(sums[:, c, :], cst("heads"), t1[:, c, :], start=True, stop=True)
            last.then_inc(k_summed, 1)
            pe.wait_ge(bonus_ready, 1)
            for c in range(HC):
                last = nc.tensor.matmul(sums_b[:, c, :], cst("heads"), t2[:, c, :], start=True, stop=True)
            last.then_inc(bonus_summed, 1)

        @block.scalar
        def _(act):
            act.wait_ge(k_summed, 1)
            nc.scalar.activation(t1[:, :, :], sums, ACT.Sqrt).then_inc(k_rooted, 1)
            act.wait_ge(cum_ready, 1)
            nc.scalar.activation(t2[:, :, :], t2[:, :, :], ACT.Exp).then_inc(exp_ready, 1)
            nc.scalar.activation(log_decay[:, :, :], t1[:, :, :], ACT.Exp, scale=-1.0).then_inc(exp_ready, 1)
            act.wait_ge(exp_ready, 2)
            nc.scalar.activation(t1[:, :, :], t1[:, :, :], ACT.Exp).then_inc(exp_ready, 1)


def solve_corrections(pin, left, right, pairs, *, nc, sem, sbuf, cst, ps, scratch):
    space = pin[:, C_Q:C_Q + 12, :].rearrange("p c t -> p (c t)")
    low, inverse, tmp = (space[:, CH * CH * i:CH * CH * (i + 1)].rearrange("p (j t) -> p j t", j=CH) for i in range(3))
    paired, masked = sem("paired"), sem("masked")
    out1, in1, out2, in2 = sem("low_out"), sem("low_in"), sem("inverse_out"), sem("inverse_in")
    solved = sem("solved")
    order = Order(sem("solve_order"))
    with nc.Block() as block:
        @block.tensor
        def _(pe):
            for n in range(NCH):
                for e in range(2):
                    rows = slice(64 * e, 64 * e + 64)
                    bank = (2 * n + e) % 8
                    if 2 * n + e >= 8:
                        pe.wait_ge(masked, 2 * n + e - 7)
                    for c in range(HC):
                        last = nc.tensor.matmul(ps[0:64, bank, 64 * c:64 * c + 64], right[rows, c, n, :], left[rows, c, n, :],
                                                start=True, stop=True)
                    last.then_inc(paired, 1)

        @block.vector
        def _(dve):
            mask = cst("decay_mask")[0:64, :].unsqueeze(1).to_broadcast([64, HC, 2 * CH])
            order.mark(nc.vector.memset(inverse, 0.0))
            for n in range(2 * NCH):
                dve.wait_ge(paired, n + 1)
                nc.vector.tensor_tensor(pairs[:, n // 2, n % 2, :, :], ps[0:64, n % 8, :].rearrange("p (c t) -> p c t", c=HC), mask,
                                        ALU.mult).then_inc(masked, 1)
            order.settle(dve)
            order.after(dve, nc.vector.memset(space[:, CH * CH:2 * CH * CH:CH + 1], 1.0))
            dve.wait_ge(in1, 16)
            for t in range(1, CH):
                by_s = low[:, 0:t, t].unsqueeze(1).to_broadcast([P, t, t])
                order.after(dve, nc.vector.tensor_tensor(tmp[:, 0:t, 0:t], inverse[:, 0:t, 0:t], by_s, ALU.mult))
                order.after(dve, nc.vector.tensor_reduce(inverse[:, 0:t, t], tmp[:, 0:t, 0:t], AX, ALU.add))
            dve.sem_inc(solved, 1)

        @block.sync
        def _(sp):
            sp.wait_ge(masked, 2 * NCH)
            block_ab = pairs[0:CH, :, :, :, 0:CH].rearrange("j n e c t -> j (n e c) t")
            sp.dma_start(scratch["solve_in"].rearrange("m j t -> j m t"), block_ab).then_inc(out1, 16)
            sp.wait_ge(out1, 16)
            sp.dma_start(low, scratch["solve_in"]).then_inc(in1, 16)
            sp.wait_ge(solved, 1)
            sp.dma_start(scratch["solve_out"], inverse).then_inc(out2, 16)
            sp.wait_ge(out2, 16)
            sp.dma_start(block_ab, scratch["solve_out"].rearrange("m j t -> j m t")).then_inc(in2, 16)
            sp.wait_ge(in2, 16)


def recur(pin, left, right, pairs, chunk_decay, y, *, nc, sem, sbuf, cst, ps):
    flat = pin[:, :, :].rearrange("p c t -> p (c t)")
    W = H * HD
    sv = pin[0:2 * CH, 0:8, :].rearrange("p (b c) t -> p b (c t)", b=2)
    wt = pin[0:2 * CH, 8:16, :].rearrange("p (b c) t -> p b (c t)", b=2)
    rhs = pin[0:CH, C_Q:C_Q + 4, :].rearrange("p c t -> p (c t)")
    states = [pin[:, at:at + 4, :].rearrange("p c t -> p (c t)").rearrange("p (c e v) -> p c e v", c=HC, e=2) for at in (C_Q + 4, C_Q + 8)]
    v_bank, w_bank = ps[0:64, 0:2, :].rearrange("p b t -> p (b t)"), ps[0:64, 2:4, :].rearrange("p b t -> p (b t)")
    x_bank = ps[:, 4:6, :].rearrange("p b t -> p (b t)")
    s_bank = ps[:, 6:8, :].rearrange("p b t -> p (b t)")
    v_turned, w_turned = sem("v_turned"), sem("w_turned")
    v_copied, w_copied, cleared = sem("v_copied"), sem("w_copied"), sem("corrections_cleared")
    x_made, x_copied, s_made, s_copied = sem("rhs_made"), sem("rhs_copied"), sem("corrections_made"), sem("corrections_copied")
    st_made, st_added, st_done, y_made, y_copied = sem("state_made"), sem("state_added"), sem("state_done"), sem("y_made"), sem("y_copied")
    with nc.Block() as block:
        @block.tensor
        def _(pe):
            def turn_v(n):
                if n >= 1:
                    pe.wait_ge(v_copied, n)
                for c in range(HC):
                    at = (C_V + c) * T + CH * (n - 1)
                    last = nc.tensor.transpose(v_bank[:, P * c:P * c + P], flat[:, at:at + 2 * CH], cst("ident"))
                last.then_inc(v_turned, 1)

            def turn_w(n):
                if n >= 1:
                    pe.wait_ge(w_copied, n)
                for c in range(HC):
                    last = nc.tensor.transpose(w_bank[:, P * c:P * c + P], right[:, c, n, :], cst("ident"))
                last.then_inc(w_turned, 1)

            turn_v(0)
            turn_w(0)
            for n in range(NCH):
                b = n % 2
                state = states[b]
                pe.wait_ge(v_copied, n + 1)
                pe.wait_ge(cleared, n + 1)
                pe.wait_ge(st_done, 2 * n + 1)
                for c in range(HC):
                    nc.tensor.matmul(x_bank[0:CH, P * c:P * c + P], left[:, c, n, 0:CH],
                                     state[:, c, :, :].rearrange("p e v -> p (e v)"), start=(c % 4 == 0), stop=True, skip_group_check=(c % 4 > 0))
                for c in range(HC):
                    for e in range(2):
                        at = P * c + HD * e
                        last = nc.tensor.matmul(x_bank[0:CH, at:at + HD], pairs[:, n, e, c, 0:CH], sv[:, b, at:at + HD],
                                                start=False, stop=True, skip_group_check=True)
                last.then_inc(x_made, 1)
                if n + 1 < NCH:
                    turn_v(n + 1)
                pe.wait_ge(x_copied, n + 1)
                if n >= 1:
                    pe.wait_ge(y_copied, n)
                for c in range(HC):
                    for e in range(2):
                        at = P * c + HD * e
                        last = nc.tensor.matmul(s_bank[0:CH, at:at + HD], pairs[0:CH, n, e, c, 0:CH], rhs[:, at:at + HD],
                                                start=True, stop=True)
                last.then_inc(s_made, 1)
                if n + 1 < NCH:
                    turn_w(n + 1)
                pe.wait_ge(s_copied, n + 1)
                if n + 1 < NCH:
                    for c in range(HC):
                        last = nc.tensor.matmul(x_bank[:, P * c:P * c + P], wt[:, b, P * c:P * c + P], sv[:, b, P * c:P * c + P],
                                                start=True, stop=True)
                    last.then_inc(st_made, 1)
                for c in range(HC):
                    nc.tensor.matmul(s_bank[:, CH * c:CH * c + CH], state[:, c, :, :].rearrange("p e v -> p (e v)"), left[:, c, n, CH:2 * CH],
                                     start=(c == 0), stop=True, skip_group_check=(c > 0))
                for c in range(HC):
                    for e in range(2):
                        at = P * c + HD * e
                        last = nc.tensor.matmul(s_bank[64 * e:64 * e + 64, CH * c:CH * c + CH], sv[:, b, at:at + HD],
                                                pairs[:, n, e, c, CH:2 * CH], start=False, stop=True, skip_group_check=True)
                last.then_inc(y_made, 1)

        @block.scalar
        def _(act):
            def take_v(n):
                act.wait_ge(v_turned, n + 1)
                if n >= 2:
                    act.wait_ge(y_made, n - 1)
                nc.scalar.activation(sv[CH:2 * CH, n % 2, :], v_bank[CH:2 * CH, :], ACT.Copy).then_inc(v_copied, 1)

            take_v(0)
            for n in range(NCH):
                act.wait_ge(x_made, n + 1)
                if n >= 1:
                    act.wait_ge(s_made, n)
                nc.scalar.activation(rhs, x_bank[0:CH, :], ACT.Copy).then_inc(x_copied, 1)
                if n + 1 < NCH:
                    take_v(n + 1)
                act.wait_ge(y_made, n + 1)
                nc.scalar.activation(y[:, :, CH * n:CH * n + CH], s_bank[:, 0:HC * CH].rearrange("p (c t) -> p c t", c=HC),
                                     ACT.Copy).then_inc(y_copied, 1)

        @block.vector
        def _(dve):
            def clear(n):
                if n >= 2:
                    dve.wait_ge(y_made, n - 1)
                nc.vector.memset(sv[0:CH, n % 2, :], 0.0).then_inc(cleared, 1)

            def take_w(n):
                dve.wait_ge(w_turned, n + 1)
                nc.vector.tensor_copy(wt[:, n % 2, :], w_bank).then_inc(w_copied, 1)

            nc.vector.memset(pin[:, C_Q + 4:C_Q + 12, :], 0.0).then_inc(st_done, 1)
            clear(0)
            take_w(0)
            for n in range(NCH):
                if n + 1 < NCH:
                    clear(n + 1)
                dve.wait_ge(s_made, n + 1)
                dve.wait_ge(cleared, n + 1)
                nc.vector.tensor_copy(sv[0:CH, n % 2, :], s_bank[0:CH, :]).then_inc(s_copied, 1)
                if n + 1 < NCH:
                    take_w(n + 1)
                    dve.wait_ge(st_made, n + 1)
                    if n >= 1:
                        dve.wait_ge(st_done, 2 * n + 1)
                        dve.wait_ge(y_made, n)
                    for e in range(2):
                        rows = slice(64 * e, 64 * e + 64)
                        add = x_bank[rows, :].rearrange("p (c e v) -> p c e v", c=HC, e=2)[:, :, e, :]
                        nc.vector.tensor_tensor(states[(n + 1) % 2][rows, :, e, :], states[n % 2][rows, :, e, :], add, ALU.add).then_inc(st_added, 1)
                    dve.wait_ge(st_added, 2 * n + 2)
                    for e in range(2):
                        rows = slice(64 * e, 64 * e + 64)
                        to = states[(n + 1) % 2][rows, :, e, :]
                        nc.vector.tensor_tensor(to, to, chunk_decay[rows, :, n].unsqueeze(2).to_broadcast([64, HC, HD]),
                                                ALU.mult).then_inc(st_done, 1)


def center_heads(y, rms, *, nc, sem, cst, ps, prefetch):
    meaned, centered, squared, summed = sem("y_meaned"), sem("y_centered"), sem("y_squared"), sem("y_summed")
    means = ps[:, 0:4, :].rearrange("p b (c t) -> p (b c) t", c=2)
    sums = ps[:, 4:8, :].rearrange("p b (c t) -> p (b c) t", c=2)
    with nc.Block() as block:
        @block.sync
        def _(sp):
            prefetch(sp)

        @block.tensor
        def _(pe):
            for c in range(HC):
                last = nc.tensor.matmul(means[:, c, :], cst("heads"), y[:, c, :], start=True, stop=True)
            last.then_inc(meaned, 1)
            pe.wait_ge(squared, 1)
            for c in range(HC):
                last = nc.tensor.matmul(sums[:, c, :], cst("heads"), rms[:, c, :], start=True, stop=True)
            last.then_inc(summed, 1)

        @block.scalar
        def _(act):
            act.wait_ge(summed, 1)
            nc.scalar.activation(rms[:, :, :], sums, ACT.Sqrt, bias=cst("eps_gn"), scale=1.0 / HD)

        @block.vector
        def _(dve):
            dve.wait_ge(meaned, 1)
            nc.vector.scalar_tensor_tensor(y[:, :, :], means, -1.0 / HD, y[:, :, :], ALU.mult, ALU.add).then_inc(centered, 1)
            dve.wait_ge(centered, 1)
            nc.vector.tensor_tensor(rms[:, :, :], y[:, :, :], y[:, :, :], ALU.mult).then_inc(squared, 1)


def mix_branches(gates, mixed, xn, y_rwkv, y_dsa, gate, bonus, rms, *, nc, d, sem, par_at, cst, ring, ps, **_):
    STEPS = 5
    gated, x_in, finished = sem("branch_gated"), sem("x_again"), sem("rwkv_finished")
    first_part = ring.parts
    center_heads(y_rwkv, rms, nc=nc, sem=sem, cst=cst, ps=ps, prefetch=lambda sp: ring.prefetch(sp, d["w_gates"], ring.parts))

    def finish(dve, c):
        V = nc.vector
        y, dev, b, g = (a[:, bass.ds(c, 1), :] for a in (y_rwkv, rms, bonus, gate))
        V.reciprocal(dev, dev).then_inc(finished, 1)
        dve.wait_ge(finished, STEPS * c + 1)
        V.tensor_tensor(y, y, dev, ALU.mult).then_inc(finished, 1)
        dve.wait_ge(finished, STEPS * c + 2)
        V.tensor_scalar(y, y, par_at("ln_x_w", c), par_at("ln_x_b", c), ALU.mult, ALU.add).then_inc(finished, 1)
        dve.wait_ge(finished, STEPS * c + 3)
        V.tensor_tensor(y, y, b, ALU.add).then_inc(finished, 1)
        dve.wait_ge(finished, STEPS * c + 4)
        V.tensor_tensor(y, y, g, ALU.mult).then_inc(finished, 1)

    def finish_next(dve, g, sums, half, before):
        if isinstance(g, int) and g == 2 * DC // 4 - 1:
            return
        if isinstance(g, int) and g == 0:
            finish(dve, 0)
        finish(dve, g + 1)

    def to_gates(act, g, sums, half, before):
        nc.scalar.activation(gates[:, bass.ds(4 * g, 4), :], sums, ACT.Sigmoid).then_inc(ring.evacuated, 1)

    def first(dve, g, sums, half, before):
        dve.wait_ge(ring.evacuated, before)
        nc.vector.tensor_tensor(mixed[:, bass.ds(4 * g, 4), :], sums, gates[:, bass.ds(4 * g, 4), :], ALU.mult).then_inc(ring.evacuated, 1)

    def second(dve, g, sums, half, before):
        b = gates[:, bass.ds(DC + 4 * g, 4), :]
        nc.vector.tensor_tensor(b, sums, b, ALU.mult).then_inc(ring.evacuated, 1)
        dve.wait_ge(ring.evacuated, before + 1)
        m = mixed[:, bass.ds(4 * g, 4), :]
        nc.vector.tensor_tensor(m, m, b, ALU.add).then_inc(gated, 1)

    def x_again(sp):
        sp.wait_ge(ring.split, first_part + DC // 4)
        sp.dma_start(xn[:, :, :], d["x"]).then_inc(x_in, 16)

    def add(dve, g, sums, half, before):
        dve.wait_ge(x_in, 16)
        to = xn[:, bass.ds(4 * g, 4), :]
        nc.vector.tensor_tensor(to, sums, to, ALU.add).then_inc(ring.evacuated, 1)

    linear(nc, ring, ps, [
        Product(d["w_gates"], 2 * DC, xn, dict(scalar=to_gates, vector=finish_next)),
        Product(d["w_branch_rwkv"], DC, y_rwkv, dict(vector=first), ready=(finished, 4 * STEPS), alongside=x_again),
        Product(d["w_branch_dsa"], DC, y_dsa, dict(vector=second)),
        Product(d["w_out"], DC, mixed, dict(vector=add), ready=(gated, 1))])


def peer(h, x1, *, nc, d, sem, sbuf, par, par_at, cst, ps, ring, **_):
    with ExitStack() as scope:
        h_tok = sbuf(scope, "h_tok", [TT, D])
        tmp = sbuf(scope, "ffn_rms", [T])
        partial = sbuf(scope, "partial", [TT, D])
        hn = partial[:, :, :].rearrange("p i (c t) -> p (i c) t", t=T)
        rmsnorm(nc, sem, cst, ps, h[:, :, :], hn, par("norm_ffn", 0, DC), tmp[:, :], DC, "eps_rms",
                lambda sp: ring.prefetch(sp, d["w_query"], ring.parts))
        product = sbuf(scope, "product", [D])
        keys = product[:, :].rearrange("p (s n) -> p s n", n=PK_KEYS)
        keys_in = sem("keys_in")
        linear(nc, ring, ps, [Product(d["w_query"], DC, hn, dict(scalar=copy_out(nc, ring, x1)),
                                      alongside=lambda sp: sp.dma_start(keys, d["sub_keys"]).then_inc(keys_in, 16))])
        experts(h, x1, hn, h_tok, partial, product, keys, keys_in, nc=nc, d=d, sem=sem, sbuf=sbuf, cst=cst, ps=ps)
        rmsnorm(nc, sem, cst, ps, h[:, :, :], x1[:, :, :], par("norm_final", 0, DC), tmp[:, :], DC, "eps_rms",
                lambda sp: ring.prefetch(sp, d["a_w_z"], ring.parts))


def experts(h, query, hn, h_tok, partial, product, keys, keys_in, *, nc, d, sem, sbuf, cst, ps):
    S = 2 * PK_HEADS
    K = PK_TOP
    SLOTS = 8
    BY_VECTOR = (3, 7)
    BY_TENSOR = [s for s in range(SLOTS) if s not in BY_VECTOR]
    TURNS = PK_SEL // SLOTS
    with ExitStack() as scope:
        expert = sbuf(scope, "expert", [TT, PK_SEL], U32)
        weight = sbuf(scope, "weight", [TT, PK_SEL])
        score = sbuf(scope, "key_score", [S, PK_KEYS])
        rest = sbuf(scope, "key_rest", [S, PK_KEYS])
        best = sbuf(scope, "best", [S, K])
        best_at = sbuf(scope, "best_at", [S, K], U32)
        best_f = sbuf(scope, "best_f", [S, K])
        cand = score[:, :, :].rearrange("p (h s) n -> p h (s n)", h=PK_HEADS)
        cand_rest = rest[:, :, :].rearrange("p (h s) n -> p h (s n)", h=PK_HEADS)
        top = sbuf(scope, "top_sum", [PK_HEADS, K])
        top_at = sbuf(scope, "top_sum_at", [PK_HEADS, K], U32)
        place = sbuf(scope, "place", [2, PK_HEADS, K], U32)
        place_f = sbuf(scope, "place_f", [2, PK_HEADS, K])
        half_id = sbuf(scope, "half_id", [2, PK_HEADS, K])
        total = sbuf(scope, "gate_total", [PK_HEADS])
        row = sbuf(scope, "row", [SLOTS, D])
        index = sbuf(scope, "index", [SLOTS], U32)
        dot = sbuf(scope, "dot", [2, SLOTS])
        act_in = sbuf(scope, "act_in", [TT, PK_SEL])
        diag = sbuf(scope, "diag", [SLOTS, P])
        zero = sbuf(scope, "zero", [P])
        turned, h_copied = sem("h_turned"), sem("h_copied")
        scored, s_copied, searched = sem("keys_scored"), sem("keys_copied"), sem("tile_searched")
        shifted, exped, chosen = sem("gate_shifted"), sem("gate_exped"), sem("tile_chosen")
        order = Order(sem("choose_order"))
        index_set = sem("index_set")
        index_seen = sem("index_seen")
        arrived = [sem(f"row_arrived{s}") for s in range(SLOTS)]
        row_free = [sem(f"row_free{s}") for s in range(SLOTS)]
        diag_ready = [sem(f"diag_ready{s}") for s in range(SLOTS)]
        collected, gelued, weighted, zeroed = sem("collected"), sem("gelued"), sem("weighted"), sem("zeroed")
        summed, sum_copied, turned_back = sem("experts_summed"), sem("sum_copied"), sem("turned_back")
        partial_added, sum_whole = sem("partial_added"), sem("sum_whole")

        def top16(dve, jobs):
            V = nc.vector
            for x, _, v, _ in jobs:
                order.mark(V.max(v[:, 0:8], x))
            order.settle(dve)
            for x, r, v, at in jobs:
                order.mark(V.max_index(at[:, 0:8], v[:, 0:8], x))
                order.mark(V.match_replace(r, v[:, 0:8], x, TAKEN))
            order.settle(dve)
            for _, r, v, _ in jobs:
                order.mark(V.max(v[:, 8:16], r))
            order.settle(dve)
            for _, r, v, at in jobs:
                order.mark(V.max_index(at[:, 8:16], v[:, 8:16], r))
            order.settle(dve)

        def search_keys(dve, i, half):
            dve.wait_ge(s_copied, i + 1)
            top16(dve, [(score[:, s, :], rest[:, s, :], best[:, s, :], best_at[:, s, :]) for s in range(S // 2 * half, S // 2 * half + S // 2)])

        def search_sums(dve, i):
            V = nc.vector
            order.mark(V.tensor_copy(best_f[:, :, :], best_at[:, :, :]))
            order.after(dve, V.tensor_tensor(cand.rearrange("p h (a b) -> p h a b", a=K),
                                             best[:, 0::2, :].unsqueeze(3).to_broadcast([P, PK_HEADS, K, K]),
                                             best[:, 1::2, :].unsqueeze(2).to_broadcast([P, PK_HEADS, K, K]), ALU.add))
            top16(dve, [(cand[:, h, :], cand_rest[:, h, :], top[:, h, :], top_at[:, h, :]) for h in range(PK_HEADS)])
            dve.sem_inc(searched, 1)

        def take_experts(dve, i):
            V = nc.vector
            wide = [P, PK_HEADS, K, K]
            hot = rest[:, :, :].rearrange("p (h s) (a b) -> p h (s a) b", h=PK_HEADS, b=K)
            w = weight[:, i, :].rearrange("p (h k) -> p h k", h=PK_HEADS)
            V.tensor_tensor(w, top[:, :, :], top[:, :, 0:1].to_broadcast([P, PK_HEADS, K]), ALU.subtract).then_inc(shifted, 1)
            order.mark(V.tensor_scalar(place[:, 0, :, :], top_at[:, :, :], 4, None, ALU.logical_shift_right))
            order.mark(V.tensor_scalar(place[:, 1, :, :], top_at[:, :, :], 15, None, ALU.bitwise_and))
            order.settle(dve)
            order.after(dve, V.tensor_copy(place_f[:, :, :, :], place[:, :, :, :]))
            for half in range(2):
                order.after(dve, V.tensor_tensor(hot, place_f[:, half, :, :].unsqueeze(3).to_broadcast(wide),
                                                 cst("iota").unsqueeze(1).unsqueeze(1).to_broadcast(wide), ALU.is_equal))
                order.after(dve, V.tensor_tensor(hot, hot, best_f[:, half::2, :].unsqueeze(2).to_broadcast(wide), ALU.mult))
                order.after(dve, V.tensor_reduce(half_id[:, half, :, :], hot, AX, ALU.add))
            e = half_id[:, 0, :, :]
            order.after(dve, V.scalar_tensor_tensor(e, e, float(PK_KEYS), half_id[:, 1, :, :], ALU.mult, ALU.add))
            V.tensor_copy(expert[:, i, :].rearrange("p (h k) -> p h k", h=PK_HEADS), e).then_inc(chosen, 1)
            dve.wait_ge(exped, i + 1)
            order.after(dve, V.tensor_reduce(total[:, :], w, AX, ALU.add))
            order.after(dve, V.reciprocal(total[:, :], total[:, :]))
            order.after(dve, V.tensor_tensor(w, w, total[:, :].unsqueeze(2).to_broadcast([P, PK_HEADS, K]), ALU.mult))

        def dot_rows(dve, i, t):
            V = nc.vector
            at = TURNS * i + t
            for s in range(SLOTS):
                dve.wait_ge(arrived[s], 16 * at + 16)
                V.tensor_tensor_reduce(product[:, :], row[:, s, :], h_tok[:, i, :], 1.0, 0.0, ALU.mult, ALU.add,
                                       dot[:, 0, s:s + 1]).then_inc(row_free[s], 1)
                dve.wait_ge(row_free[s], at + 2)
            V.tensor_copy(act_in[:, i, bass.ds(SLOTS * t, SLOTS)], dot[:, 0, :]).then_inc(collected, 1)
            dve.wait_ge(collected, at + 1)

        with nc.Block() as block:
            @block.gpsimd
            def _(pool):
                for i in range(2 * TT):
                    table = d["peer_u"] if i < TT else d["peer_v"]
                    if i < TT:
                        pool.wait_ge(chosen, i + 1)
                    with pool.Fori(0, TURNS) as t:
                        for s in range(SLOTS):
                            at = TURNS * i + t
                            pool.wait_ge(row_free[s], at + 1)
                            nc.gpsimd.tensor_copy(index[:, s:s + 1], expert[:, i % TT, bass.ds(SLOTS * t + s, 1)]).then_inc(index_set, 1)
                            pool.wait_ge(index_set, SLOTS * at + s + 1)
                            pool.sem_inc(index_seen, 1)
                            nc.gpsimd.indirect_dma_start(row[:, s, :], None, table, bass.IndirectOffsetOnAxis(ap=index[:, s:s + 1], axis=0)).then_inc(arrived[s], 16)

            @block.vector
            def _(dve):
                V = nc.vector
                V.memset(zero[:, :], 0.0).then_inc(zeroed, 1)
                for s in range(SLOTS):
                    dve.sem_inc(row_free[s], 1)
                for half in range(2):
                    search_keys(dve, 0, half)
                search_sums(dve, 0)
                take_experts(dve, 0)
                search_keys(dve, 1, 0)
                dve.wait_ge(h_copied, TT)
                dve.wait_ge(scored, TT)
                with dve.Fori(0, 2) as t:
                    dot_rows(dve, 0, t)
                search_keys(dve, 1, 1)
                with dve.Fori(2, 4) as t:
                    dot_rows(dve, 0, t)
                search_sums(dve, 1)
                with dve.Fori(4, 6) as t:
                    dot_rows(dve, 0, t)
                take_experts(dve, 1)
                V.memset(partial[:, :, :], 0.0).then_inc(partial_added, 1)
                with dve.Fori(6, TURNS) as t:
                    dot_rows(dve, 0, t)
                with dve.Fori(0, TURNS) as t:
                    dot_rows(dve, 1, t)
                for i in range(TT):
                    dve.wait_ge(gelued, i + 1)
                    V.tensor_tensor(weight[:, i, :], weight[:, i, :], act_in[:, i, :], ALU.mult).then_inc(weighted, 1)
                dve.wait_ge(weighted, TT)
                for i in range(TT):
                    with dve.Fori(0, TURNS) as t:
                        at = TURNS * i + t
                        for s in BY_TENSOR:
                            dve.wait_ge(row_free[s], TT * TURNS + at + 1)
                            V.tensor_scalar(diag[:, s, :], cst("ident"), weight[:, i, bass.ds(SLOTS * t + s, 1)], None, ALU.mult).then_inc(diag_ready[s], 1)
                        for n, s in enumerate(BY_VECTOR):
                            dve.wait_ge(arrived[s], 16 * (TT * TURNS + at) + 16)
                            dve.wait_ge(partial_added, len(BY_VECTOR) * at + n + 1)
                            V.scalar_tensor_tensor(partial[:, i, :], row[:, s, :], weight[:, i, bass.ds(SLOTS * t + s, 1)], partial[:, i, :],
                                                   ALU.mult, ALU.add).then_inc(partial_added, 1)
                            dve.wait_ge(partial_added, len(BY_VECTOR) * at + n + 2)
                            dve.sem_inc(row_free[s], 1)
                for i in range(TT):
                    dve.wait_ge(sum_copied, i + 1)
                    V.tensor_tensor(h_tok[:, i, :], h_tok[:, i, :], partial[:, i, :], ALU.add).then_inc(sum_whole, 1)
                for i in range(TT):
                    for q in range(4):
                        dve.wait_ge(turned_back, 4 * i + q + 1)
                        to = h[:, 4 * q:4 * q + 4, P * i:P * i + P]
                        V.tensor_tensor(to, to, ps[:, 4 * i + q, :].rearrange("p (c t) -> p c t", c=4), ALU.add)

            @block.scalar
            def _(act):
                for i in range(TT):
                    act.wait_ge(scored, i + 1)
                    if i:
                        act.wait_ge(searched, i)
                    nc.scalar.activation(score[:, :, :], ps[:, 0:4, :].rearrange("p b (s n) -> p (b s) n", s=4), ACT.Copy).then_inc(s_copied, 1)
                    act.wait_ge(turned, i + 1)
                    nc.scalar.activation(h_tok[:, i, :], ps[:, 4:8, :].rearrange("p b n -> p (b n)"), ACT.Copy).then_inc(h_copied, 1)
                    act.wait_ge(shifted, i + 1)
                    w = weight[:, i, :]
                    nc.scalar.activation(w, w, ACT.Exp).then_inc(exped, 1)
                for i in range(TT):
                    act.wait_ge(collected, TURNS * (i + 1))
                    nc.scalar.activation(act_in[:, i, :], act_in[:, i, :], ACT.Gelu).then_inc(gelued, 1)
                for i in range(TT):
                    act.wait_ge(summed, i + 1)
                    nc.scalar.activation(h_tok[:, i, :], ps[:, 4 * i:4 * i + 4, :].rearrange("p b n -> p (b n)"), ACT.Copy).then_inc(sum_copied, 1)

            @block.tensor
            def _(pe):
                pe.wait_ge(keys_in, 16)
                for i in range(TT):
                    if i:
                        pe.wait_ge(s_copied, i)
                    for s in range(S):
                        last = nc.tensor.matmul(ps[:, s // 4, PK_KEYS * (s % 4):PK_KEYS * (s % 4) + PK_KEYS],
                                                query[:, s, P * i:P * i + P], keys[:, s, :], start=True, stop=True)
                    last.then_inc(scored, 1)
                    if i:
                        pe.wait_ge(h_copied, i)
                    for c in range(DC):
                        last = nc.tensor.transpose(ps[:, 4 + c // 4, P * (c % 4):P * (c % 4) + P], hn[:, c, P * i:P * i + P], cst("ident"))
                    last.then_inc(turned, 1)
                pe.wait_ge(zeroed, 1)
                pe.wait_ge(s_copied, TT)
                pe.wait_ge(h_copied, TT)
                for i in range(TT):
                    for q in range(4):
                        nc.tensor.matmul(ps[:, 4 * i + q, :], zero[:, :], h_tok[:, i, 512 * q:512 * q + 512],
                                         start=True, stop=False)
                    with pe.Fori(0, TURNS) as t:
                        at = TURNS * i + t
                        for s in BY_TENSOR:
                            pe.wait_ge(arrived[s], 16 * (TT * TURNS + at) + 16)
                            pe.wait_ge(diag_ready[s], at + 1)
                            for q in range(4):
                                last = nc.tensor.matmul(ps[:, 4 * i + q, :], diag[:, s, :], row[:, s, 512 * q:512 * q + 512],
                                                        start=False, stop=False)
                            last.then_inc(row_free[s], 1)
                    for q in range(4):
                        last = nc.tensor.matmul(ps[:, 4 * i + q, :], zero[:, :], h_tok[:, i, 512 * q:512 * q + 512], start=False, stop=True)
                    last.then_inc(summed, 1)
                for i in range(TT):
                    pe.wait_ge(sum_whole, i + 1)
                    for q in range(4):
                        for c in range(4):
                            at = P * (4 * q + c)
                            last = nc.tensor.transpose(ps[:, 4 * i + q, P * c:P * c + P], h_tok[:, i, at:at + P], cst("ident"))
                        last.then_inc(turned_back, 1)


def mamba(x1, x2, z, xbc, recycle, *, nc, d, sem, sbuf, par, par_at, cst, ps, ring, **_):
    with ExitStack() as scope:
        w = d["a_w_out"]
        dt = sbuf(scope, "dt", [2, T])
        with ExitStack() as inner:
            project_mamba(inner, x1, z, xbc, dt, nc=nc, d=d, sem=sem, sbuf=sbuf, par=par, par_at=par_at, cst=cst, ps=ps, ring=ring)
        with ExitStack() as inner:
            ssd(inner, xbc, dt, nc=nc, sem=sem, sbuf=sbuf, par=par, cst=cst, ps=ps)
        with ExitStack() as inner:
            gate_groups(inner, xbc, z, nc=nc, sem=sem, sbuf=sbuf, par=par, cst=cst, ps=ps,
                        prefetch=lambda sp: ring.prefetch(sp, w[:, :, 0:ZC // 2, :], ring.parts))

        def add(dve, g, sums, half, before):
            nc.vector.scalar_tensor_tensor(x2[:, bass.ds(4 * g, 4), :], x1[:, bass.ds(4 * g, 4), :], ALPHA, sums,
                                           ALU.mult, ALU.add).then_inc(ring.evacuated, 1)

        def add_more(dve, g, sums, half, before):
            dve.wait_ge(ring.evacuated, before)
            to = x2[:, bass.ds(4 * g, 4), :]
            nc.vector.tensor_tensor(to, sums, to, ALU.add).then_inc(ring.evacuated, 1)

        linear(nc, ring, ps, [
            Product(w[:, :, 0:ZC // 2, :], DC, xbc[:, 0:ZC // 2, :], dict(vector=add)),
            Product(w[:, :, ZC // 2:ZC, :], DC, xbc[:, ZC // 2:ZC, :], dict(vector=add_more))], d["w_kv"])
    layernorm(x2, 0, nc=nc, sem=sem, sbuf=sbuf, par=par, cst=cst, ps=ps)


def layernorm(x, layer, *, nc, sem, sbuf, par, cst, ps, out=None):
    with ExitStack() as scope:
        sq = sbuf(scope, f"ln_squared{layer}", [DC, T])
        rstd = sbuf(scope, f"ln_rstd{layer}", [T])
        mean = sbuf(scope, f"ln_mean{layer}", [T])
        meaned, centered, squared, summed, rooted = (sem("ln_meaned"), sem("ln_centered"), sem("ln_squared"),
                                                     sem("ln_summed"), sem("ln_rooted"))
        scaled, shifted, stored = sem("ln_scaled"), sem("ln_shifted"), sem("stored")
        order = Order(sem("ln_order"))
        blocks = [slice(c, c + 4) for c in range(0, DC, 4)]
        with nc.Block() as block:
            if out is not None:
                @block.sync
                def _(sp):
                    for w in blocks:
                        sp.wait_ge(shifted, w.stop)
                        sp.dma_start(out[:, w, :], x[:, w, :]).then_inc(stored, 16)
                    sp.wait_ge(stored, 16 * len(blocks))

            @block.tensor
            def _(pe):
                sum_over_channels(pe, nc, cst("ones"), x, ps[:, 0, 0:T], DC).then_inc(meaned, 1)
                sum_over_channels(pe, nc, cst("ones"), sq, ps[:, 1, 0:T], DC, squared).then_inc(summed, 1)

            @block.scalar
            def _(act):
                for i, w in enumerate(blocks):
                    act.wait_ge(centered, i + 1)
                    nc.scalar.activation(sq[:, w, :], x[:, w, :], ACT.Square).then_inc(squared, 1)
                act.wait_ge(summed, 1)
                nc.scalar.activation(rstd[:, :], ps[:, 1, 0:T], ACT.Sqrt, bias=cst("eps_2"), scale=1.0 / D).then_inc(rooted, 1)
                for c in range(DC):
                    act.wait_ge(scaled, c + 1)
                    nc.scalar.activation(x[:, c, :], x[:, c, :], ACT.Identity, bias=par("ln_b", DC * layer + c)).then_inc(shifted, 1)

            @block.vector
            def _(dve):
                dve.wait_ge(meaned, 1)
                order.after(dve, nc.vector.tensor_scalar(mean[:, :], ps[:, 0, 0:T], 1.0 / D, None, ALU.mult))
                for w in blocks:
                    nc.vector.tensor_tensor(x[:, w, :], x[:, w, :], mean[:, :].unsqueeze(1).to_broadcast([P, 4, T]), ALU.subtract).then_inc(centered, 1)
                dve.wait_ge(centered, len(blocks))
                dve.wait_ge(rooted, 1)
                order.after(dve, nc.vector.reciprocal(rstd[:, :], rstd[:, :]))
                for c in range(DC):
                    nc.vector.scalar_tensor_tensor(x[:, c, :], x[:, c, :], par("ln_g", DC * layer + c), rstd[:, :],
                                                   ALU.mult, ALU.mult).then_inc(scaled, 1)


def project_mamba(scope, x1, z, xbc, dt, *, nc, d, sem, sbuf, par, par_at, cst, ps, ring):
    TAPS = 4
    raw = sbuf(scope, "conv_raw", [2, 4, TAPS - 1 + T])
    cleared = sem("conv_cleared")
    with nc.Block() as block:
        @block.vector
        def _(dve):
            nc.vector.memset(raw[:, :, :, 0:TAPS - 1], 0.0).then_inc(cleared, 1)

    def silu_z(act, g, sums, half, before):
        nc.scalar.activation(z[:, bass.ds(4 * g, 4), :], sums, ACT.Silu).then_inc(ring.evacuated, 1)

    raw_ready, tapped, activated = sem("conv_raw_ready"), sem("conv_tapped"), sem("conv_activated")

    def activate(act, g):
        act.wait_ge(tapped, TAPS * g + TAPS)
        to = xbc[:, bass.ds(4 * g, 4), :]
        nc.scalar.activation(to, to, ACT.Silu).then_inc(activated, 1)

    def evac(act, g, sums, half, before):
        nc.scalar.activation(raw[:, half, :, TAPS - 1:TAPS - 1 + T], sums, ACT.Copy).then_inc(ring.evacuated, 1)
        if not isinstance(g, int) or g > 0:
            activate(act, g - 1)

    def tap_now(dve, g, sums, half, before):
        dve.wait_ge(ring.evacuated, before + 1)
        for n in range(4):
            last = nc.vector.tensor_scalar(xbc[:, bass.ds(4 * g + n, 1), :], raw[:, half, n:n + 1, TAPS - 1:TAPS - 1 + T],
                                           par_at("conv_w", 3 * CONVC + 4 * g + n), par_at("conv_b", 4 * g + n), ALU.mult, ALU.add)
        last.then_inc(tapped, 1)

    def tap_before(dve, g, half, tap):
        dve.wait_ge(tapped, TAPS * g + tap + 1)
        for n in range(4):
            to = xbc[:, bass.ds(4 * g + n, 1), :]
            last = nc.vector.scalar_tensor_tensor(to, raw[:, half, n:n + 1, tap:tap + T], par_at("conv_w", tap * CONVC + 4 * g + n), to,
                                                  ALU.mult, ALU.add)
        last.then_inc(tapped, 1)

    def tap_first(dve, g, sums, half, before):
        tap_before(dve, g, half, 0)

    def tap_others(dve, g, sums, half, before):
        for tap in range(1, TAPS - 1):
            tap_before(dve, g, half, tap)

    def take_dt(act, g, sums, half, before):
        activate(act, CONVC // 4 - 1)
        nc.scalar.activation(dt[0:SSM_H, 0, :], sums[0:SSM_H, 0, :], ACT.Copy).then_inc(ring.evacuated, 1)

    linear(nc, ring, ps, [
        Product(d["a_w_z"], ZC, x1, dict(scalar=silu_z)),
        Product(d["a_w_conv"], CONVC, x1, dict(scalar=evac, vector=(tap_now, tap_first, tap_others))),
        Product(d["a_w_dt"], 1, x1, dict(scalar=take_dt))])


def ssd(scope, xbc, dt, *, nc, sem, sbuf, par, cst, ps):
    heads_a = GROUPS
    cum = sbuf(scope, "cum", [T])
    a = sbuf(scope, "a", [1])
    dt_tok = sbuf(scope, "dt_tok", [TT, SSM_H])
    cum_tok = sbuf(scope, "cum_tok", [TT, SSM_H])
    last_tok = sbuf(scope, "last_tok", [SSM_H])
    xdt = sbuf(scope, "xdt", [2, TT, 512])
    xst = sbuf(scope, "xst", [512])
    b_tok = sbuf(scope, "b_tok", [P])
    cb = sbuf(scope, "cb", [2, P])
    pair = sbuf(scope, "pair", [2, TT, 8, P])
    off_side = sbuf(scope, "off_side", [2, 8, P])
    state = sbuf(scope, "state", [512])
    tmp = sbuf(scope, "ssd_tmp", [T])
    order = Order(sem("ssd_order"))
    act_order = Order(sem("ssd_act_order"))
    dt_done, cum_done, dt_turned, tok_copied, last_made = (sem("dt_done"), sem("cum_done"), sem("dt_turned"), sem("tok_copied"),
                                                           sem("last_made"))
    with nc.Block() as block:
        @block.scalar
        def _(act):
            raw, d1, t = dt[0:SSM_H, 0, :], dt[0:SSM_H, 1, :], tmp[0:SSM_H, :]
            act_order.after(act, nc.scalar.activation(raw, raw, ACT.Identity, bias=par("dt_bias")[0:SSM_H]))
            act_order.after(act, nc.scalar.activation(t, raw, ACT.Abs))
            act_order.after(act, nc.scalar.activation(t, t, ACT.Exp, scale=-1.0))
            act_order.after(act, nc.scalar.activation(t, t, ACT.Ln, bias=1.0))
            act_order.after(act, nc.scalar.activation(d1, raw, ACT.Relu))
            nc.scalar.activation(a[0:SSM_H, :], par("a_log")[0:SSM_H], ACT.Exp).then_inc(dt_done, 1)

        @block.vector
        def _(dve):
            V = nc.vector
            d1, t = dt[0:SSM_H, 1, :], tmp[0:SSM_H, :]
            dve.wait_ge(dt_done, 1)
            order.after(dve, V.tensor_tensor(d1, d1, t, ALU.add))
            order.after(dve, V.tensor_scalar(t, d1, a[0:SSM_H, :], -1.0, ALU.mult, ALU.mult))
            ones = cst("ones")[0:SSM_H, :]
            for i in range(TT):
                w = slice(P * i, P * i + P)
                order.mark(V.tensor_tensor_scan(cum[0:SSM_H, w], ones, t[:, w], 0.0, ALU.mult, ALU.add))
            order.settle(dve)
            dve.sem_inc(cum_done, 1)
            dve.wait_ge(dt_turned, 1)
            order.mark(V.tensor_copy(dt_tok[:, :, :], ps[:, 0, 0:P].rearrange("p (i h) -> p i h", i=TT)))
            order.mark(V.tensor_copy(cum_tok[:, :, :], ps[:, 1, 0:P].rearrange("p (i h) -> p i h", i=TT)))
            order.settle(dve)
            dve.wait_ge(last_made, 1)
            order.mark(V.tensor_tensor(last_tok[:, :], ps[:, 2, 0:SSM_H], cum_tok[:, 0, :], ALU.subtract))
            order.settle(dve)
            dve.sem_inc(tok_copied, 1)

        @block.tensor
        def _(pe):
            pe.wait_ge(cum_done, 1)
            ident = cst("ident")[0:SSM_H, 0:SSM_H]
            for i in range(TT):
                w = slice(P * i, P * i + P)
                nc.tensor.transpose(ps[:, 0, SSM_H * i:SSM_H * i + SSM_H], dt[0:SSM_H, 1, w], ident)
                last = nc.tensor.transpose(ps[:, 1, SSM_H * i:SSM_H * i + SSM_H], cum[0:SSM_H, w], ident)
            last.then_inc(dt_turned, 1)
            nc.tensor.matmul(ps[:, 2, 0:SSM_H], cum[0:SSM_H, P - 1:P].to_broadcast([SSM_H, P]), ident, start=True, stop=True).then_inc(last_made, 1)

    with nc.Block() as block:
        @block.scalar
        def _(act):
            nc.scalar.activation(last_tok[:, :], last_tok[:, :], ACT.Exp)

    x_turned, xdt_made, xst_made, b_turned, b_copied = sem("x_turned"), sem("xdt_made"), sem("xst_made"), sem("b_turned"), sem("b_copied")
    cb_made, cb_masked, spread, differed, decayed, pair_made = (sem("cb_made"), sem("cb_masked"), sem("cum_spread"), sem("differed"),
                                                              sem("decayed"), sem("pair_made"))
    grown, off_made, state_made, state_copied = sem("grown"), sem("off_made"), sem("state_copied_p"), sem("ssm_state_copied")
    y_made, y_added = sem("ssm_y_made"), sem("ssm_y_added")
    UNITS = GROUPS * TT
    b_chunk, c_chunk = ZC, ZC + GROUPS
    masks = sbuf(scope, "causal", [P])
    masked_ready = sem("causal_ready")

    def xd(g):
        return xdt[:, g % 2, :, :]

    with nc.Block() as block:
        @block.gpsimd
        def _(pool):
            nc.gpsimd.affine_select(out=masks[:, :], in_=cst("ones"), compare_op=ALU.is_ge, fill=0.0, base=0, pattern=[[1, P]],
                                    channel_multiplier=-1).then_inc(masked_ready, 1)

        @block.tensor
        def _(pe):
            def spread_sums(g):
                if g:
                    pe.wait_ge(differed, 2 * g)
                    pe.wait_ge(grown, g)
                for i in range(TT):
                    for e in range(8):
                        h = 8 * g + e
                        last = nc.tensor.matmul(ps[:, 4 + 2 * i + e // 4, P * (e % 4):P * (e % 4) + P],
                                                cst("ident")[0:SSM_H, h:h + 1].to_broadcast([SSM_H, P]), cum[0:SSM_H, P * i:P * i + P],
                                                start=True, stop=True)
                    last.then_inc(spread, 1)

            spread_sums(0)
            for g in range(GROUPS):
                if g:
                    pe.wait_ge(y_added, 2 * g)
                for i in range(TT):
                    for c in range(4):
                        last = nc.tensor.transpose(ps[:, i, P * c:P * c + P], xbc[:, 4 * g + c, P * i:P * i + P], cst("ident"))
                    last.then_inc(x_turned, 1)
                if g:
                    pe.wait_ge(state_copied, g)
                    pe.wait_ge(cb_masked, 2 * g)
                nc.tensor.transpose(ps[:, 3, 0:P], xbc[:, b_chunk + g, 0:P], cst("ident")).then_inc(b_turned, 1)
                for i in range(TT):
                    w = slice(P * i, P * i + P)
                    nc.tensor.matmul(ps[:, 2, P * i:P * i + P], xbc[:, b_chunk + g, w], xbc[:, c_chunk + g, w],
                                     start=True, stop=True).then_inc(cb_made, 1)
                pe.wait_ge(b_copied, g + 1)
                pe.wait_ge(xst_made, g + 1)
                nc.tensor.matmul(ps[:, 3, :], b_tok[:, :], xst[:, :], start=True, stop=True).then_inc(state_made, 1)
                if g + 1 < GROUPS:
                    spread_sums(g + 1)
                pe.wait_ge(xdt_made, 2 * g + 2)
                for i in range(TT):
                    pe.wait_ge(pair_made, 2 * g + i + 1)
                    if i:
                        pe.wait_ge(state_copied, g + 1)
                        pe.wait_ge(off_made, g + 1)
                    for e in range(8):
                        rows = slice(64 * (e % 2), 64 * (e % 2) + 64)
                        to = ps[rows, i, P * (e // 2):P * (e // 2) + P]
                        last = nc.tensor.matmul(to, xd(g)[:, i, HD * e:HD * e + HD], pair[:, g % 2, i, e, :], start=True, stop=(i == 0))
                        if i:
                            last = nc.tensor.matmul(to, state[:, HD * e:HD * e + HD], off_side[:, g % 2, e, :], start=False, stop=True)
                    last.then_inc(y_made, 1)

        @block.scalar
        def _(act):
            def exponentials(g):
                act.wait_ge(spread, 2 * g + 2)
                if g >= 2:
                    act.wait_ge(y_made, 2 * g - 2)
                nc.scalar.activation(off_side[:, g % 2, :, :], ps[:, 6:8, :].rearrange("p b (e q) -> p (b e) q", e=4), ACT.Exp).then_inc(grown, 1)
                for i in range(TT):
                    act.wait_ge(differed, 2 * g + i + 1)
                    nc.scalar.activation(pair[:, g % 2, i, :, :], pair[:, g % 2, i, :, :], ACT.Exp).then_inc(decayed, 1)

            exponentials(0)
            for g in range(GROUPS):
                act.wait_ge(b_turned, g + 1)
                if g:
                    act.wait_ge(state_made, g)
                nc.scalar.activation(b_tok[:, :], ps[:, 3, 0:P], ACT.Copy).then_inc(b_copied, 1)
                act.wait_ge(state_made, g + 1)
                nc.scalar.activation(state[:, :], ps[:, 3, :], ACT.Copy).then_inc(state_copied, 1)
                if g + 1 < GROUPS:
                    exponentials(g + 1)

        @block.vector
        def _(dve):
            V = nc.vector
            dve.wait_ge(masked_ready, 1)
            by_q = [P, 8, P]

            def differences(g):
                hs = slice(8 * g, 8 * g + 8)
                if g >= 2:
                    dve.wait_ge(y_made, 2 * g - 2)
                for i in range(TT):
                    dve.wait_ge(spread, 2 * g + i + 1)
                    if i:
                        dve.wait_ge(grown, g + 1)
                    to = pair[:, g % 2, i, :, :]
                    order.after(dve, V.tensor_tensor(to, ps[:, 4 + 2 * i:6 + 2 * i, :].rearrange("p b (e q) -> p (b e) q", e=4),
                                                     cum_tok[:, i, hs].unsqueeze(2).to_broadcast(by_q), ALU.subtract))
                    V.tensor_scalar(to, to, 0.0, None, ALU.min).then_inc(differed, 1)

            differences(0)
            for g in range(GROUPS):
                hs = slice(8 * g, 8 * g + 8)
                for i in range(TT):
                    dve.wait_ge(x_turned, 2 * g + i + 1)
                    V.tensor_tensor(xd(g)[:, i, :].rearrange("p (e v) -> p e v", e=8), ps[:, i, :].rearrange("p (e v) -> p e v", e=8),
                                    dt_tok[:, i, hs].unsqueeze(2).to_broadcast([P, 8, HD]), ALU.mult).then_inc(xdt_made, 1)
                dve.wait_ge(xdt_made, 2 * g + 1)
                if g:
                    dve.wait_ge(state_made, g)
                V.tensor_tensor(xst[:, :].rearrange("p (e v) -> p e v", e=8), xd(g)[:, 0, :].rearrange("p (e v) -> p e v", e=8),
                                last_tok[:, hs].unsqueeze(2).to_broadcast([P, 8, HD]), ALU.mult).then_inc(xst_made, 1)
                for i in range(TT):
                    dve.wait_ge(cb_made, 2 * g + 2)
                    V.tensor_tensor(cb[:, i, :], ps[:, 2, P * i:P * i + P], masks[:, :], ALU.mult).then_inc(cb_masked, 1)
                for i in range(TT):
                    to = pair[:, g % 2, i, :, :]
                    dve.wait_ge(decayed, 2 * g + i + 1)
                    dve.wait_ge(cb_masked, 2 * g + i + 1)
                    V.tensor_tensor(to, to, cb[:, i, :].unsqueeze(1).to_broadcast(by_q), ALU.mult).then_inc(pair_made, 1)
                dve.wait_ge(grown, g + 1)
                to = off_side[:, g % 2, :, :]
                V.tensor_tensor(to, to, xbc[:, c_chunk + g, P:T].unsqueeze(1).to_broadcast(by_q), ALU.mult).then_inc(off_made, 1)
                if g + 1 < GROUPS:
                    differences(g + 1)
                for i in range(TT):
                    dve.wait_ge(y_made, 2 * g + i + 1)
                    for c in range(4):
                        to = xbc[:, 4 * g + c, P * i:P * i + P]
                        last = V.scalar_tensor_tensor(to, to, par("a_d", 4 * g + c), ps[:, i, P * c:P * c + P], ALU.mult, ALU.add)
                    last.then_inc(y_added, 1)


def gate_groups(scope, y, z, *, nc, sem, sbuf, par, cst, ps, prefetch):
    sq = sbuf(scope, "group_squared", [2, 4, T])
    rms = sbuf(scope, "group_rms", [4, T])
    gated, squared, summed, rooted, inverted = (sem("group_gated"), sem("group_sq_ready"), sem("group_summed"), sem("group_rooted"),
                                                sem("group_inverted"))
    with nc.Block() as block:
        @block.sync
        def _(sp):
            prefetch(sp)

        @block.vector
        def _(dve):
            V = nc.vector

            def scale(g):
                dve.wait_ge(rooted, g + 1)
                V.reciprocal(rms[:, g % 4, :], rms[:, g % 4, :]).then_inc(inverted, 1)
                dve.wait_ge(inverted, g + 1)
                for c in range(4 * g, 4 * g + 4):
                    V.scalar_tensor_tensor(y[:, c, :], y[:, c, :], par("a_norm", c), rms[:, g % 4, :], ALU.mult, ALU.mult)

            for g in range(GROUPS):
                to = y[:, 4 * g:4 * g + 4, :]
                V.tensor_tensor(to, to, z[:, 4 * g:4 * g + 4, :], ALU.mult).then_inc(gated, 1)
                if g >= 2:
                    scale(g - 2)
            scale(GROUPS - 2)
            scale(GROUPS - 1)

        @block.scalar
        def _(act):
            def root(g):
                act.wait_ge(summed, g + 1)
                if g >= 4:
                    act.wait_ge(inverted, g - 3)
                nc.scalar.activation(rms[:, g % 4, :], ps[:, g, 0:T], ACT.Sqrt, bias=cst("eps_2"), scale=1.0 / 512).then_inc(rooted, 1)

            for g in range(GROUPS):
                act.wait_ge(gated, g + 1)
                if g >= 2:
                    act.wait_ge(summed, g - 1)
                nc.scalar.activation(sq[:, g % 2, :, :], y[:, 4 * g:4 * g + 4, :], ACT.Square).then_inc(squared, 1)
                if g >= 1:
                    root(g - 1)
            root(GROUPS - 1)

        @block.tensor
        def _(pe):
            for g in range(GROUPS):
                pe.wait_ge(squared, g + 1)
                sum_over_channels(pe, nc, cst("ones"), sq[:, g % 2, :, :], ps[:, g, 0:T], 4).then_inc(summed, 1)


def attention(x2, x3, z, spare, out, *, nc, d, sem, sbuf, par, par_at, cst, ps, ring, **_):
    with ExitStack() as scope:
        query, gate = z[:, 0:QH // 2, :], z[:, QH // 2:QH, :]
        key = sbuf(scope, "swa_k", [KVH, T])
        VC = KVH * HD // P
        value_t = spare[:, 0:VC, :]

        def take_keys_values(act, g, sums, half, before):
            to, bias, count = (key, "k_bias", KVH) if g == 0 else (value_t, "v_bias", VC)
            for n in range(count):
                last = nc.scalar.activation(to[:, n, :], sums[:, n, :], ACT.Identity, bias=par(bias, n))
            last.then_inc(ring.evacuated, 1)

        def take_query(act, g, sums, half, before):
            for n in range(4):
                last = nc.scalar.activation(query[:, bass.ds(4 * g + n, 1), :], sums[:, n:n + 1, :], ACT.Identity, bias=par_at("q_bias", 4 * g + n))
            last.then_inc(ring.evacuated, 1)

        def take_gate(act, g, sums, half, before):
            nc.scalar.activation(gate[:, bass.ds(4 * g, 4), :], sums, ACT.Silu).then_inc(ring.evacuated, 1)

        linear(nc, ring, ps, [
            Product(d["w_kv"], KVH + VC, x2, dict(scalar=take_keys_values)),
            Product(d["b_w_in"][0:4], QH // 2, x2, dict(scalar=take_query)),
            Product(d["b_w_in"][4:8], QH // 2, x2, dict(scalar=take_gate))])
        value = sbuf(scope, "swa_v", [TT, KVH * HD])
        cos = sbuf(scope, "rope_cos", [T])
        sin = sbuf(scope, "rope_sin", [T])
        mask = sbuf(scope, "window", [3 * P])
        sinks = sbuf(scope, "sinks_all", [QH])
        with ExitStack() as inner:
            make_tables(inner, value_t, value, cos, sin, mask, sinks, nc=nc, d=d, sem=sem, sbuf=sbuf, cst=cst, ps=ps)
        rotate(query, key, cos, sin, nc=nc, sem=sem, sbuf=sbuf, cst=cst, ps=ps)
        with ExitStack() as inner:
            window_attention(inner, query, key, value, mask, sinks, gate, nc=nc, sem=sem, sbuf=sbuf, cst=cst, ps=ps,
                             prefetch=lambda sp: ring.prefetch(sp, d["b_w_out"], ring.parts))

        def add(dve, g, sums, half, before):
            nc.vector.scalar_tensor_tensor(x3[:, bass.ds(4 * g, 4), :], x2[:, bass.ds(4 * g, 4), :], ALPHA, sums,
                                           ALU.mult, ALU.add).then_inc(ring.evacuated, 1)

        linear(nc, ring, ps, [Product(d["b_w_out"], DC, gate, dict(vector=add))])
    layernorm(x3, 1, nc=nc, sem=sem, sbuf=sbuf, par=par, cst=cst, ps=ps, out=out)


def make_tables(scope, value_t, value, cos, sin, mask, sinks, *, nc, d, sem, sbuf, cst, ps):
    pos = sbuf(scope, "pos", [T], I32)
    angle = sbuf(scope, "angle", [T])
    turns = sbuf(scope, "turns", [2, T])
    pos_in, sinks_in = sem("pos_in"), sem("sinks_in")
    reduced, valued, masked = sem("angles_reduced"), sem("swa_v_made"), sem("window_made")
    order, pool_order = Order(sem("table_order")), Order(sem("window_order"))
    with nc.Block() as block:
        @block.sync
        def _(sp):
            sp.dma_start(pos[:, :], d["positions"].to_broadcast([P, T])).then_inc(pos_in, 16)
            sp.dma_start(sinks[:, :], d["sinks"].to_broadcast([P, QH])).then_inc(sinks_in, 16)
            sp.wait_ge(sinks_in, 16)

        @block.gpsimd
        def _(pool):
            G = nc.gpsimd
            pool_order.after(pool, G.memset(mask[:, :], 0.0))
            pool_order.mark(G.affine_select(out=mask[:, 0:P], in_=mask[:, 0:P], compare_op=ALU.is_ge, fill=NEG, base=0,
                                            pattern=[[-1, P]], channel_multiplier=1))
            pool_order.mark(G.affine_select(out=mask[:, P:2 * P], in_=mask[:, P:2 * P], compare_op=ALU.is_gt, fill=NEG, base=0,
                                            pattern=[[1, P]], channel_multiplier=-1))
            pool_order.mark(G.affine_select(out=mask[:, 2 * P:3 * P], in_=mask[:, 2 * P:3 * P], compare_op=ALU.is_ge, fill=NEG, base=0,
                                            pattern=[[-1, P]], channel_multiplier=1))

        @block.vector
        def _(dve):
            V = nc.vector
            dve.wait_ge(pos_in, 16)
            order.after(dve, V.tensor_copy(angle[:, :], pos[:, :]))
            order.after(dve, V.tensor_scalar(angle[:, :], angle[:, :], cst("freq"), None, ALU.mult))
            for i, (to, quarter, ahead) in enumerate(((sin, 0.0, 0.0), (cos, 0.25, np.pi / 2))):
                n = turns[:, i, :]
                order.after(dve, V.tensor_scalar(n, angle[:, :], 1 / TWO_PI, quarter, ALU.mult, ALU.add))
                order.after(dve, V.tensor_scalar(n, n, ROUND, None, ALU.add))
                order.after(dve, V.tensor_scalar(n, n, -ROUND, None, ALU.add))
                order.after(dve, V.scalar_tensor_tensor(to[:, :], n, -PI_A, angle[:, :], ALU.mult, ALU.add))
                order.after(dve, V.scalar_tensor_tensor(to[:, :], n, -PI_B, to[:, :], ALU.mult, ALU.add))
                order.after(dve, V.scalar_tensor_tensor(to[:, :], n, -PI_C, to[:, :], ALU.mult, ALU.add))
                order.after(dve, V.tensor_scalar(to[:, :], to[:, :], float(ahead), PI_LOW, ALU.add, ALU.min))
                V.tensor_scalar(to[:, :], to[:, :], -PI_LOW, None, ALU.max).then_inc(reduced, 1)

        @block.scalar
        def _(act):
            for i, to in enumerate((sin, cos)):
                act.wait_ge(reduced, i + 1)
                nc.scalar.activation(to[:, :], to[:, :], ACT.Sin)
            for i in range(TT):
                act.wait_ge(valued, i + 1)
                nc.scalar.activation(value[:, i, :], ps[:, i, 0:T], ACT.Copy)

        @block.tensor
        def _(pe):
            for i in range(TT):
                for c in range(KVH * HD // P):
                    last = nc.tensor.transpose(ps[:, i, P * c:P * c + P], value_t[:, c, P * i:P * i + P], cst("ident"))
                last.then_inc(valued, 1)


def rotate(query, key, cos, sin, *, nc, sem, sbuf, cst, ps):
    jobs = [query[:, 4 * g:4 * g + 4, :] for g in range(4)] + [key[:, :, :]]
    by_t = [P, 4, T]
    turned, multiplied = sem("rope_turned"), sem("rope_multiplied")
    order = Order(sem("rope_order"))
    with ExitStack() as scope:
        part = sbuf(scope, "rope_part", [2, 4, T])
        with nc.Block() as block:
            @block.tensor
            def _(pe):
                for n, x in enumerate(jobs):
                    if n >= 4:
                        pe.wait_ge(multiplied, n - 3)
                    for c in range(4):
                        last = nc.tensor.matmul(ps[:, 2 * (n % 4) + c // 2, T * (c % 2):T * (c % 2) + T], cst("turn"), x[:, c, :],
                                                start=True, stop=True)
                    last.then_inc(turned, 1)

            @block.vector
            def _(dve):
                V = nc.vector
                for n, x in enumerate(jobs):
                    dve.wait_ge(turned, n + 1)
                    sums = ps[:, 2 * (n % 4):2 * (n % 4) + 2, :].rearrange("p b (c t) -> p (b c) t", c=2)
                    V.tensor_tensor(part[:, n % 2, :, :], sums, sin[:, :].unsqueeze(1).to_broadcast(by_t), ALU.mult).then_inc(multiplied, 1)
                    order.mark(V.tensor_tensor(x, x, cos[:, :].unsqueeze(1).to_broadcast(by_t), ALU.mult))
                    dve.wait_ge(multiplied, n + 1)
                    order.settle(dve)
                    order.after(dve, V.tensor_tensor(x, x, part[:, n % 2, :, :], ALU.add))


def window_attention(scope, query, key, value, mask, sinks, gate, *, nc, sem, sbuf, cst, ps, prefetch):
    G, N = KVH, QH // KVH
    B = 3
    logits = sbuf(scope, "swa_logits", [B, N, 3 * P])
    p_t = sbuf(scope, "swa_p_t", [2, 3 * P])
    peak = sbuf(scope, "swa_peak", [B, 2, N])
    total = sbuf(scope, "swa_total", [B, 2, N])
    sunk = sbuf(scope, "swa_sunk", [B, 2, N])
    dotted, added, shifted, exped, scaled = sem("swa_dotted"), sem("swa_added"), sem("swa_shifted"), sem("swa_exped"), sem("swa_scaled")
    turned, copied, valued, gated = sem("swa_turned"), sem("swa_p_copied"), sem("swa_valued"), sem("swa_gated")
    order = Order(sem("swa_order"))
    with nc.Block() as block:
        @block.sync
        def _(sp):
            prefetch(sp)

        @block.tensor
        def _(pe):
            def dots(h):
                g = h // N
                rows = slice(64 * (h % 2), 64 * (h % 2) + 64)
                if h >= 4:
                    pe.wait_ge(added, h - 3)
                nc.tensor.matmul(ps[:, h % 4, 0:P], query[rows, h // 2, 0:P], key[rows, g, 0:P], start=True, stop=True)
                nc.tensor.matmul(ps[:, h % 4, P:3 * P], query[rows, h // 2, P:T], key[rows, g, :], start=True, stop=True).then_inc(dotted, 1)

            def values(h):
                rows, pair = slice(64 * (h % 2), 64 * (h % 2) + 64), h // 2
                pe.wait_ge(copied, h + 1)
                if pair >= 2:
                    pe.wait_ge(gated, pair - 1)
                v = [value[:, s, HD * (h // N):HD * (h // N) + HD] for s in range(TT)]
                p = [p_t[:, h % 2, P * s:P * s + P] for s in range(3)]
                bank = ps[rows, 6 + pair % 2, :]
                nc.tensor.matmul(bank[:, 0:P], v[0], p[0], start=True, stop=True)
                nc.tensor.matmul(bank[:, P:T], v[0], p[1], start=True, stop=False)
                nc.tensor.matmul(bank[:, P:T], v[1], p[2], start=False, stop=True).then_inc(valued, 1)

            for h in range(2 * N):
                dots(h)
            for g in range(G):
                for h in range(N * g, N * g + N):
                    if h % (N // 2) == 0:
                        pe.wait_ge(scaled, h // (N // 2) + 1)
                    if h >= 2:
                        pe.wait_ge(copied, h - 1)
                    for s in range(3):
                        last = nc.tensor.transpose(ps[:, 4 + h % 2, P * s:P * s + P], logits[:, g % B, h % N, P * s:P * s + P], cst("ident"))
                    last.then_inc(turned, 1)
                    if g + 2 < G:
                        dots(h + 2 * N)
                    if h > N * g:
                        values(h - 1)
                values(N * g + N - 1)

        @block.vector
        def _(dve):
            V = nc.vector

            def add_mask(h):
                dve.wait_ge(dotted, h + 1)
                if h >= B * N:
                    dve.wait_ge(turned, N * (h // N - B + 1))
                V.scalar_tensor_tensor(logits[:, h // N % B, h % N, :], ps[:, h % 4, 0:3 * P], SA_SCALE, mask[:, :], ALU.mult, ALU.add).then_inc(added, 1)

            def find_peaks(g):
                b = g % B
                dve.wait_ge(added, N * (g + 1))
                order.mark(V.tensor_reduce(peak[:, b, 0, :], logits[:, b, :, 0:P], AX, ALU.max))
                order.mark(V.tensor_reduce(peak[:, b, 1, :], logits[:, b, :, P:3 * P], AX, ALU.max))
                order.settle(dve)
                sink = sinks[:, N * g:N * g + N].unsqueeze(1).to_broadcast([P, 2, N])
                order.after(dve, V.tensor_tensor(peak[:, b, :, :], peak[:, b, :, :], sink, ALU.max))
                order.after(dve, V.tensor_scalar(peak[:, b, :, :], peak[:, b, :, :], -1.0, None, ALU.mult))
                V.tensor_tensor(sunk[:, b, :, :], peak[:, b, :, :], sink, ALU.add).then_inc(shifted, 1)

            def gates(pair):
                dve.wait_ge(valued, 2 * pair + 2)
                to = gate[:, pair, :]
                V.tensor_tensor(to, to, ps[:, 6 + pair % 2, 0:T], ALU.mult).then_inc(gated, 1)

            for g in range(2):
                for e in range(N):
                    add_mask(N * g + e)
                if g == 0:
                    find_peaks(0)
            for g in range(G):
                b = g % B
                dve.wait_ge(exped, g + 1)
                order.after(dve, V.tensor_tensor(total[:, b, :, :], total[:, b, :, :], sunk[:, b, :, :], ALU.add))
                order.after(dve, V.reciprocal(total[:, b, :, :], total[:, b, :, :]))
                for half in range(2):
                    heads = slice(N // 2 * half, N // 2 * (half + 1))
                    for i, keys in enumerate((slice(0, P), slice(P, 3 * P))):
                        last = V.tensor_tensor(logits[:, b, heads, keys], logits[:, b, heads, keys],
                                               total[:, b, i, heads].unsqueeze(2).to_broadcast([P, N // 2, keys.stop - keys.start]), ALU.mult)
                        order.mark(last)
                    order.settle(dve)
                    dve.sem_inc(scaled, 1)
                if g + 1 < G:
                    find_peaks(g + 1)
                for e in range(N):
                    if g + 2 < G:
                        add_mask(N * (g + 2) + e)
                    if e >= 2 and e % 2 == 0:
                        gates(N // 2 * g + e // 2 - 1)
                gates(N // 2 * (g + 1) - 1)

        @block.scalar
        def _(act):
            def exps(g, heads):
                b = g % B
                act.wait_ge(shifted, g + 1)
                for i, w in enumerate((slice(0, P), slice(P, 3 * P))):
                    for e in heads:
                        nc.scalar.activation(logits[:, b, e, w], logits[:, b, e, w], ACT.Exp, bias=peak[:, b, i, e:e + 1],
                                             accum_out=total[:, b, i, e:e + 1])

            def exp_sinks(g):
                nc.scalar.activation(sunk[:, g % B, :, :], sunk[:, g % B, :, :], ACT.Exp).then_inc(exped, 1)

            exps(0, range(N))
            exp_sinks(0)
            for g in range(G):
                for e in range(N):
                    h = N * g + e
                    act.wait_ge(turned, h + 1)
                    if h >= 2:
                        act.wait_ge(valued, h - 1)
                    nc.scalar.activation(p_t[:, h % 2, :], ps[:, 4 + h % 2, 0:3 * P], ACT.Copy).then_inc(copied, 1)
                    if g + 1 < G and e >= 2:
                        exps(g + 1, {2: (0, 1), N - 1: (N - 2, N - 1)}.get(e, (e - 1,)))
                if g + 1 < G:
                    exp_sinks(g + 1)


def pack_params(np, v):
    def chunks(a, n):
        a = np.asarray(a).reshape(-1)
        full = np.zeros(n * P, np.float32)
        full[:a.size] = a
        return full.reshape(n, P).T

    mix = v["shift_mix"][0]
    conv = v["a_conv_w_2"][0].reshape(4 * CONVC, P).T
    kb = np.repeat(v["kv_b_2"][:256].reshape(4, 1, 64), 2, axis=1)
    ab = np.concatenate
    cols = dict(
        norm_mix=chunks(v["norm_mix_g"], 16), mix=chunks(mix, C_IN), w0=chunks(v["w0"], 8), a0=chunks(v["a0"], 8),
        k_k=chunks(v["k_k"], 8), k_a=chunks(v["k_a"], 8), r_k=chunks(v["r_k"], 8), ln_x_w=chunks(v["ln_x_w"], 8),
        ln_x_b=chunks(v["ln_x_b"], 8), kv_norm=chunks(v["kv_norm_g"], 2), norm_ffn=chunks(v["norm_ffn_g"], 16),
        norm_final=chunks(v["norm_final_g"], 16), ln_g=chunks(v["ln_g_2"], 32), ln_b=chunks(v["ln_b_2"], 32),
        conv_w=conv, conv_b=chunks(v["a_conv_b_2"], CONVC), dt_bias=chunks(v["a_dt_bias_2"], 1),
        a_log=chunks(v["a_log_2"], 1), a_d=chunks(np.repeat(v["a_d_2"][0], 64), 32), a_norm=chunks(v["a_norm_w_2"], 32),
        q_bias=chunks(v["b_q_bias_2"], 16), k_bias=chunks(kb, 4), v_bias=chunks(v["kv_b_2"][256:], 2))
    return np.ascontiguousarray(ab([cols[n] for n in PARAM_COLS], axis=1))


def make_const(np):
    j, t = np.arange(2 * CH)[:, None], np.arange(2 * CH)[None, :]
    mask = np.zeros((P, 2 * CH), np.float32)
    mask[:2 * CH] = np.where(t < CH, j % CH < t % CH, j % CH <= t % CH)
    heads = np.kron(np.eye(2), np.ones((64, 64)))
    turn = np.zeros((P, P), np.float32)
    freq = np.zeros((P, 1), np.float32)
    f = (np.float32(500000.0) ** (-np.arange(0, 16, 2, dtype=np.float32) / np.float32(16))).astype(np.float32)
    for base in (0, 64):
        for i in range(8):
            turn[base + i + 8, base + i] = -1.0
            turn[base + i, base + i + 8] = 1.0
            freq[base + i] = freq[base + i + 8] = f[i]
    full = lambda x: np.full((P, 1), x, np.float32)
    cols = dict(ident=np.eye(P), ones=np.ones((P, P)), heads=heads, flip=np.eye(P)[::-1], decay_mask=mask, turn=turn, freq=freq,
                iota=np.tile(np.arange(16), (P, 1)), eps_rms=full(EPS_RMS), eps_gn=full(EPS_GN), eps_2=full(EPS_2))
    return np.ascontiguousarray(np.concatenate([cols[n] for n in CONST_COLS], axis=1).astype(np.float32))


def make_buckets(np):
    rel = np.arange(2 * T) - (T - 1)
    n = np.abs(rel)
    large = 8 + (np.log(np.maximum(n, 1).astype(np.float32) / np.float32(8)).astype(np.float32)
                 / np.float32(np.log(1024 / 8)) * np.float32(8)).astype(np.int32)
    bucket = (rel > 0) * 16 + np.where(n < 8, n, np.minimum(large, 15))
    return np.ascontiguousarray((np.arange(32)[:, None] == bucket[None, :]).astype(np.float32))


def kernel(**inputs):
    import concourse.bacc as bacc
    from concourse.bass_utils import run_bass_kernel_spmd

    v = {k: np.asarray(a) for k, a in inputs.items()}

    def rows(w):
        return np.ascontiguousarray(w.reshape(w.shape[0] // P, P, w.shape[1]).transpose(1, 0, 2))

    def pack(w):
        k, n = w.shape
        g = (n + 511) // 512
        full = np.zeros((k, g * 512), w.dtype)
        full[:, :n] = w
        return np.ascontiguousarray(full.reshape(k // P, P, g, 512).transpose(2, 1, 0, 3))

    w_in = v["w_in"][0]
    rw = w_in[:, :3360]
    q, ckv, iq, ik, iw, gates = np.split(w_in[:, 3360:], np.cumsum([1024, 256, 512, 64, 8]), axis=1)
    blank = np.zeros((D, P - IW_ROW - IDX_HEADS), np.float32)
    kv = v["kv_w_2"]
    k_twice = np.repeat(kv[:, :256].reshape(D, 4, 1, 64), 2, axis=2).reshape(D, 512)
    up = v["w_gate_up"][0]
    gate_up = np.zeros((2, P, H * HD), np.float32)
    gate_up[0] = up[:P]
    gate_up[1, :GATE_RANK - P] = up[P:]
    data = dict(
        x=rows(v["x"][0].T), params=pack_params(np, v), const=make_const(np), bucket_hot=make_buckets(np),
        w_in=pack(np.concatenate([rw, iw, blank, q, ckv, iq, ik, ik], axis=1)), w_gates=pack(gates),
        lora=np.ascontiguousarray(np.concatenate([v["w_decay_up"][0], v["w_icl_up"][0]], axis=0)),
        gate_up=np.ascontiguousarray(gate_up.transpose(1, 0, 2)), rel_bias=np.ascontiguousarray(v["rel_bias"]),
        w_uk=rows(v["w_uk"][0].transpose(1, 0, 2).reshape(256, 1024)),
        w_uv=rows(v["w_uv"][0].transpose(1, 0, 2).reshape(256, 1024)),
        w_branch_rwkv=pack(v["w_branch_rwkv"][0]), w_branch_dsa=pack(v["w_branch_dsa"][0]), w_out=pack(v["w_out"][0]),
        w_query=pack(v["w_peer_query"][0]),
        sub_keys=np.ascontiguousarray(v["peer_sub_keys"][0].transpose(3, 0, 1, 2).reshape(P, 16, P)),
        peer_u=np.ascontiguousarray(v["peer_u"][0]), peer_v=np.ascontiguousarray(v["peer_v"][0]),
        a_w_z=pack(v["a_w_in_2"][0][:, :4096]), a_w_conv=pack(v["a_w_in_2"][0][:, 4096:10240]),
        a_w_dt=pack(v["a_w_in_2"][0][:, 10240:]), a_w_out=pack(v["a_w_out_2"][0]),
        w_kv=pack(np.concatenate([k_twice, kv[:, 256:]], axis=1)),
        sinks=np.ascontiguousarray(v["b_sinks_2"].reshape(1, QH)),
        positions=np.ascontiguousarray(v["positions_2"].reshape(1, T)),
        b_w_in=pack(v["b_w_in_2"][0]), b_w_out=pack(v["b_w_out_2"][0]),
    )
    nc = bacc.Bacc("TRN2", target_bir_lowering=False, num_devices=1)
    d = {n: nc.dram_tensor(f"in_{n}", a.shape, mybir.dt.from_np(a.dtype), kind="ExternalInput").ap()
         for n, a in data.items()}
    out = nc.dram_tensor("out_t", [P, DC, T], F32, kind="ExternalOutput").ap()
    build(nc, d, out)
    got = run_bass_kernel_spmd(nc, [{f"in_{n}": a for n, a in data.items()}], core_ids=[0]).results[0]["out_t"]
    return np.ascontiguousarray(got.transpose(2, 1, 0).reshape(1, T, D))
```
